# Optimizing a Trainium2 kernel written in Bass

```python
import jax
import jax.numpy as jnp
from jax import lax
import numpy as np

D_MODEL = 1024
BATCH = 1
SEQ = 512
DEPTH = 1
DEC_BATCH = 8
DEC_SEQ = 4
PAST_LEN = 4096
PAGE_SIZE = 128

N_MEM = 256
EPS = 1e-6
ML_HEADS = 4
ML_DH = D_MODEL // 8
ML_W = ML_HEADS * ML_DH
ML_CONV = 4
ML_CHUNK = 64
RW_DH = 64
RW_HEADS = (D_MODEL // 2) // RW_DH
RW_W = RW_HEADS * RW_DH
RW_LORA_W = 64
RW_LORA_A = 64
RW_LORA_G = 128
RW_IN = 3 * RW_W + RW_LORA_W + RW_LORA_A + RW_LORA_G
RW_GN_EPS = 64e-5
XA_HEADS = 4
XA_DH = D_MODEL // 8
XA_W = XA_HEADS * XA_DH
N_BRANCH = 3
BR_W = D_MODEL // 2
IN_W = 2 * ML_W + ML_W + ML_W + 2 * ML_HEADS + RW_IN + XA_W + N_BRANCH * D_MODEL
PK_HEADS = 8
PK_NKEYS = 128
PK_N_EXP = PK_NKEYS * PK_NKEYS
PK_DKEY = 256
PK_TOPK = 16
PK_BLOCK = 128

kernel_name = 'hybrid_mlstm_rwkv7_memattn_peer_step'

def rmsnorm(x, g):
    x32 = x.astype(jnp.float32)
    y = x32 * lax.rsqrt(jnp.mean(x32 * x32, axis=-1, keepdims=True) + EPS)
    return y * g.astype(jnp.float32)

def head_layernorm(x, eps):
    x32 = x.astype(jnp.float32)
    mu = jnp.mean(x32, axis=-1, keepdims=True)
    xc = x32 - mu
    return xc * lax.rsqrt(jnp.mean(xc * xc, axis=-1, keepdims=True) + eps)

def heads(a, n):
    return a.reshape(a.shape[:-1] + (n, a.shape[-1] // n))

def split_points(sizes):
    pts, acc = [], 0
    for s in sizes[:-1]:
        acc += s
        pts.append(acc)
    return pts

def causal_conv(u, buf, w, b):
    T = u.shape[1]
    full = jnp.concatenate([buf.astype(u.dtype), u], axis=1)
    y = b + sum(full[:, j:j + T] * w[j] for j in range(ML_CONV))
    return y, full[:, T:]

def token_shift(u, prev, mu):
    shifted = jnp.concatenate([prev.astype(u.dtype)[:, None, :], u[:, :-1, :]], axis=1)
    return u + (shifted - u) * mu, u[:, -1, :]

def mlstm_chunkwise(q, k, v, i_pre, f_pre, C0, n0, m0):
    B, T, H, Dh = q.shape
    L = ML_CHUNK if T % ML_CHUNK == 0 else T
    nc = T // L

    def to_chunks(a):
        a = a.astype(jnp.float32).reshape((B, nc, L) + a.shape[2:])
        return jnp.moveaxis(jnp.moveaxis(a, 3, 2), 1, 0)

    xs = (to_chunks(q) * (Dh ** -0.5), to_chunks(k), to_chunks(v), to_chunks(i_pre),
          to_chunks(jax.nn.log_sigmoid(f_pre.astype(jnp.float32))))
    causal = jnp.tril(jnp.ones((L, L), dtype=bool))

    def step(carry, inp):
        C, n, m = carry
        qb, kb, vb, ib, lfb = inp
        cumf = jnp.cumsum(lfb, axis=-1)
        logw = jnp.where(causal, cumf[..., :, None] - cumf[..., None, :] + ib[..., None, :], -jnp.inf)
        b_inter = cumf + m[..., None]
        m_t = jnp.maximum(b_inter, jnp.max(logw, axis=-1))
        s = jnp.einsum('bhtd,bhsd->bhts', qb, kb) * jnp.exp(logw - m_t[..., None])
        inter = jnp.exp(b_inter - m_t)
        num = jnp.einsum('bhts,bhsd->bhtd', s, vb) + inter[..., None] * jnp.einsum('bhvk,bhtk->bhtv', C, qb)
        den = jnp.sum(s, axis=-1) + inter * jnp.einsum('bhk,bhtk->bht', n, qb)
        h = num / jnp.maximum(jnp.abs(den), jnp.exp(-m_t))[..., None]
        total = cumf[..., -1]
        logw_end = total[..., None] - cumf + ib
        m_new = jnp.maximum(total + m, jnp.max(logw_end, axis=-1))
        w_end = jnp.exp(logw_end - m_new[..., None])
        decay = jnp.exp(total + m - m_new)
        C_new = decay[..., None, None] * C + jnp.einsum('bhs,bhsv,bhsk->bhvk', w_end, vb, kb)
        n_new = decay[..., None] * n + jnp.einsum('bhs,bhsk->bhk', w_end, kb)
        return (C_new, n_new, m_new), h

    init = (C0.astype(jnp.float32), n0.astype(jnp.float32), m0.astype(jnp.float32))
    (C, n, m), hs = lax.scan(step, init, xs)
    h = jnp.transpose(hs, (1, 0, 3, 2, 4)).reshape(B, T, H, Dh)
    return h, C, n, m

def rwkv7_scan(r, w, k, v, a, b, S0):
    xs = tuple(jnp.moveaxis(t.astype(jnp.float32), 1, 0) for t in (r, w, k, v, a, b))

    def step(S, inp):
        rt, wt, kt, vt, at, bt = inp
        sa = jnp.einsum('bhvk,bhk->bhv', S, at)
        S = S * wt[:, :, None, :] + sa[..., None] * bt[:, :, None, :] + vt[..., None] * kt[:, :, None, :]
        return S, jnp.einsum('bhvk,bhk->bhv', S, rt)

    S, ys = lax.scan(step, S0.astype(jnp.float32), xs)
    return jnp.moveaxis(ys, 0, 1), S

def rwkv7_branch(u, shift0, S0, mu, w0, w2, a0, a2, g2, kk_w, ka_w, rk_w, ln_w, ln_b):
    B, T, _ = u.shape
    us, shift_new = token_shift(u, shift0, mu)
    r, k, v, wl, al, gl = jnp.split(us, split_points([RW_W, RW_W, RW_W, RW_LORA_W, RW_LORA_A, RW_LORA_G]), axis=-1)
    w_log = -jax.nn.softplus(-(w0 + jnp.tanh(wl) @ w2)) - 0.5
    decay = jnp.exp(-jnp.exp(w_log.astype(jnp.float32)))
    a = jax.nn.sigmoid(a0 + al @ a2)
    g = jax.nn.sigmoid(gl) @ g2
    kk = heads(k * kk_w, RW_HEADS).astype(jnp.float32)
    kk = kk * lax.rsqrt(jnp.maximum(jnp.sum(kk * kk, axis=-1, keepdims=True), 1e-24))
    k = k * (1.0 + (a - 1.0) * ka_w)
    rh, kh, vh, ah = heads(r, RW_HEADS), heads(k, RW_HEADS), heads(v, RW_HEADS), heads(a, RW_HEADS)
    y, S_new = rwkv7_scan(rh, heads(decay, RW_HEADS), kh, vh, -kk, kk * ah, S0)
    y = head_layernorm(y, RW_GN_EPS).reshape(B, T, RW_W) * ln_w + ln_b
    bonus = jnp.sum(rh * kh * rk_w, axis=-1, keepdims=True) * vh
    y = (y + bonus.reshape(B, T, RW_W)) * g
    return y, S_new, shift_new

def memory_kv(mem, g, w_k, w_v):
    m = rmsnorm(mem, g)
    return heads(m @ w_k, XA_HEADS), heads(m @ w_v, XA_HEADS)

def memory_attention(q, k, v):
    s = jnp.einsum('bthd,bshd->bhts', q.astype(jnp.float32), k.astype(jnp.float32)) * (XA_DH ** -0.5)
    p = jax.nn.softmax(s, axis=-1)
    return jnp.einsum('bhts,bshd->bthd', p, v.astype(jnp.float32))

def peer(x, w_q, sub_k1, sub_k2, u_tab, v_tab):
    shape = x.shape
    xt = x.reshape(-1, shape[-1])
    n_tok = xt.shape[0]
    n_blk = -(-n_tok // PK_BLOCK)
    xt = jnp.pad(xt, ((0, n_blk * PK_BLOCK - n_tok), (0, 0))).reshape(n_blk, PK_BLOCK, shape[-1])

    def block(xb):
        q = (xb @ w_q).reshape(PK_BLOCK, PK_HEADS, 2, PK_DKEY // 2).astype(jnp.float32)
        s1 = jnp.einsum('thd,kd->thk', q[:, :, 0], sub_k1.astype(jnp.float32))
        s2 = jnp.einsum('thd,kd->thk', q[:, :, 1], sub_k2.astype(jnp.float32))
        v1, i1 = lax.top_k(s1, PK_TOPK)
        v2, i2 = lax.top_k(s2, PK_TOPK)
        cand = (v1[..., :, None] + v2[..., None, :]).reshape(PK_BLOCK, PK_HEADS, PK_TOPK * PK_TOPK)
        cidx = (i1[..., :, None] * PK_NKEYS + i2[..., None, :]).reshape(PK_BLOCK, PK_HEADS, PK_TOPK * PK_TOPK)
        top, pos = lax.top_k(cand, PK_TOPK)
        eidx = jnp.take_along_axis(cidx, pos, axis=-1)
        gate = jax.nn.softmax(top, axis=-1)
        act = jax.nn.gelu(jnp.einsum('thkd,td->thk', u_tab[eidx], xb), approximate=False)
        return jnp.einsum('thk,thkd->td', gate * act, v_tab[eidx])

    out = lax.map(block, xt)
    return out.reshape(n_blk * PK_BLOCK, shape[-1])[:n_tok].reshape(shape)

def trunk_layer(x, mem_k, mem_v, C0, n0, m0, conv0, S0, shift0, lw):
    (norm_mix, w_in, ml_conv_w, ml_conv_b, ml_gate_b, ml_norm_w,
     rw_mu, rw_w0, rw_w2, rw_a0, rw_a2, rw_g2, rw_kk, rw_ka, rw_rk, rw_ln_w, rw_ln_b,
     w_branch, w_out, norm_ffn, pk_wq, pk_k1, pk_k2, pk_u, pk_v) = lw
    B, T, _ = x.shape
    h = rmsnorm(x, norm_mix)
    proj = h @ w_in
    qk_pre, ml_v, ml_o, ml_if, rw_pre, xa_q, gate_pre = jnp.split(
        proj, split_points([2 * ML_W, ML_W, ML_W, 2 * ML_HEADS, RW_IN, XA_W, N_BRANCH * D_MODEL]), axis=-1)
    qk, conv_new = causal_conv(qk_pre, conv0, ml_conv_w, ml_conv_b)
    ml_q, ml_k = jnp.split(jax.nn.silu(qk), 2, axis=-1)
    ml_if = ml_if + ml_gate_b
    h_ml, C_new, n_new, m_new = mlstm_chunkwise(
        heads(ml_q, ML_HEADS), heads(ml_k, ML_HEADS), heads(ml_v, ML_HEADS),
        ml_if[..., :ML_HEADS], ml_if[..., ML_HEADS:], C0, n0, m0)
    h_ml = jax.nn.sigmoid(ml_o) * (head_layernorm(h_ml, EPS).reshape(B, T, ML_W) * ml_norm_w)
    y_rw, S_new, shift_new = rwkv7_branch(rw_pre, shift0, S0, rw_mu, rw_w0, rw_w2, rw_a0, rw_a2, rw_g2,
                                          rw_kk, rw_ka, rw_rk, rw_ln_w, rw_ln_b)
    y_xa = memory_attention(heads(xa_q, XA_HEADS), mem_k, mem_v).reshape(B, T, XA_W)
    branches = jnp.stack([h_ml, y_rw, y_xa], axis=2)
    bproj = jnp.einsum('btnc,ncd->btnd', branches, w_branch)
    gates = jax.nn.sigmoid(gate_pre.reshape(B, T, N_BRANCH, D_MODEL))
    x = x + jnp.sum(gates * bproj, axis=2) @ w_out
    x = x + peer(rmsnorm(x, norm_ffn), pk_wq, pk_k1, pk_k2, pk_u, pk_v)
    return x, (C_new, n_new, m_new, conv_new, S_new, shift_new)

def setup_inputs(seed: int = 0) -> dict:
    key = jax.random.key(seed)
    ks = iter(jax.random.split(key, 48))
    f32 = jnp.float32

    def nrm(shape, scale):
        return jax.random.normal(next(ks), shape, f32) * scale

    def unif(shape, lo, hi):
        return jax.random.uniform(next(ks), shape, f32, lo, hi)

    L = DEPTH
    return {
        'x_prompt': nrm((BATCH, SEQ, D_MODEL), 1.0),
        'x_sample': nrm((DEC_BATCH, DEC_SEQ, D_MODEL), 1.0),
        'state_mlstm_C': nrm((L, DEC_BATCH, ML_HEADS, ML_DH, ML_DH), 0.3),
        'state_mlstm_n': nrm((L, DEC_BATCH, ML_HEADS, ML_DH), 0.3),
        'state_mlstm_m': nrm((L, DEC_BATCH, ML_HEADS), 1.0),
        'state_mlstm_conv': nrm((L, DEC_BATCH, ML_CONV - 1, 2 * ML_W), 1.0),
        'state_rwkv_S': nrm((L, DEC_BATCH, RW_HEADS, RW_DH, RW_DH), 0.3),
        'state_rwkv_shift': nrm((L, DEC_BATCH, RW_IN), 1.0),
        'cache_mem_k': nrm((L, DEC_BATCH, N_MEM, XA_HEADS, XA_DH), 1.0),
        'cache_mem_v': nrm((L, DEC_BATCH, N_MEM, XA_HEADS, XA_DH), 1.0),
        'mem_prompt': nrm((BATCH, N_MEM, D_MODEL), 1.0),
        'norm_mix': 1.0 + nrm((L, D_MODEL), 0.02),
        'w_in': nrm((L, D_MODEL, IN_W), D_MODEL ** -0.5),
        'ml_conv_w': nrm((L, ML_CONV, 2 * ML_W), 0.5),
        'ml_conv_b': nrm((L, 2 * ML_W), 0.02),
        'ml_gate_b': nrm((L, 2 * ML_HEADS), 0.3) + jnp.repeat(jnp.array([0.0, 3.0], f32), ML_HEADS),
        'ml_norm_w': 1.0 + nrm((L, ML_W), 0.02),
        'rw_mu': unif((L, RW_IN), 0.0, 1.0),
        'rw_w0': -1.5 + nrm((L, RW_W), 0.5),
        'rw_w2': nrm((L, RW_LORA_W, RW_W), 0.1),
        'rw_a0': nrm((L, RW_W), 0.1),
        'rw_a2': nrm((L, RW_LORA_A, RW_W), 0.1),
        'rw_g2': nrm((L, RW_LORA_G, RW_W), RW_LORA_G ** -0.5),
        'rw_kk': 1.0 + nrm((L, RW_W), 0.1),
        'rw_ka': 1.0 + nrm((L, RW_W), 0.1),
        'rw_rk': nrm((L, RW_HEADS, RW_DH), 0.1),
        'rw_ln_w': 1.0 + nrm((L, RW_W), 0.02),
        'rw_ln_b': nrm((L, RW_W), 0.02),
        'mem_norm': 1.0 + nrm((L, D_MODEL), 0.02),
        'w_mk': nrm((L, D_MODEL, XA_W), D_MODEL ** -0.5),
        'w_mv': nrm((L, D_MODEL, XA_W), D_MODEL ** -0.5),
        'w_branch': nrm((L, N_BRANCH, BR_W, D_MODEL), BR_W ** -0.5),
        'w_out': nrm((L, D_MODEL, D_MODEL), D_MODEL ** -0.5),
        'norm_ffn': 1.0 + nrm((L, D_MODEL), 0.02),
        'pk_wq': nrm((L, D_MODEL, PK_HEADS * PK_DKEY), D_MODEL ** -0.5),
        'pk_k1': nrm((L, PK_NKEYS, PK_DKEY // 2), (PK_DKEY // 2) ** -0.5),
        'pk_k2': nrm((L, PK_NKEYS, PK_DKEY // 2), (PK_DKEY // 2) ** -0.5),
        'pk_u': nrm((L, PK_N_EXP, D_MODEL), D_MODEL ** -0.5),
        'pk_v': nrm((L, PK_N_EXP, D_MODEL), 0.3),
        'norm_final': 1.0 + nrm((D_MODEL,), 0.02),
    }

def reference(x_prompt, x_sample, state_mlstm_C, state_mlstm_n, state_mlstm_m, state_mlstm_conv,
              state_rwkv_S, state_rwkv_shift, cache_mem_k, cache_mem_v, mem_prompt,
              norm_mix, w_in, ml_conv_w, ml_conv_b, ml_gate_b, ml_norm_w,
              rw_mu, rw_w0, rw_w2, rw_a0, rw_a2, rw_g2, rw_kk, rw_ka, rw_rk, rw_ln_w, rw_ln_b,
              mem_norm, w_mk, w_mv, w_branch, w_out, norm_ffn, pk_wq, pk_k1, pk_k2, pk_u, pk_v,
              norm_final):
    f32 = jnp.float32
    bp = x_prompt.shape[0]
    xp, xs = x_prompt, x_sample
    p_st, s_st = [], []
    for l in range(DEPTH):
        lw = (norm_mix[l], w_in[l], ml_conv_w[l], ml_conv_b[l], ml_gate_b[l], ml_norm_w[l],
              rw_mu[l], rw_w0[l], rw_w2[l], rw_a0[l], rw_a2[l], rw_g2[l], rw_kk[l], rw_ka[l], rw_rk[l],
              rw_ln_w[l], rw_ln_b[l], w_branch[l], w_out[l], norm_ffn[l],
              pk_wq[l], pk_k1[l], pk_k2[l], pk_u[l], pk_v[l])
        mk, mv = memory_kv(mem_prompt, mem_norm[l], w_mk[l], w_mv[l])
        xp, stp = trunk_layer(
            xp, mk, mv,
            jnp.zeros((bp, ML_HEADS, ML_DH, ML_DH), f32), jnp.zeros((bp, ML_HEADS, ML_DH), f32),
            jnp.zeros((bp, ML_HEADS), f32), jnp.zeros((bp, ML_CONV - 1, 2 * ML_W), f32),
            jnp.zeros((bp, RW_HEADS, RW_DH, RW_DH), f32), jnp.zeros((bp, RW_IN), f32), lw)
        p_st.append(stp + (mk, mv))
        xs, sts = trunk_layer(xs, cache_mem_k[l], cache_mem_v[l], state_mlstm_C[l], state_mlstm_n[l],
                              state_mlstm_m[l], state_mlstm_conv[l], state_rwkv_S[l], state_rwkv_shift[l], lw)
        s_st.append(sts)
    y_prompt = rmsnorm(xp, norm_final)
    y_sample = rmsnorm(xs, norm_final)

    def stk(sts, i):
        return jnp.stack([st[i] for st in sts])

    return (y_prompt, y_sample,
            stk(p_st, 0), stk(p_st, 1), stk(p_st, 2), stk(p_st, 3), stk(p_st, 4), stk(p_st, 5),
            stk(p_st, 6), stk(p_st, 7),
            stk(s_st, 0), stk(s_st, 1), stk(s_st, 2), stk(s_st, 3), stk(s_st, 4), stk(s_st, 5))


_drawn_inputs = setup_inputs


def setup_inputs(seed=0):
    import zlib

    import numpy as np

    out = dict(_drawn_inputs(seed))
    spreads = {}
    factors = {'ml_norm_w': 59.792,
     'rw_ln_w': 65.322,
     'rw_ln_b': 61.772,
     'mem_norm': 7.563,
     'norm_final': 20.092,
     'norm_ffn': 19.442,
     'cache_mem_k': 7.963,
     'cache_mem_v': 6.123,
     'rw_rk': 5.668}
    for name, (base, spread) in spreads.items():
        noise = np.random.default_rng([zlib.crc32(name.encode()), seed]).standard_normal(out[name].shape)
        drawn = base * np.exp(spread * noise) if base else spread * noise
        out[name] = jnp.asarray(drawn.astype(out[name].dtype))
    for name, factor in factors.items():
        out[name] = (out[name] * factor).astype(out[name].dtype)
    return out
```

```python
from contextlib import ExitStack

import concourse.bass as bass
from concourse import mybir

F32 = mybir.dt.float32
U32 = mybir.dt.uint32
I32 = mybir.dt.int32
ALU = mybir.AluOpType
ACT = mybir.ActivationFunctionType
AX_X = mybir.AxisListType.X

P = 128
D = 1024
DT = D // P
TP = 512
NB, NS = 8, 4
TS = NB * NS
T = TP + TS
NTT = TP // P + 1
MH = 4
RH, RD = 8, 64
RP = RH // 2
CH = 64
NC = TP // CH
NMEM = 256
NRW = 14
PH, PK, NK = 8, 16, 128
EPS = 1e-6
GN_EPS = 64e-5
SCALE = float(P) ** -0.5
DECAY = -float.fromhex("0x1.368b2fc6f9609p-1")
LOW = -3.0e38
COLS = [(0, TP), (TP, TS)]

OFF_QK, OFF_V, OFF_O, OFF_IF, OFF_RW = 0, 1024, 1536, 2048, 2056
OFF_XQ = OFF_RW + NRW * P
OFF_GATE = OFF_XQ + 512
NW = 6
NSLOT = 4

VEC = {}
_at = 0
for _name, _n in [("norm_mix", 8), ("conv_w", 32), ("conv_b", 8), ("ml_norm", 4), ("mu", 14), ("w0", 4), ("a0", 4),
                  ("kk", 4), ("ka", 4), ("rk", 4), ("ln_w", 4), ("ln_b", 4), ("mem_norm", 8), ("norm_ffn", 8),
                  ("norm_final", 8)]:
    VEC[_name] = _at
    _at += _n
NVEC = _at

EB = 32
NEB = T // EB
EG = 4
NG = NK // EG
AREN = 28400


def product_order():
    o = ["ms0"] + [f"qk{n}" for n in range(8)] + [f"v{t}" for t in range(NTT)] + [f"o{h}" for h in range(MH)]
    o += ["gi", "gf", "gt"]
    for h in range(MH):
        o += [f"mb{h}"] + [f"s{h}_{i}" for i in range(4)] + [f"n{h}", f"m{h}", f"kt{h}", f"c{h}", f"cs{h}", f"t{h}"]
    o += [f"r{n}" for n in range(NRW)]
    for p in range(RP):
        o += [f"w{p}", f"a{p}", f"kn{p}", f"bn{p}"]
    for c in range(NC):
        o += [f"ab{c}", f"nt{c}"] + [f"i{c}_{i}" for i in range(1, 11)]
        o += [f"vt{c}", f"bt{c}", f"u{c}", f"uu{c}", f"y{c}"]
    o += ["abs", "nts", "is1", "is2", "vts", "bts", "us", "uus", "ys"] + [f"ss{p}" for p in range(RP)]
    for p in range(RP):
        o += [f"ym{p}", f"yv{p}", f"g{p}"]
    o += ["ms1"] + [f"mk{h}" for h in range(MH)] + ["mv0", "mv1"] + [f"xq{h}" for h in range(MH)]
    for h in range(MH):
        o += [f"as{h}", f"at{h}", f"ao{h}"]
    o += [f"ds{h}" for h in range(MH)] + ["dt"] + [f"do{h}" for h in range(MH)]
    for n in range(DT):
        for j in range(3):
            o += [f"gg{n}_{j}", f"gb{n}_{j}"]
    o += [f"x{n}" for n in range(DT)]
    o += ["ms2"] + [f"pq{i}" for i in range(16)]
    for t in range(NTT):
        o += [f"ps{t}_0", f"ps{t}_1", f"pt{t}"]
    return o + ["ms3"]


ORDER = product_order()
NO = {k: i for i, k in enumerate(ORDER)}
NPROD = len(ORDER)


def weight_stream():
    s = [(f"qk{n}", "w_in", 0, DT, OFF_QK + n * P, P, f"qk{n}") for n in range(8)]
    s += [(f"v{c}", "w_in", 0, DT, OFF_V + c * P, P, f"v{NTT - 1}") for c in range(4)]
    s += [(f"o{h}", "w_in", 0, DT, OFF_O + h * P, P, f"o{h}") for h in range(MH)]
    s += [("if", "w_in", 0, DT, OFF_IF, 8, "gf")]
    s += [(f"r{n}", "w_in", 0, DT, OFF_RW + n * P, P, f"r{n}") for n in range(NRW)]
    s += [(f"mk{h}", "w_mk", 0, DT, h * P, P, f"mk{h}") for h in range(MH)]
    s += [(f"mv{c}", "w_mv", 0, DT, c * P, P, "mv1") for c in range(4)]
    s += [(f"xq{h}", "w_in", 0, DT, OFF_XQ + h * P, P, f"xq{h}") for h in range(MH)]
    for n in range(DT):
        for j in range(3):
            s += [(f"gg{n}_{j}", "w_in", 0, DT, OFF_GATE + j * D + n * P, P, f"gg{n}_{j}")]
            s += [(f"gb{n}_{j}", "w_branch", 4 * j, 4, n * P, P, f"gb{n}_{j}")]
    s += [(f"x{n}", "w_out", 0, DT, n * P, P, f"x{n}") for n in range(DT)]
    s += [(f"pq{i}", "wq", 0, DT, i * P, P, f"pq{i}") for i in range(16)]
    return s


WS = weight_stream()
WNO = {w[0]: i for i, w in enumerate(WS)}


def bc(ap, axis, n):
    a = ap.unsqueeze(axis)
    shape = list(a.shape)
    shape[axis] = n
    return a.to_broadcast(shape)


class Steps:

    def __init__(self, eng, own):
        self.eng, self.own, self.n = eng, own, {}

    def __call__(self, ins, sem=None):
        sem = self.own if sem is None else sem
        k = id(sem)
        self.n[k] = self.n.get(k, 0) + 1
        ins.then_inc(sem, 1)
        self.eng.wait_ge(sem, self.n[k])


def hybrid_layer(nc, a, o):
    ctx = ExitStack()
    with ctx:
        def sb(name, shape, dt=F32):
            return ctx.enter_context(nc.sbuf_tensor(name, shape, dt))

        sems = {}

        def S(name):
            if name not in sems:
                sems[name] = ctx.enter_context(nc.semaphore(name))
            return sems[name]

        XT = sb("XT", [P, DT, T])
        HT = sb("HT", [P, DT, T])
        BR = sb("BR", [P, 12, T])
        W = sb("W", [P, NW, DT, P])
        vec = sb("vec", [P, NVEC])
        ident = sb("ident", [P, P])
        ones = sb("ones", [P, P])
        blk = sb("blk", [P, P])
        tri = sb("tri", [P, P])
        rmask = sb("rmask", [P, 2, CH])
        low = sb("low", [CH, CH])
        b16 = sb("b16", [CH, CH])
        smask = sb("smask", [TS, TS])
        slow = sb("slow", [TS, TS])
        srm = sb("srm", [2 * TS, 2, TS])
        bmask = sb("bmask", [P, NB, TS])
        bexp = sb("bexp", [2 * TS, NB])
        reset = sb("reset", [P, T])
        sel = sb("sel", [MH, MH, P])
        iota = sb("iota", [P, P])
        rstd = sb("rstd", [P, T])
        arena = sb("arena", [P, AREN])
        PS = ctx.enter_context(nc.psum_tensor("PS", [P, NSLOT, 2, 512], F32))

        def carve(at, *shapes):
            out = []
            for shape in shapes:
                n = 1
                for d in shape:
                    n *= d
                v = arena[:, at:at + n]
                if len(shape) > 1:
                    names = "abcd"[:len(shape)]
                    v = v.rearrange("p (" + " ".join(names) + ") -> p " + " ".join(names),
                                    **{names[i]: shape[i] for i in range(len(shape) - 1)})
                out.append(v)
                at += n
            assert at <= AREN, at
            return out + [at]

        (QKP, QK, VX, SO, CN, CO, MB, DD, DS, NU, HH, SQ, KW, VB, QM, QS, GTM, CT, CHI, s1, s2, s3, s4, EI, GB, M0, MO, EIL,
         _) = carve(0, (8, 3 + TP + NB * 7), (8, T), (NTT, MH, 129), (MH, T), (MH, NB, 129), (MH, 129), (T + TS,),
                    (4, 512), (TS,), (NTT, 129), (NTT, P), (NTT, P), (NTT, P), (NB, 129), (NB, TS), (TS,),
                    (NTT, 3, MH), (8, 27), (8, 24), (NTT,), (NTT,), (NTT,), (NTT,), (TS,), (2,), (NB,), (1 + NB,), (NB,))
        CV = DD.rearrange("p a b -> p (a b)")[:, 0:2 * T].rearrange("p (a b) -> p a b", a=2)
        rows = QKP.rearrange("p a b -> p (a b)")[0:MH, 0:8 * T].rearrange("p (a b) -> p a b", a=8)
        IR, FR, LR, FC, GR, MR, MT, EM = [rows[:, i, :] for i in range(8)]
        ONR, WG = EM, LR

        RW, AR, BK, ARS, BKS, WA, G2, S0, ST, WE, WES, LO, SH, bt = carve(
            0, (NRW, T), (RP, NC, 2, CH), (RP, NC, 2, CH), (RP, 2, TS), (RP, 2, TS), (512,), (512,), (RP, NB, RD),
            (RP, RD), (RP, NC), (RP, NB), (NRW, 9), (NRW, NB))
        RPD, TW, LW, AG, KN, SQB, CC, EW, EN, EP, KPB, OMK, _ = carve(
            bt, (2, 1 + TP + NB * 5), (T,), (T,), (T,), (T,), (T,), (T,), (T,), (T,), (T,), (T,), (RP,))
        AB, PQ, PQD, PQ2, XX, MM, U0S, UV, BKT, _ = carve(
            bt, (RH, 2 * CH), (2, RH, CH), (2, RH, CH), (2, RH, CH), (2, RH, CH), (2, RH, CH), (RH, CH), (RH, RD),
            (RP, P))
        ABS, QSS, MS, XS, AM, UVS, BKTS, UVE, _ = carve(
            bt, (RH, 2 * TS), (RH, TS), (RH, TS), (RH, TS), (2, RP, NB, TS), (RH, RD), (RP, P), (2, NB, RD))
        YC, YQ, _ = carve(bt, (T,), (T,))

        (MEM, MN, MKT, MV, XQ, PA, PAT, KB, VBM, XM, PM, PT3, c1, c2, c3, _) = carve(
            0, (DT, NMEM), (DT, NMEM), (MH, NMEM), (2, 512), (MH, T), (4, NMEM), (2, 512), (2, NB * NMEM),
            (2, NB * NMEM), (MH, NB, TS), (2, MH, NB, TS), (2, P), (4,), (4,), (4,))

        SGB, TMP, YM, _ = carve(0, (3, T), (2, T), (DT, T))

        IT, = carve(AREN - 3 * T, (3, T))[:1]
        (QT, SC, SC2, V16, IX, IF, CAND, CAND2, EQ, TOP, PX, PAX, PBX, AFX, BFX, KSEL, GAT, e1, e2, _) = carve(
            0, (16, T), (16, P), (P,), (16, PK), (16, PK), (16, PK), (PH, PK, PK), (PK * PK,), (P, PK), (PH, PK),
            (PH, PK), (P,), (P,), (P,), (P,), (2, P), (PH, PK), (PH,), (PH,))
        IX, PX, PAX, PBX = [x.bitcast(U32) for x in (IX, PX, PAX, PBX)]

        UB, VU, fg, = carve(0, (2, EG, DT, P), (2, EG, D))
        OH, GST, _ = carve(fg, (8, 2, P), (2, P, EB))
        GQ, AC, _ = carve(fg, (2, NEB, EG, EB), (2, EG, T))

        gate_table = nc.dram_tensor("gate_table", [NG, P, NEB * EG * EB], F32, kind="Internal").ap()

        mm = S("mm")
        ev = [S(f"ev{i}") for i in range(NSLOT)]
        wl = [S(f"wl{i}") for i in range(NW)]
        ld = S("ld")
        bar = S("bar")

        def slot(key):
            return PS[:, NO[key] % NSLOT]

        def take(eng, key):
            eng.wait_ge(mm, NO[key] + 1)
            return slot(key)

        def give(eng, ins, key):
            s = ev[NO[key] % NSLOT]
            ins.then_inc(s, 1)
            eng.wait_ge(s, NO[key] // NSLOT + 1)

        def barrier(eng, k):
            eng.sem_inc(bar, 1)
            eng.wait_ge(bar, 4 * k + max(0, k - 4))

        def tcols(t):
            return (t * P, P) if t < NTT - 1 else (TP, TS)

        def v(name, i):
            return vec[:, VEC[name] + i:VEC[name] + i + 1]

        block = ctx.enter_context(nc.Block())

        @block.sync
        def _(sp):
            sp.dma_start(XT[:], a["xT"].rearrange("(k p) t -> p k t", p=P)).then_inc(S("ldx"), 16)
            sp.dma_start(vec[:], a["vecs"]).then_inc(S("ldv"), 16)
            for i, (_, name, k0, nk, c0, wd, _) in enumerate(WS):
                if i >= NW:
                    sp.wait_ge(mm, NO[WS[i - NW][6]] + 1)
                src = a[name][k0 * P:(k0 + nk) * P, c0:c0 + wd].rearrange("(k p) n -> p k n", p=P)
                sp.dma_start(W[:, i % NW, 0:nk, 0:wd], src).then_inc(wl[i % NW], 16)
            barrier(sp, 5)

            def load_u(g, b):
                sp.dma_start(UB[:, b], a["uT"][:, bass.ds(g * EG, EG)]).then_inc(S(f"ul{b}"), 16)

            def load_v(g, b):
                sp.dma_start(VU[:, b], a["vT"][:, bass.ds(g * EG, EG)]).then_inc(S(f"vl{b}"), 16)

            def load_g(g, b):
                sp.dma_start(GQ[:, b].rearrange("p a b c -> p (a b c)"),
                             gate_table[bass.ds(g, 1)].rearrange("a p n -> p (a n)")).then_inc(S(f"gl{b}"), 16)

            for b in range(2):
                load_u(b, b)
                load_v(b, b)
            for k in range(NEB):
                sp.wait_ge(S("ge"), 4 * (k + 1))
                sp.dma_start(gate_table[:, :, k * EG * EB:(k + 1) * EG * EB].rearrange("g p n -> p g n"),
                             GST[:, k % 2].rearrange("p (g e) t -> p g (e t)", e=EG)).then_inc(S(f"gw{k % 2}"), 16)
            sp.wait_ge(S("gw0"), 16 * ((NEB + 1) // 2))
            sp.wait_ge(S("gw1"), 16 * (NEB // 2))
            barrier(sp, 6)
            for b in range(2):
                load_g(b, b)
            with sp.Fori(1, NG // 2) as j:
                for b in range(2):
                    sp.wait_ge(S("pa"), 8 * j + 4 * b - 4)
                    load_u(2 * j + b, b)
                    sp.wait_ge(S("wr"), 8 * j + 4 * b - 4)
                    load_g(2 * j + b, b)
                    sp.wait_ge(S("po"), 16 * j + 8 * b - 8)
                    load_v(2 * j + b, b)
            sp.wait_ge(S("hn"), 4)
            sp.dma_start(o["yT"].rearrange("(k p) t -> p k t", p=P), HT[:]).then_inc(S("oy"), 16)
            sp.wait_ge(S("oy"), 16)

        @block.gpsimd
        def _(pool):
            step = Steps(pool, S("pl"))

            def fill(tile, value):
                step(pool.memset(tile, value))

            def keep(tile, pattern, base, row):
                step(pool.affine_select(out=tile, in_=tile, compare_op=ALU.is_ge, fill=0.0, base=base,
                                        pattern=pattern, channel_multiplier=row))

            fill(ident[:], 0.0)
            step(pool.affine_select(out=ident[:], in_=ident[:], compare_op=ALU.not_equal, fill=1.0, base=0,
                                    pattern=[[-1, P]], channel_multiplier=1))
            fill(ones[:], 1.0)
            fill(blk[:], 0.0)
            for h in range(2):
                fill(blk[h * RD:(h + 1) * RD, h * RD:(h + 1) * RD], 1.0)
            fill(tri[:], 1.0)
            keep(tri[:], [[1, P]], 0, -1)
            fill(rmask[:], 1.0)
            for r in range(2):
                for x in range(2):
                    keep(rmask[r * CH:(r + 1) * CH, x, :], [[1, CH]], x - 1, -1)
            fill(low[:], 1.0)
            keep(low[:], [[-1, CH]], -1, 1)
            fill(b16[:], 1.0)
            b16v = b16[:].rearrange("p (a b) -> p a b", b=16)
            keep(b16v, [[-16, CH // 16], [0, 16]], 0, 1)
            keep(b16v, [[16, CH // 16], [0, 16]], 15, -1)
            fill(smask[:], 1.0)
            keep(smask[:].rearrange("p (a b) -> p a b", b=NS), [[-NS, NB], [0, NS]], 0, 1)
            keep(smask[:], [[1, TS]], 0, -1)
            fill(slow[:], 1.0)
            keep(slow[:].rearrange("p (a b) -> p a b", b=NS), [[NS, NB], [0, NS]], NS - 1, -1)
            keep(slow[:], [[-1, TS]], -1, 1)
            fill(srm[:], 1.0)
            for r in range(2):
                for x in range(2):
                    m = srm[r * TS:(r + 1) * TS, x, :]
                    keep(m.rearrange("p (a b) -> p a b", b=NS), [[-NS, NB], [0, NS]], 0, 1)
                    keep(m, [[1, TS]], x - 1, -1)
            fill(bmask[:], 0.0)
            for b in range(NB):
                fill(bmask[:, b, b * NS:(b + 1) * NS], 1.0)
            fill(bexp[:], 1.0)
            for r in range(2):
                m = bexp[r * TS:(r + 1) * TS, :]
                keep(m, [[-NS, NB]], 0, 1)
                keep(m, [[NS, NB]], NS - 1, -1)
            fill(reset[:], 1.0)
            fill(reset[:, 0:TP].rearrange("p (a b) -> p a b", b=CH)[:, :, 0:1], 0.0)
            fill(reset[:, TP:T].rearrange("p (a b) -> p a b", b=NS)[:, :, 0:1], 0.0)
            fill(sel[:], 1.0)
            keep(sel[:], [[-1, MH], [0, P]], 0, 1)
            keep(sel[:], [[1, MH], [0, P]], 0, -1)
            step(pool.iota(iota[:], [[1, P]], base=0, channel_multiplier=0, allow_small_or_imprecise_dtypes=True))
            for n in range(8):
                fill(QKP[:, n, 0:3], 0.0)
            fill(VX[:, :, :, P:P + 1], 1.0)
            fill(NU, 0.0)
            fill(GTM, 1.0)
            pool.sem_inc(S("const"), 1)
            for dst, src, n in ((CHI, "convT", "ldc"), (CN, "cnT", "ldn"), (M0[0:MH], "m0T", "ldm"),
                                (GB[0:MH], "gateb", "ldg")):
                pool.dma_start(dst, a[src]).then_inc(S(n), 16)
            pool.wait_ge(S("ctail"), 8)
            pool.dma_start(o["conv"], CT).then_inc(S("oa"), 16)
            pool.wait_ge(S("gates"), 1)
            pool.dma_start(o["m"], MO[0:MH]).then_inc(S("oa"), 16)
            pool.wait_ge(S("cnew"), MH)
            pool.dma_start(o["cn"], CO).then_inc(S("oa"), 16)
            pool.dma_start(o["cns"], CN).then_inc(S("oa"), 16)
            pool.wait_ge(S("oa"), 64)
            barrier(pool, 1)
            for i in range(2):
                fill(RPD[:, i, 0:1], 0.0)
            fill(ST, 0.0)
            pool.sem_inc(S("rzero"), 1)
            for dst, src, n in ((SH, "shT", "ldsh"), (WA, "wa", "ldwa"), (G2, "g2", "ldg2"), (S0, "s0T", "lds0")):
                pool.dma_start(dst, a[src]).then_inc(S(n), 16)
            pool.wait_ge(S("rwin"), 2 * NRW)
            pool.dma_start(o["shift"], LO).then_inc(S("ob"), 16)
            pool.wait_ge(S("stnew"), NC)
            pool.dma_start(o["S"], ST).then_inc(S("ob"), 16)
            pool.wait_ge(S("s0new"), RP)
            pool.dma_start(o["Ss"], S0).then_inc(S("ob"), 16)
            pool.wait_ge(S("ob"), 48)
            barrier(pool, 2)
            pool.dma_start(MEM, a["memT"].rearrange("(k p) t -> p k t", p=P)).then_inc(S("ldmem"), 16)
            for r in range(2):
                for h in (2 * r, 2 * r + 1):
                    if r:
                        pool.wait_ge(mm, NO[f"ds{h - 2}"] + 1)
                    pool.dma_start(KB[:, h % 2], a["memkT"][:, h]).then_inc(S(f"ldk{h % 2}"), 16)
                for h in (2 * r, 2 * r + 1):
                    if r:
                        pool.wait_ge(mm, NO[f"do{h - 2}"] + 1)
                    pool.dma_start(VBM[:, h % 2], a["memv"][:, h]).then_inc(S(f"ldvv{h % 2}"), 16)
            pool.wait_ge(S("mkv"), MH + 2)
            pool.dma_start(o["mk"], MKT).then_inc(S("oc"), 16)
            pool.dma_start(o["mv"], MV).then_inc(S("oc"), 16)
            pool.wait_ge(S("oc"), 32)
            barrier(pool, 3)
            barrier(pool, 4)
            pool.dma_start(KSEL, a["keysT"]).then_inc(S("ldkeys"), 16)
            barrier(pool, 5)
            barrier(pool, 6)

        @block.scalar
        def _(act):
            step = Steps(act, S("ac"))

            def f(out, in_, func, sem=None, bias=None, scale=None):
                kw = {}
                if bias is not None:
                    kw["bias"] = bias
                if scale is not None:
                    kw["scale"] = scale
                step(nc.scalar.activation(out, in_, func, **kw), sem)

            def out_of(key, out, in_, func, **kw):
                give(act, nc.scalar.activation(out, in_, func, **kw), key)

            def both(key, dst, func, sem=None, **kw):
                ps = take(act, key)
                m = dst.shape[0]
                f(dst[:, 0:TP], ps[0:m, 0, :], func, **kw)
                out_of(key, dst[:, TP:T], ps[0:m, 1, 0:TS], func, **kw)
                if sem is not None:
                    act.sem_inc(sem, 1)

            def root(i, n):
                act.wait_ge(S("rc"), i + 1)
                f(rstd[:, 0:n], rstd[:, 0:n], ACT.Sqrt, S("rs"))

            act.wait_ge(S("ldx"), 16)
            f(HT[:], XT[:], ACT.Square, S("sq"))
            root(0, T)
            act.wait_ge(S("const"), 1)
            act.wait_ge(S("ldc"), 16)
            for n in range(9):
                if n < 8:
                    ps = take(act, f"qk{n}")
                    f(QKP[:, n, 3:3 + TP], ps[:, 0, :], ACT.Copy)
                    q = QKP[:, n, 3 + TP:].rearrange("p (b t) -> p b t", b=NB)
                    f(q[:, :, 0:3], CHI[:, n, :].rearrange("p (b t) -> p b t", b=NB), ACT.Copy)
                    out_of(f"qk{n}", q[:, :, 3:7], ps[:, 1, 0:TS].rearrange("p (b t) -> p b t", b=NB), ACT.Copy)
                    f(CT[:, n, 0:3], QKP[:, n, TP:TP + 3], ACT.Copy)
                    f(CT[:, n, 3:27].rearrange("p (b t) -> p b t", b=NB), q[:, :, 4:7], ACT.Copy, S("ctail"))
                if n:
                    act.wait_ge(S("cv"), n)
                    f(QK[:, n - 1, :], CV[:, (n - 1) % 2, :], ACT.Silu, S("silu"))
            for t in range(NTT):
                _, m = tcols(t)
                ps = take(act, f"v{t}")
                out_of(f"v{t}", VX[0:m, t, :, 0:P], ps[0:m, 0, :].rearrange("p (h d) -> p h d", h=MH), ACT.Copy)
                act.sem_inc(S("vx"), 1)
            for h in range(MH):
                both(f"o{h}", SO[:, h, :], ACT.Sigmoid)
            act.wait_ge(S("gi"), 1)
            f(LR, FR, ACT.Abs)
            f(LR, LR, ACT.Exp, scale=-1.0)
            f(LR, LR, ACT.Ln, S("ls"), bias=1.0)
            act.wait_ge(S("gi"), 2)
            f(EM, MT, ACT.Exp, S("grows"), scale=-1.0)
            f(WG, WG, ACT.Exp)
            f(EI[0:MH], EI[0:MH], ACT.Exp, S("wg"))
            for h in range(MH):
                both_done = take(act, f"mb{h}")
                if h:
                    act.wait_ge(S("hnorm"), h)
                f(MB[:, 0:TP], both_done[:, 0, :], ACT.Copy)
                out_of(f"mb{h}", MB[:, TP:T + TS], both_done[:, 1, 0:2 * TS], ACT.Copy)
                act.sem_inc(S("mbr"), 1)
                for i in range(4):
                    act.wait_ge(S("dd"), 5 * h + i + 1)
                    f(DD[:, i, i * P:TP], DD[:, i, i * P:TP], ACT.Exp, S("ddx"), scale=-1.0)
                act.wait_ge(S("dd"), 5 * h + 5)
                f(DS[0:TS], DS[0:TS], ACT.Exp, S("ddx"), scale=-1.0)
                act.wait_ge(S("hv"), h + 1)
                f(s3, s3, ACT.Sqrt, S("hs"))
            barrier(act, 1)

            act.wait_ge(S("rzero"), 1)
            act.wait_ge(S("ldsh"), 16)
            for n in range(NRW):
                ps = take(act, f"r{n}")
                if n >= 2:
                    act.wait_ge(S("rsh"), n - 1)
                r = RPD[:, n % 2, :]
                q = r[:, 1 + TP:].rearrange("p (b t) -> p b t", b=NB)
                f(r[:, 1:1 + TP], ps[:, 0, :], ACT.Copy)
                f(q[:, :, 0], SH[:, n, :], ACT.Copy)
                out_of(f"r{n}", q[:, :, 1:5], ps[:, 1, 0:TS].rearrange("p (b t) -> p b t", b=NB), ACT.Copy)
                f(LO[:, n, 0:1], r[:, TP:TP + 1], ACT.Copy, S("rwin"))
                f(LO[:, n, 1:9], q[:, :, 4], ACT.Copy, S("rwin"))
            act.wait_ge(S("rsh"), NRW)
            f(TW[0:64], RW[0:64, 12, :], ACT.Tanh, S("tanh"))
            f(RW[:, 13, :], RW[:, 13, :], ACT.Sigmoid)
            for p in range(RP):
                if p:
                    act.wait_ge(S("rwops"), p)
                both(f"w{p}", LW, ACT.Sigmoid, bias=v("w0", p))
                both(f"a{p}", AG, ACT.Sigmoid, bias=v("a0", p))
                act.sem_inc(S("wa"), 1)
                act.wait_ge(S("kv"), p + 1)
                f(KN, KN, ACT.Sqrt, S("ks"))
                act.wait_ge(S("cum"), p + 1)
                f(EW, CC, ACT.Exp)
                f(EN, CC, ACT.Exp, scale=-1.0)
                f(EP, EP, ACT.Exp, S("dec"))
            for c in range(NC + 1):
                key, n = (f"y{c}", CH) if c < NC else ("ys", TS)
                ps = take(act, key)
                dst, src = RW[:, 4:8, c * CH:c * CH + n], ps[:, 0, 0:RP * n].rearrange("p (a b) -> p a b", a=RP)
                f(dst, src, ACT.Copy, S("yev"))
            for p in range(RP):
                act.wait_ge(S("yv"), p + 1)
                f(rstd[:], rstd[:], ACT.Sqrt, S("ysq"))
            barrier(act, 2)

            act.wait_ge(S("ldmem"), 16)
            f(MN, MEM, ACT.Square, S("sq"))
            root(1, NMEM)
            for h in range(MH):
                ps = take(act, f"mk{h}")
                out_of(f"mk{h}", MKT[:, h, :], ps[:, 0, 0:NMEM], ACT.Copy)
                act.sem_inc(S("mkv"), 1)
            for s in range(2):
                ps = take(act, f"mv{s}")
                out_of(f"mv{s}", MV[:, s, :], ps[:, 0, :], ACT.Copy)
                act.sem_inc(S("mkv"), 1)
            for h in range(MH):
                both(f"xq{h}", XQ[:, h, :], ACT.Copy)
                act.sem_inc(S("xq"), 1)
            for h in range(MH):
                act.wait_ge(S("sx"), h + 1)
                f(PA, PA, ACT.Exp, S("sxe"), scale=SCALE)
                ps = take(act, f"at{h}")
                if h:
                    act.wait_ge(mm, NO[f"ao{h - 1}"] + 1)
                out_of(f"at{h}", PAT, ps, ACT.Copy)
                act.sem_inc(S("pat"), 1)
                ps = take(act, f"ao{h}")
                out_of(f"ao{h}", BR[:, 8 + h, 0:TP], ps[:, 0, :], ACT.Copy)
            act.wait_ge(S("sx"), MH + 1)
            f(PA[:, 0, :], PA[:, 0, :], ACT.Exp, S("sxe"), scale=SCALE)
            for h in range(MH):
                ps = take(act, f"do{h}")
                out_of(f"do{h}", BR[:, 8 + h, TP:T], ps[:, 0, 0:TS], ACT.Copy)
            barrier(act, 3)

            for n in range(DT):
                for j in range(3):
                    i = 3 * n + j
                    if i >= 3:
                        act.wait_ge(S("gated"), i - 2)
                    both(f"gg{n}_{j}", SGB[:, i % 3, :], ACT.Sigmoid, S("sgb"))
            barrier(act, 4)

            f(HT[:], XT[:], ACT.Square, S("sq"))
            root(2, T)
            for i in range(2 * PH):
                both(f"pq{i}", QT[:, i, :], ACT.Copy, S("pqe"))
            for t in range(NTT):
                _, m = tcols(t)
                if t:
                    act.wait_ge(S("scf"), t)
                for x in range(2):
                    ps = take(act, f"ps{t}_{x}")
                    out_of(f"ps{t}_{x}", SC[0:m, 8 * x:8 * x + 8, :],
                           ps[0:m].rearrange("p a (b n) -> p (a b) n", b=4), ACT.Copy)
                    act.sem_inc(S("sce"), 1)
                act.wait_ge(S("gx"), t + 1)
                f(GAT[0:m], GAT[0:m], ACT.Exp, S("gxe"))
            barrier(act, 5)

            def gate_block(i, b, write):
                if write is not None:
                    act.wait_ge(S(f"gw{b}"), write)
                for q in range(4):
                    act.wait_ge(S("ohf"), 8 * i + 2 * q + 2)
                    nc.scalar.activation(GST[:, b, :, q * 8:(q + 1) * 8].rearrange("p n t -> p t n"),
                                         PS[:, q].rearrange("p a (t n) -> p (a t) n", t=4), ACT.Copy).then_inc(S("ge"), 1)

            gate_block(0, 0, None)
            gate_block(1, 1, None)
            gate_block(2, 0, 16)
            with act.Fori(1, NEB // 2) as j:
                gate_block(2 * j + 1, 1, 16 * j)
                gate_block(2 * j + 2, 0, 16 * j + 16)
            act.wait_ge(S("ge"), 4 * NEB)
            barrier(act, 6)

            def gelus(g, b, done):
                if done is not None:
                    act.wait_ge(S("po"), done)
                for e in range(EG):
                    act.wait_ge(S("pa"), 4 * g + e + 1)
                    nc.scalar.activation(AC[:, b, e, :].rearrange("p (a n) -> p a n", a=2), PS[:, e, :, 0:T // 2],
                                         ACT.Gelu).then_inc(S("af"), 1)

            gelus(0, 0, None)
            gelus(1, 1, None)
            with act.Fori(1, NG // 2) as j:
                gelus(2 * j, 0, 16 * j - 8)
                gelus(2 * j + 1, 1, 16 * j)
            act.wait_ge(S("of"), 8 * NG)
            f(HT[:], XT[:], ACT.Square, S("sq"))
            root(3, T)

        @block.tensor
        def _(pe):
            made = [0]

            def room(key):
                assert ORDER[made[0]] == key, (ORDER[made[0]], key)
                made[0] += 1
                if NO[key] >= NSLOT:
                    pe.wait_ge(ev[NO[key] % NSLOT], NO[key] // NSLOT)
                return slot(key)

            def mul(out, lhsT, rhs, first=True, last=True):
                return nc.tensor.matmul(out, lhsT, rhs, start=first, stop=last)

            def turn(out, in_):
                n = in_.shape[0]
                return nc.tensor.transpose(out, in_, ident[0:n, 0:n])

            def weights(key):
                i = WNO[key]
                pe.wait_ge(wl[i % NW], 16 * (i // NW + 1))
                return W[:, i % NW]

            def both(ps, lhs, src, nk, m=P, last=True):
                for part, (c0, n) in enumerate(COLS):
                    for k in range(nk):
                        ins = mul(ps[0:m, part, 0:n], lhs(k), src(k)[:, c0:c0 + n], k == 0, k == nk - 1)
                return ins

            def project(key, src, nk=DT, wkey=None):
                w = weights(wkey or key)
                ps = room(key)
                both(ps, lambda k: w[:, k, :], src, nk).then_inc(mm, 1)

            def norm(i, src, n):
                pe.wait_ge(S("sq"), i + 1)
                ps = room(f"ms{i}")
                if n == T:
                    ins = both(ps, lambda k: ones[:], src, DT)
                else:
                    for k in range(DT):
                        ins = mul(ps[:, 0, 0:n], ones[:], src(k), k == 0, k == DT - 1)
                ins.then_inc(mm, 1)

            ht = lambda k: HT[:, k, :]

            pe.wait_ge(S("const"), 1)
            norm(0, ht, T)
            pe.wait_ge(S("hn"), 1)
            for n in range(8):
                project(f"qk{n}", ht)
            for t in range(NTT):
                c0, m = tcols(t)
                ps = room(f"v{t}")
                for c in range(4):
                    w = weights(f"v{c}")
                    for k in range(DT):
                        ins = mul(ps[0:m, 0, c * P:(c + 1) * P], HT[:, k, c0:c0 + m], w[:, k, :], k == 0, k == DT - 1)
                ins.then_inc(mm, 1)
            for h in range(MH):
                project(f"o{h}", ht)
            w = weights("if")
            for i, key in enumerate(("gi", "gf")):
                ps = room(key)
                both(ps, lambda k: w[:, k, i * MH:(i + 1) * MH], ht, DT, MH).then_inc(mm, 1)
            pe.wait_ge(S("grows"), 1)
            pe.wait_ge(S("wg"), 1)
            ps = room("gt")
            for t in range(NTT):
                c0, m = tcols(t)
                for i, r in enumerate((GR, EM, WG)):
                    ins = turn(ps[0:m, 0, (t * 3 + i) * MH:(t * 3 + i + 1) * MH], r[:, c0:c0 + m])
            ins.then_inc(mm, 1)
            for h in range(MH):
                ps = room(f"mb{h}")
                both(ps, lambda k: sel[:, h, :], lambda k: MR, 1)
                mul(ps[:, 1, TS:2 * TS], sel[:, h, :], EI[0:MH]).then_inc(mm, 1)
                qh, kh = QK[:, h, :], QK[:, MH + h, :]
                pe.wait_ge(S("silu"), 8)
                for i in range(4):
                    ps = room(f"s{h}_{i}")
                    ins = mul(ps[:, 0, 0:TP - i * P], kh[:, i * P:(i + 1) * P], qh[:, i * P:TP])
                    if i == 3:
                        ins = mul(ps[0:TS, 1, 0:TS], kh[:, TP:T], qh[:, TP:T])
                    ins.then_inc(mm, 1)
                pe.wait_ge(S("probs"), h + 1)
                pe.wait_ge(S("vx"), NTT)
                ps = room(f"n{h}")
                for t in range(4):
                    for i in range(t + 1):
                        ins = mul(ps[:, t // 2, (t % 2) * 256:(t % 2) * 256 + 129], DD[:, i, t * P:(t + 1) * P],
                                  VX[:, i, h, :], i == 0, i == t)
                ins.then_inc(mm, 1)
                ps = room(f"m{h}")
                mul(ps[0:TS, 0, 0:129], DS[0:TS], VX[0:TS, NTT - 1, h, :], True, False)
                pe.wait_ge(S("ldn"), 16)
                for b in range(NB):
                    ins = mul(ps[0:TS, 0, 0:129], QM[:, b, :], CN[:, h, b, :], False, b == NB - 1)
                ins.then_inc(mm, 1)
                ps = room(f"kt{h}")
                for t in range(NTT):
                    c0, m = tcols(t)
                    ins = turn(ps[0:m, t // 4, (t % 4) * P:(t % 4 + 1) * P], kh[:, c0:c0 + m])
                ins.then_inc(mm, 1)
                pe.wait_ge(S("kw"), h + 1)
                ps = room(f"c{h}")
                for t in range(4):
                    mul(ps[:, 0, 0:129], KW[:, t, :], VX[:, t, h, :], t == 0, t == 3)
                mul(ps[:, 1, 0:258], KW[0:TS, 4, :], VB[0:TS, 6:8, :].rearrange("p a b -> p (a b)")).then_inc(mm, 1)
                ps = room(f"cs{h}")
                for i in range(2):
                    ins = mul(ps[:, i, 0:387], KW[0:TS, 4, :], VB[0:TS, 3 * i:3 * i + 3, :].rearrange("p a b -> p (a b)"))
                ins.then_inc(mm, 1)
                pe.wait_ge(S("hnorm"), h + 1)
                ps = room(f"t{h}")
                for t in range(NTT):
                    c0, m = tcols(t)
                    ins = turn(ps[:, t // 4, (t % 4) * P:(t % 4) * P + m], HH[0:m, t, :])
                ins.then_inc(mm, 1)
            barrier(pe, 1)

            for n in range(NRW):
                project(f"r{n}", ht)
            pe.wait_ge(S("ldwa"), 16)
            for p in range(RP):
                if p == 0:
                    pe.wait_ge(S("tanh"), 1)
                ps = room(f"w{p}")
                both(ps, lambda k: WA[0:64, p * P:(p + 1) * P], lambda k: TW[0:64], 1).then_inc(mm, 1)
                ps = room(f"a{p}")
                both(ps, lambda k: WA[64:P, p * P:(p + 1) * P], lambda k: RW[64:P, 12, :], 1).then_inc(mm, 1)
                pe.wait_ge(S("kk2"), 2 * p + 1)
                ps = room(f"kn{p}")
                both(ps, lambda k: blk[:], lambda k: SQB, 1).then_inc(mm, 1)
                pe.wait_ge(S("kk2"), 2 * p + 2)
                ps = room(f"bn{p}")
                both(ps, lambda k: blk[:], lambda k: SQB, 1).then_inc(mm, 1)
            pe.wait_ge(S("rwops"), RP)
            for c in range(NC):
                ps = room(f"ab{c}")
                for h in range(RH):
                    r = slice(CH * (h % 2), CH * (h % 2) + CH)
                    ins = mul(ps[:, h % 2, (h // 2) * P:(h // 2 + 1) * P], BK[r, h // 2, c].rearrange("p a b -> p (a b)"),
                              AR[r, h // 2, c].rearrange("p a b -> p (a b)"))
                ins.then_inc(mm, 1)
                ps = room(f"nt{c}")
                for h in range(RH):
                    r = slice(CH * (h % 2), CH * (h % 2) + CH)
                    ins = mul(ps[0:CH, h % 2, (h // 2) * CH:(h // 2 + 1) * CH], AR[r, h // 2, c, 0], BK[r, h // 2, c, 0])
                ins.then_inc(mm, 1)

                def pair(i, one, two=None):
                    pe.wait_ge(S("inv"), 10 * c + i)
                    ps = room(f"i{c}_{i}")
                    for bank, x in enumerate((one, two)):
                        for h in range(RH if x else 0):
                            ins = mul(ps[0:CH, bank, h * CH:(h + 1) * CH], x[0][0:CH, h, :], x[1][0:CH, h, :])
                    ins.then_inc(mm, 1)

                Nd, Qd, No, Qo = PQD[:, 0], PQD[:, 1], PQ[:, 0], PQ[:, 1]
                N2, Q2, X, XT_, M, MTt = PQ2[:, 0], PQ2[:, 1], XX[:, 0], XX[:, 1], MM[:, 0], MM[:, 1]
                pair(1, (Qd, Nd), (Nd, Qd))
                pair(2, (Q2, X), (N2, XT_))
                pair(3, (Q2, N2), (N2, Q2))
                pair(4, (Q2, X), (N2, XT_))
                pair(5, (Q2, N2), (N2, Q2))
                pair(6, (Q2, X), (N2, XT_))
                pair(7, (XT_, No), (No, XT_))
                pair(8, (M, MTt))
                pair(9, (N2, X))
                pair(10, (MTt, Q2))
                ps = room(f"vt{c}")
                for p in range(RP):
                    ins = mul(ps[CH:P, 0, p * P:(p + 1) * P], RW[:, 8 + p, c * CH:(c + 1) * CH], ident[:])
                ins.then_inc(mm, 1)
                ps = room(f"bt{c}")
                for p in range(RP):
                    ins = turn(ps[:, 0, p * P:(p + 1) * P], BK[:, p, c].rearrange("p a b -> p (a b)"))
                ins.then_inc(mm, 1)
                pe.wait_ge(S("vbk"), c + 1)
                if c:
                    pe.wait_ge(S("stnew"), c)
                else:
                    pe.wait_ge(S("rzero"), 1)
                ps = room(f"u{c}")
                for h in range(RH):
                    r = slice(CH * (h % 2), CH * (h % 2) + CH)
                    q = slice(h * CH, (h + 1) * CH)
                    mul(ps[0:CH, h % 2, q], AR[r, h // 2, c, 0], ST[r, h // 2, :], True, h % 2 == 0)
                    ins = mul(ps[0:CH, 1, q], AB[CH:P, h, 0:CH], UV[CH:P, h, :], h % 2 == 0, True)
                ins.then_inc(mm, 1)
                pe.wait_ge(S("u0"), c + 1)
                ps = room(f"uu{c}")
                for h in range(RH):
                    ins = mul(ps[0:CH, 0, h * CH:(h + 1) * CH], XX[0:CH, 0, h, :], U0S[0:CH, h, :])
                ins.then_inc(mm, 1)
                pe.wait_ge(S("uev"), c + 1)
                ps = room(f"y{c}")
                for h in range(RH):
                    r = slice(CH * (h % 2), CH * (h % 2) + CH)
                    q = slice((h // 2) * CH, (h // 2 + 1) * CH)
                    mul(ps[r, 0, q], ST[r, h // 2, :], AR[r, h // 2, c, 1], True, False)
                    mul(ps[r, 0, q], UV[:, h, :], AB[:, h, CH:2 * CH], False, True)
                    ins = mul(ps[r, 1, q], BKT[:, h // 2, (h % 2) * CH:(h % 2 + 1) * CH], UV[:, h, :])
                ins.then_inc(mm, 1)
            pe.wait_ge(S("stnew"), NC)
            ps = room("abs")
            for h in range(RH):
                r = slice(CH * (h % 2), CH * (h % 2) + CH)
                ins = mul(ps[0:2 * TS, h % 2, (h // 2) * 2 * TS:(h // 2 + 1) * 2 * TS], BKS[r, h // 2].rearrange("p a b -> p (a b)"),
                          ARS[r, h // 2].rearrange("p a b -> p (a b)"))
            ins.then_inc(mm, 1)
            ps = room("nts")
            for h in range(RH):
                r = slice(CH * (h % 2), CH * (h % 2) + CH)
                ins = mul(ps[0:TS, h % 2, (h // 2) * TS:(h // 2 + 1) * TS], ARS[r, h // 2, 0], BKS[r, h // 2, 0])
            ins.then_inc(mm, 1)
            pe.wait_ge(S("sinv"), 1)
            ps = room("is1")
            for h in range(RH):
                ins = mul(ps[0:TS, 0, h * TS:(h + 1) * TS], ABS[0:TS, h, 0:TS], QSS[0:TS, h, :])
            ins.then_inc(mm, 1)
            pe.wait_ge(S("sinv"), 2)
            ps = room("is2")
            for h in range(RH):
                ins = mul(ps[0:TS, 0, h * TS:(h + 1) * TS], MS[0:TS, h, :], XS[0:TS, h, :])
            ins.then_inc(mm, 1)
            ps = room("vts")
            for p in range(RP):
                ins = mul(ps[TS:2 * TS, 0, p * P:(p + 1) * P], RW[:, 8 + p, TP:T], ident[:])
            ins.then_inc(mm, 1)
            ps = room("bts")
            for p in range(RP):
                ins = turn(ps[0:2 * TS, 0, p * P:(p + 1) * P], BKS[:, p].rearrange("p a b -> p (a b)"))
            ins.then_inc(mm, 1)
            pe.wait_ge(S("svbk"), 1)
            pe.wait_ge(S("lds0"), 16)
            ps = room("us")
            for h in range(RH):
                r = slice(CH * (h % 2), CH * (h % 2) + CH)
                q = slice((h // 2) * RD, (h // 2 + 1) * RD)
                for b in range(NB):
                    mul(ps[0:TS, h % 2, q], AM[r, 0, h // 2, b], S0[r, h // 2, b], b == 0, False)
                ins = mul(ps[0:TS, h % 2, q], ABS[TS:2 * TS, h, 0:TS], UVS[TS:2 * TS, h, :], False, True)
            ins.then_inc(mm, 1)
            pe.wait_ge(S("su"), 1)
            ps = room("uus")
            for h in range(RH):
                ins = mul(ps[0:TS, 0, h * RD:(h + 1) * RD], XS[0:TS, h, :], UVE[0:TS, 0, h, :])
            ins.then_inc(mm, 1)
            pe.wait_ge(S("su"), 2)
            ps = room("ys")
            for h in range(RH):
                r = slice(CH * (h % 2), CH * (h % 2) + CH)
                q = slice((h // 2) * TS, (h // 2 + 1) * TS)
                for b in range(NB):
                    mul(ps[r, 0, q], S0[r, h // 2, b], AM[r, 1, h // 2, b], b == 0, b == NB - 1)
                ins = mul(ps[r, 1, q], UVS[0:2 * TS, h, :], ABS[0:2 * TS, h, TS:2 * TS])
            ins.then_inc(mm, 1)
            for p in range(RP):
                pe.wait_ge(S("uve"), p + 1)
                ps = room(f"ss{p}")
                for x in range(2):
                    ins = mul(ps[CH * x:CH * x + CH, 0, :], BKTS[0:2 * TS, p, CH * x:CH * x + CH],
                              UVE[0:2 * TS, x].rearrange("p a b -> p (a b)"))
                ins.then_inc(mm, 1)
            pe.wait_ge(S("ldg2"), 16)
            for p in range(RP):
                if p == 0:
                    pe.wait_ge(S("ysum"), 1)
                ps = room(f"ym{p}")
                both(ps, lambda k: blk[:], lambda k: RW[:, 4 + p, :], 1).then_inc(mm, 1)
                pe.wait_ge(S("yq"), p + 1)
                ps = room(f"yv{p}")
                both(ps, lambda k: blk[:], lambda k: YQ, 1).then_inc(mm, 1)
                ps = room(f"g{p}")
                both(ps, lambda k: G2[:, p * P:(p + 1) * P], lambda k: RW[:, 13, :], 1).then_inc(mm, 1)
            barrier(pe, 2)

            norm(1, lambda k: MN[:, k, :], NMEM)
            pe.wait_ge(S("hn"), 2)
            for h in range(MH):
                w = weights(f"mk{h}")
                ps = room(f"mk{h}")
                for k in range(DT):
                    ins = mul(ps[:, 0, 0:NMEM], w[:, k, :], MN[:, k, :], k == 0, k == DT - 1)
                ins.then_inc(mm, 1)
            for s in range(2):
                ps = room(f"mv{s}")
                for c in range(4):
                    w = weights(f"mv{c}")
                    for k in range(DT):
                        ins = mul(ps[:, 0, c * P:(c + 1) * P], MN[:, k, s * P:(s + 1) * P], w[:, k, :],
                                  k == 0, k == DT - 1)
                ins.then_inc(mm, 1)
            for h in range(MH):
                project(f"xq{h}", ht)
            pe.wait_ge(S("xq"), MH)
            for h in range(MH):
                ps = room(f"as{h}")
                for t in range(4):
                    ins = mul(ps[:, t // 2, (t % 2) * NMEM:(t % 2 + 1) * NMEM], XQ[:, h, t * P:(t + 1) * P], MKT[:, h, :])
                ins.then_inc(mm, 1)
                pe.wait_ge(S("soft"), h + 1)
                ps = room(f"at{h}")
                for s in range(2):
                    for t in range(4):
                        ins = turn(ps[:, s, t * P:(t + 1) * P], PA[:, t, s * P:(s + 1) * P])
                ins.then_inc(mm, 1)
                pe.wait_ge(S("pat"), h + 1)
                ps = room(f"ao{h}")
                for s in range(2):
                    ins = mul(ps[:, 0, :], MV[:, s, h * P:(h + 1) * P], PAT[:, s, :], s == 0, s == 1)
                ins.then_inc(mm, 1)
            pe.wait_ge(S("xm"), 1)
            for h in range(MH):
                pe.wait_ge(S(f"ldk{h % 2}"), 16 * (h // 2 + 1))
                ps = room(f"ds{h}")
                for b in range(NB):
                    ins = mul(ps[h * TS:(h + 1) * TS, 0, 0:NMEM], XM[:, h, b, :], KB[:, h % 2, b * NMEM:(b + 1) * NMEM],
                              b == 0, b == NB - 1)
                ins.then_inc(mm, 1)
            pe.wait_ge(S("soft"), MH + 1)
            ps = room("dt")
            for s in range(2):
                ins = turn(ps[:, 0, s * P:(s + 1) * P], PA[:, 0, s * P:(s + 1) * P])
            ins.then_inc(mm, 1)
            pe.wait_ge(S("pm"), 1)
            for h in range(MH):
                pe.wait_ge(S(f"ldvv{h % 2}"), 16 * (h // 2 + 1))
                ps = room(f"do{h}")
                for b in range(NB):
                    for s in range(2):
                        ins = mul(ps[:, 0, 0:TS], VBM[:, h % 2, (b * 2 + s) * P:(b * 2 + s + 1) * P], PM[:, s, h, b, :],
                                  b + s == 0, b + s == NB)
                ins.then_inc(mm, 1)
            barrier(pe, 3)

            for n in range(DT):
                for j in range(3):
                    project(f"gg{n}_{j}", ht)
                    project(f"gb{n}_{j}", lambda k: BR[:, 4 * j + k, :], 4)
            pe.wait_ge(S("merged"), DT)
            for n in range(DT):
                project(f"x{n}", lambda k: YM[:, k, :])
            barrier(pe, 4)

            norm(2, ht, T)
            pe.wait_ge(S("hn"), 3)
            for i in range(2 * PH):
                project(f"pq{i}", ht)
            pe.wait_ge(S("pqe"), 2 * PH)
            pe.wait_ge(S("ldkeys"), 16)
            for t in range(NTT):
                c0, m = tcols(t)
                for x in range(2):
                    ps = room(f"ps{t}_{x}")
                    for i in range(8):
                        q = 8 * x + i
                        ins = mul(ps[0:m, i // 4, (i % 4) * P:(i % 4 + 1) * P], QT[:, q, c0:c0 + m], KSEL[:, q % 2, :])
                    ins.then_inc(mm, 1)
                pe.wait_ge(S("picks"), t + 1)
                ps = room(f"pt{t}")
                for i, x in enumerate((AFX, BFX, GAT.rearrange("p a b -> p (a b)"))):
                    ins = turn(ps[:, 0, i * P:i * P + m], x[0:m, :])
                ins.then_inc(mm, 1)
            barrier(pe, 5)


            def gate_units(i, first):
                for u in range(8):
                    pe.wait_ge(S("oh"), 8 * i + u + 1)
                    if not first and u % 2 == 0:
                        pe.wait_ge(S("ge"), 4 * i + u // 2 - 3)
                    for x in range(4):
                        ins = mul(PS[:, u // 2, u % 2, x * P:(x + 1) * P], OH[:, (u % 2) * 4 + x, 0],
                                  OH[:, (u % 2) * 4 + x, 1])
                    ins.then_inc(S("ohf"), 1)

            gate_units(0, True)
            with pe.Fori(1, NEB) as i:
                gate_units(i, False)
            barrier(pe, 6)

            def first_products(g, b, n, freed=None):
                pe.wait_ge(S(f"ul{b}"), n)
                for e in range(EG):
                    if freed is not None:
                        pe.wait_ge(S("of"), freed + e)
                    elif b:
                        pe.wait_ge(S("af"), e + 1)
                    for x in range(2):
                        for k in range(DT):
                            ins = mul(PS[:, e, x, 0:T // 2], UB[:, b, e, k, :], HT[:, k, x * (T // 2):(x + 1) * (T // 2)],
                                      k == 0, k == DT - 1)
                    ins.then_inc(S("pa"), 1)

            def second_products(g, b, n, last=False):
                pe.wait_ge(S(f"vl{b}"), n)
                pe.wait_ge(S("wr"), 4 * g + 4)
                for d in range(DT):
                    if d >= EG or last:
                        pe.wait_ge(S("of"), 8 * g + d - 3)
                    else:
                        pe.wait_ge(S("af"), 4 * g + d + 5)
                    for x in range(2):
                        for e in range(EG):
                            ins = mul(PS[:, d % EG, x, 0:T // 2], VU[:, b, e, d * P:(d + 1) * P],
                                      AC[:, b, e, x * (T // 2):(x + 1) * (T // 2)], e == 0, e == EG - 1)
                    ins.then_inc(S("po"), 1)

            first_products(0, 0, 16)
            first_products(1, 1, 16)
            second_products(0, 0, 16)
            with pe.Fori(1, NG // 2) as j:
                first_products(2 * j, 0, 16 * j + 16, 16 * j - 11)
                second_products(2 * j - 1, 1, 16 * j)
                first_products(2 * j + 1, 1, 16 * j + 16, 16 * j - 3)
                second_products(2 * j, 0, 16 * j + 16)
            second_products(NG - 1, 1, 8 * NG, True)
            norm(3, ht, T)

        @block.vector
        def _(dve):
            step = Steps(dve, S("dv"))

            def tt(out, x, y, op=ALU.mult, sem=None):
                step(dve.tensor_tensor(out, x, y, op), sem)

            def ts(out, x, s1_, op0, s2_=None, op1=None, sem=None):
                if op1 is None:
                    step(dve.tensor_scalar(out, x, s1_, None, op0), sem)
                else:
                    step(dve.tensor_scalar(out, x, s1_, s2_, op0, op1), sem)

            def stt(out, x, s, y, op0=ALU.mult, op1=ALU.mult, sem=None):
                step(dve.scalar_tensor_tensor(out=out, in0=x, scalar=s, in1=y, op0=op0, op1=op1), sem)

            def tally(out, x, op=ALU.add):
                step(dve.tensor_reduce(out, x, AX_X, op))

            def copy(out, x, sem=None):
                step(dve.tensor_copy(out, x), sem)

            def parts(key, fn):
                ps = take(dve, key)
                step(fn(ps[:, 0, :], slice(0, TP)))
                give(dve, fn(ps[:, 1, 0:TS], slice(TP, T)), key)

            def norm(i, src, dst, g, n):
                if n == T:
                    parts(f"ms{i}", lambda x, c: dve.tensor_scalar(rstd[:, c], x, 1.0 / D, EPS, ALU.mult, ALU.add))
                else:
                    ps = take(dve, f"ms{i}")
                    give(dve, dve.tensor_scalar(rstd[:, 0:n], ps[:, 0, 0:n], 1.0 / D, EPS, ALU.mult, ALU.add), f"ms{i}")
                step(dve.reciprocal(rstd[:, 0:n], rstd[:, 0:n]), S("rc"))
                dve.wait_ge(S("rs"), i + 1)
                for k in range(DT):
                    stt(dst[:, k, :], src[:, k, :], v(g, k), rstd[:, 0:n], sem=S("hn") if k == DT - 1 else None)

            dve.wait_ge(S("ldv"), 16)
            dve.wait_ge(S("ldx"), 16)
            norm(0, XT, HT, "norm_mix", T)
            for n in range(8):
                dve.wait_ge(S("ctail"), n + 1)
                if n >= 2:
                    dve.wait_ge(S("silu"), n - 1)
                q = QKP[:, n, 3 + TP:].rearrange("p (b t) -> p b t", b=NB)
                cp = CV[:, n % 2, 0:TP]
                cs = CV[:, n % 2, TP:T].rearrange("p (b t) -> p b t", b=NB)
                ts(cp, QKP[:, n, 0:TP], v("conv_w", n), ALU.mult, v("conv_b", n), ALU.add)
                ts(cs, q[:, :, 0:4], v("conv_w", n), ALU.mult, v("conv_b", n), ALU.add)
                for j in range(1, 4):
                    stt(cp, QKP[:, n, j:j + TP], v("conv_w", 8 * j + n), cp, ALU.mult, ALU.add)
                    stt(cs, q[:, :, j:j + 4], v("conv_w", 8 * j + n), cs, ALU.mult, ALU.add,
                        sem=S("cv") if j == 3 else None)
            dve.wait_ge(S("ldg"), 16)
            dve.wait_ge(S("ldm"), 16)
            for key, r, i in (("gi", IR, 0), ("gf", FR, 1)):
                ps = take(dve, key)
                ts(r[:, 0:TP], ps[0:MH, 0, :], GB[0:MH, i:i + 1], ALU.add)
                give(dve, dve.tensor_scalar(r[:, TP:T], ps[0:MH, 1, 0:TS], GB[0:MH, i:i + 1], None, ALU.add), key)
            step(dve.memset(ONR, 1.0), S("gi"))
            dve.wait_ge(S("ls"), 1)
            stt(FR, FR, 0.0, LR, ALU.min, ALU.subtract)
            step(dve.tensor_tensor_scan(FC[:, 0:TP], ONR[:, 0:TP], FR[:, 0:TP], 0.0, ALU.mult, ALU.add))
            fs, gs, ms_, lf = [x[:, TP:T].rearrange("p (b t) -> p b t", b=NB) for x in (FC, GR, MR, FR)]
            copy(fs[:, :, 0], lf[:, :, 0])
            for j in range(1, NS):
                tt(fs[:, :, j], fs[:, :, j - 1], lf[:, :, j], ALU.add)
            tt(GR, IR, FC, ALU.subtract)
            step(dve.tensor_tensor_scan(MR[:, 0:TP], GR[:, 0:TP], GR[:, 0:TP], 0.0, ALU.max, ALU.max))
            tt(ms_[:, :, 0], M0[0:MH], gs[:, :, 0], ALU.max)
            for j in range(1, NS):
                tt(ms_[:, :, j], ms_[:, :, j - 1], gs[:, :, j], ALU.max)
            tt(MT, FC, MR, ALU.add)
            ts(WG[:, 0:TP], GR[:, 0:TP], MR[:, TP - 1:TP], ALU.subtract)
            ws = WG[:, TP:T].rearrange("p (b t) -> p b t", b=NB)
            tt(ws, gs, bc(ms_[:, :, NS - 1], 2, NS), ALU.subtract)
            copy(MO[0:MH, 0:1], MT[:, TP - 1:TP])
            copy(MO[0:MH, 1:1 + NB], MT[:, TP:T].rearrange("p (b t) -> p b t", b=NB)[:, :, NS - 1], S("gates"))
            tt(EI[0:MH].rearrange("p (b t) -> p b t", b=NB), bc(M0[0:MH], 2, NS), ms_, ALU.subtract, S("gi"))
            ps = take(dve, "gt")
            copy(GTM[:, 0:4], ps[:, 0, 0:4 * 3 * MH].rearrange("p (a b c) -> p a b c", a=4, b=3))
            give(dve, dve.tensor_copy(GTM[0:TS, 4], ps[0:TS, 0, 4 * 3 * MH:5 * 3 * MH].rearrange("p (b c) -> p b c", b=3)),
                 "gt")
            for h in range(MH):
                dve.wait_ge(S("mbr"), h + 1)
                for i in range(4):
                    ts(DD[:, i, i * P:TP], MB[:, i * P:TP], GTM[:, i, 0, h:h + 1], ALU.subtract, 0.0, ALU.max, S("dd"))
                ts(DS[0:TS], MB[0:TS, TP:T], GTM[0:TS, 4, 0, h:h + 1], ALU.subtract, 0.0, ALU.max, S("dd"))
                for i in range(4):
                    dve.wait_ge(S("ddx"), 5 * h + i + 1)
                    ps = take(dve, f"s{h}_{i}")
                    if i == 3:
                        dve.wait_ge(S("ddx"), 5 * h + 5)
                        stt(DS[0:TS], ps[0:TS, 1, 0:TS], SCALE, DS[0:TS])
                        tt(DS[0:TS], DS[0:TS], smask[:])
                    give(dve, dve.scalar_tensor_tensor(out=DD[:, i, i * P:TP], in0=ps[:, 0, 0:TP - i * P], scalar=SCALE,
                                                       in1=DD[:, i, i * P:TP], op0=ALU.mult, op1=ALU.mult), f"s{h}_{i}")
                    tt(DD[:, i, i * P:(i + 1) * P], DD[:, i, i * P:(i + 1) * P], tri[:])
                stt(QS, QK[:, h, TP:T], SCALE, MB[:, T:T + TS])
                tt(QM, bc(QS, 1, NB), bmask[:], sem=S("probs"))
                ps = take(dve, f"n{h}")
                give(dve, dve.tensor_copy(NU[:, 0:4, :], ps.rearrange("p a (b n) -> p (a b) n", b=2)[:, :, 0:129]), f"n{h}")
                ps = take(dve, f"m{h}")
                give(dve, dve.tensor_copy(NU[0:TS, 4, :], ps[0:TS, 0, 0:129]), f"m{h}")
                ps = take(dve, f"kt{h}")
                tt(KW[:, 0:4, :], ps[:, 0, :].rearrange("p (a b) -> p a b", a=4), bc(GTM[:, 0:4, 2, h], 2, P))
                give(dve, dve.tensor_scalar(KW[0:TS, 4, :], ps[0:TS, 1, 0:P], GTM[0:TS, 4, 2, h:h + 1], None, ALU.mult),
                     f"kt{h}")
                tt(VB[0:TS], bc(VX[0:TS, NTT - 1, h, :], 1, NB), bc(bexp[0:TS, :], 2, 129), sem=S("kw"))
                den, em = NU[:, :, P], GTM[:, :, 1, h]
                stt(s1, den, -1.0, den, ALU.mult, ALU.max)
                tt(s1, s1, em, ALU.max)
                step(dve.reciprocal(s1, s1))
                tt(HH, NU[:, :, 0:P], bc(s1, 2, P))
                tally(s2, HH)
                ts(s2, s2, 1.0 / P, ALU.mult)
                tt(HH, HH, bc(s2, 2, P), ALU.subtract)
                tt(SQ, HH, HH)
                tally(s3, SQ)
                ts(s3, s3, 1.0 / P, ALU.mult, EPS, ALU.add)
                step(dve.reciprocal(s3, s3), S("hv"))
                ps = take(dve, f"c{h}")
                tt(CN[:, h], CN[:, h], bc(MB[:, T:T + TS].rearrange("p (b t) -> p b t", b=NB)[:, :, NS - 1], 2, 129))
                copy(CO[:, h, :], ps[:, 0, 0:129])
                cn = CN[:, h].rearrange("p a b -> p (a b)")
                give(dve, dve.tensor_tensor(cn[:, 774:1032], cn[:, 774:1032], ps[:, 1, 0:258], ALU.add), f"c{h}")
                ps = take(dve, f"cs{h}")
                tt(cn[:, 0:387], cn[:, 0:387], ps[:, 0, 0:387], ALU.add)
                give(dve, dve.tensor_tensor(cn[:, 387:774], cn[:, 387:774], ps[:, 1, 0:387], ALU.add), f"cs{h}")
                dve.sem_inc(S("cnew"), 1)
                dve.wait_ge(S("hs"), h + 1)
                tt(HH, HH, bc(s3, 2, P), sem=S("hnorm"))
                parts(f"t{h}", lambda x, c: dve.scalar_tensor_tensor(out=BR[:, h, c], in0=x, scalar=v("ml_norm", h),
                                                                     in1=SO[:, h, c], op0=ALU.mult, op1=ALU.mult))
            barrier(dve, 1)

            for n in range(NRW):
                dve.wait_ge(S("rwin"), 2 * n + 2)
                r = RPD[:, n % 2, :]
                q = r[:, 1 + TP:].rearrange("p (b t) -> p b t", b=NB)
                o1, o2 = RW[:, n, 0:TP], RW[:, n, TP:T].rearrange("p (b t) -> p b t", b=NB)
                tt(o1, r[:, 0:TP], r[:, 1:1 + TP], ALU.subtract)
                tt(o2, q[:, :, 0:4], q[:, :, 1:5], ALU.subtract)
                stt(o1, o1, v("mu", n), r[:, 1:1 + TP], ALU.mult, ALU.add)
                stt(o2, o2, v("mu", n), q[:, :, 1:5], ALU.mult, ALU.add, sem=S("rsh"))
            ts(OMK, vec[:, VEC["ka"]:VEC["ka"] + RP], -1.0, ALU.mult, 1.0, ALU.add)
            for p in range(RP):
                dve.wait_ge(S("wa"), p + 1)
                r_, k_, v_ = RW[:, p, :], RW[:, 4 + p, :], RW[:, 8 + p, :]
                ts(SQB, k_, v("kk", p), ALU.mult)
                tt(SQB, SQB, SQB, sem=S("kk2"))
                ts(KPB, AG, v("ka", p), ALU.mult, OMK[:, p:p + 1], ALU.add)
                tt(KPB, KPB, k_)
                ts(LW, LW, DECAY, ALU.mult)
                step(dve.tensor_tensor_scan(CC, reset[:], LW, 0.0, ALU.mult, ALU.add))
                tt(EP, CC, LW, ALU.subtract)
                parts(f"kn{p}", lambda x, c: dve.tensor_scalar(KN[:, c], x, 1e-24, None, ALU.max))
                step(dve.reciprocal(KN, KN), S("kv"))
                dve.sem_inc(S("cum"), 1)
                stt(SQB, r_, v("rk", p), KPB, sem=S("kk2"))
                dve.wait_ge(S("ks"), p + 1)
                stt(KN, k_, v("kk", p), KN)
                tt(AG, AG, KN)
                dve.wait_ge(S("dec"), p + 1)
                chunks = lambda x: x[:, 0:TP].rearrange("p (c t) -> p c t", c=NC)
                for x, y, dst, dsts, i in ((AG, EN, BK, BKS, 0), (KPB, EN, BK, BKS, 1), (r_, EW, AR, ARS, 1)):
                    tt(dst[:, p, :, i, :], chunks(x), chunks(y))
                    tt(dsts[:, p, i, :], x[:, TP:T], y[:, TP:T])
                stt(AR[:, p, :, 0, :], chunks(KN), -1.0, chunks(EP))
                stt(ARS[:, p, 0, :], KN[:, TP:T], -1.0, EP[:, TP:T])
                copy(WE[:, p, :], chunks(EW)[:, :, CH - 1])
                copy(WES[:, p, :], EW[:, TP:T].rearrange("p (b t) -> p b t", b=NB)[:, :, NS - 1])
                parts(f"bn{p}", lambda x, c: dve.tensor_tensor(RW[:, p, c], x, RW[:, 8 + p, c], ALU.mult))
                dve.sem_inc(S("rwops"), 1)
            hb = slice(0, CH)
            split = lambda x: x.rearrange("p (b a) n -> p a b n", a=2)
            banks = lambda ps, m, n: ps[0:m, :, 0:RP * n].rearrange("p a (b n) -> p a b n", b=RP)
            bank = lambda ps, i, n=CH: ps[0:n, i, 0:RH * n].rearrange("p (h n) -> p h n", h=RH)
            for c in range(NC):
                ps = take(dve, f"ab{c}")
                give(dve, dve.tensor_tensor(split(AB), ps.rearrange("p a (b n) -> p a b n", b=RP),
                                            bc(bc(rmask[:].rearrange("p a b -> p (a b)"), 1, RP), 1, 2), ALU.mult), f"ab{c}")
                ps = take(dve, f"nt{c}")
                give(dve, dve.tensor_tensor(split(PQ[hb, 1]), banks(ps, CH, CH), bc(bc(low[:], 1, RP), 1, 2), ALU.mult),
                     f"nt{c}")
                tt(PQD[hb, 0], AB[hb, :, 0:CH], bc(b16[:], 1, RH))
                tt(PQD[hb, 1], PQ[hb, 1], bc(b16[:], 1, RH))
                tt(PQ[hb, 0], AB[hb, :, 0:CH], PQD[hb, 0], ALU.subtract)
                tt(PQ[hb, 1], PQ[hb, 1], PQD[hb, 1], ALU.subtract)
                tt(XX[hb, 0], PQD[hb, 0], bc(ident[hb, hb], 1, RH), ALU.add)
                tt(XX[hb, 1], PQD[hb, 1], bc(ident[hb, hb], 1, RH), ALU.add, S("inv"))
                for i in range(1, 11):
                    key = f"i{c}_{i}"
                    ps = take(dve, key)
                    two = ps[hb].rearrange("p a (h n) -> p a h n", h=RH)
                    if i in (1, 3, 5):
                        ins = dve.tensor_copy(PQ2[hb], two)
                    elif i in (2, 4, 6):
                        fl = lambda x: x[hb].rearrange("p a h n -> p (a h n)")
                        ins = dve.tensor_tensor(fl(XX), fl(XX), ps[hb].rearrange("p a n -> p (a n)"), ALU.add)
                    elif i == 7:
                        ins = dve.tensor_copy(MM[hb], two)
                    elif i == 8:
                        ins = dve.tensor_copy(PQ2[hb, 0], bank(ps, 0))
                    elif i == 9:
                        ins = dve.tensor_tensor(PQ2[hb, 1], XX[hb, 0], bank(ps, 0), ALU.add)
                    else:
                        ins = dve.tensor_tensor(XX[hb, 0], PQ2[hb, 1], bank(ps, 0), ALU.add)
                    give(dve, ins, key)
                    if i < 10:
                        dve.sem_inc(S("inv"), 1)
                ps = take(dve, f"vt{c}")
                give(dve, dve.tensor_copy(UV[CH:P], ps[CH:P, 0, :].rearrange("p (h n) -> p h n", h=RH)), f"vt{c}")
                ps = take(dve, f"bt{c}")
                give(dve, dve.tensor_copy(BKT, ps[:, 0, :].rearrange("p (h n) -> p h n", h=RP)), f"bt{c}")
                dve.sem_inc(S("vbk"), 1)
                ps = take(dve, f"u{c}")
                copy(U0S[hb], bank(ps, 1))
                even = split(U0S[hb])[:, 0]
                give(dve, dve.tensor_tensor(even, even, split(bank(ps, 0))[:, 0], ALU.add), f"u{c}")
                dve.sem_inc(S("u0"), 1)
                ps = take(dve, f"uu{c}")
                give(dve, dve.tensor_copy(UV[hb], bank(ps, 0)), f"uu{c}")
                dve.sem_inc(S("uev"), 1)
                ps = take(dve, f"y{c}")
                dve.wait_ge(S("yev"), c + 1)
                give(dve, dve.tensor_tensor(ST, ps[:, 1, 0:RP * RD].rearrange("p (a b) -> p a b", a=RP), ST, ALU.add),
                     f"y{c}")
                tt(ST, ST, bc(WE[:, :, c], 2, RD), sem=S("stnew"))
            sl = slice(0, TS)
            ps = take(dve, "abs")
            give(dve, dve.tensor_tensor(split(ABS[0:2 * TS]), banks(ps, 2 * TS, 2 * TS),
                                        bc(bc(srm[:].rearrange("p a b -> p (a b)"), 1, RP), 1, 2), ALU.mult), "abs")
            ps = take(dve, "nts")
            give(dve, dve.tensor_tensor(split(QSS[sl]), banks(ps, TS, TS), bc(bc(slow[:], 1, RP), 1, 2), ALU.mult), "nts")
            tt(XS[sl], ABS[sl, :, 0:TS], bc(ident[sl, sl], 1, RH), ALU.add, S("sinv"))
            ps = take(dve, "is1")
            give(dve, dve.tensor_copy(MS[sl], bank(ps, 0, TS)), "is1")
            dve.sem_inc(S("sinv"), 1)
            ps = take(dve, "is2")
            give(dve, dve.tensor_tensor(XS[sl], XS[sl], bank(ps, 0, TS), ALU.add), "is2")
            ps = take(dve, "vts")
            give(dve, dve.tensor_copy(UVS[TS:2 * TS], ps[TS:2 * TS, 0, :].rearrange("p (h n) -> p h n", h=RH)), "vts")
            ps = take(dve, "bts")
            give(dve, dve.tensor_copy(BKTS[0:2 * TS], ps[0:2 * TS, 0, :].rearrange("p (h n) -> p h n", h=RP)), "bts")
            for x in range(2):
                for p in range(RP):
                    tt(AM[:, x, p], bc(ARS[:, p, x, :], 1, NB), bmask[:])
            dve.sem_inc(S("svbk"), 1)
            ps = take(dve, "us")
            give(dve, dve.tensor_copy(split(UVE[sl, 0]), banks(ps, TS, RD)), "us")
            dve.sem_inc(S("su"), 1)
            ps = take(dve, "uus")
            give(dve, dve.tensor_copy(UVS[sl], ps[sl, 0, :].rearrange("p (h n) -> p h n", h=RH)), "uus")
            dve.sem_inc(S("su"), 1)
            ps = take(dve, "ys")
            dve.wait_ge(S("yev"), NC + 1)
            ysm = RW[:, 4:8, TP:T]
            give(dve, dve.tensor_tensor(ysm, ysm, ps[:, 1, 0:RP * TS].rearrange("p (a b) -> p a b", a=RP), ALU.add), "ys")
            dve.sem_inc(S("ysum"), 1)
            for p in range(RP):
                for x in range(2):
                    tt(UVE[0:2 * TS, x], bc(UVS[0:2 * TS, 2 * p + x, :], 1, NB), bc(bexp[:], 2, RD),
                       sem=S("uve") if x else None)
                ps = take(dve, f"ss{p}")
                give(dve, dve.tensor_tensor(S0[:, p], ps[:, 0, :].rearrange("p (a b) -> p a b", a=NB), S0[:, p], ALU.add),
                     f"ss{p}")
                tt(S0[:, p], S0[:, p], bc(WES[:, p, :], 2, RD), sem=S("s0new"))
            for p in range(RP):
                parts(f"ym{p}", lambda x, c: dve.scalar_tensor_tensor(out=YC[:, c], in0=x, scalar=-1.0 / RD,
                                                                      in1=RW[:, 4 + p, c], op0=ALU.mult, op1=ALU.add))
                tt(YQ, YC, YC, sem=S("yq"))
                parts(f"yv{p}", lambda x, c: dve.tensor_scalar(rstd[:, c], x, 1.0 / RD, GN_EPS, ALU.mult, ALU.add))
                step(dve.reciprocal(rstd[:], rstd[:]), S("yv"))
                dve.wait_ge(S("ysq"), p + 1)
                tt(YC, YC, rstd[:])
                ts(YC, YC, v("ln_w", p), ALU.mult, v("ln_b", p), ALU.add)
                tt(YC, YC, RW[:, p, :], ALU.add)
                parts(f"g{p}", lambda x, c: dve.tensor_tensor(BR[:, 4 + p, c], x, YC[:, c], ALU.mult))
            barrier(dve, 2)

            dve.wait_ge(S("ldmem"), 16)
            norm(1, MEM, MN, "mem_norm", NMEM)

            def softmax(i, q, src):
                tally(c1[:, 0:q], src, ALU.max)
                ins = dve.tensor_tensor(PA[:, 0:q], src, bc(c1[:, 0:q], 2, NMEM), ALU.subtract)
                if i < MH:
                    give(dve, ins, f"as{i}")
                else:
                    step(ins)
                dve.sem_inc(S("sx"), 1)
                dve.wait_ge(S("sxe"), i + 1)
                tally(c2[:, 0:q], PA[:, 0:q])
                step(dve.reciprocal(c2[:, 0:q], c2[:, 0:q]))
                tt(PA[:, 0:q], PA[:, 0:q], bc(c2[:, 0:q], 2, NMEM), sem=S("soft"))

            dve.wait_ge(S("xq"), MH)
            for h in range(MH):
                tt(XM[:, h], bc(XQ[:, h, TP:T], 1, NB), bmask[:], sem=S("xm") if h == MH - 1 else None)
            for h in range(MH):
                ps = take(dve, f"as{h}")
                softmax(h, 4, ps.rearrange("p a (b n) -> p (a b) n", b=2))
            for h in range(MH):
                ps = take(dve, f"ds{h}")
                q = slice(h * TS, (h + 1) * TS)
                give(dve, dve.tensor_copy(PA[q, 0, :], ps[q, 0, 0:NMEM]), f"ds{h}")
            softmax(MH, 1, PA[:, 0:1, :])
            ps = take(dve, "dt")
            give(dve, dve.tensor_copy(PT3, ps[:, 0, 0:2 * P].rearrange("p (a b) -> p a b", a=2)), "dt")
            for s in range(2):
                for h in range(MH):
                    tt(PM[:, s, h], bc(PT3[:, s, h * TS:(h + 1) * TS], 1, NB), bmask[:],
                       sem=S("pm") if s * h == MH - 1 else None)
            barrier(dve, 3)

            for n in range(DT):
                for j in range(3):
                    i = 3 * n + j
                    dve.wait_ge(S("sgb"), i + 1)
                    dst = TMP[:, i % 2, :] if j else YM[:, n, :]
                    parts(f"gb{n}_{j}", lambda x, c: dve.tensor_tensor(dst[:, c], x, SGB[:, i % 3, c], ALU.mult))
                    dve.sem_inc(S("gated"), 1)
                    if j:
                        tt(YM[:, n, :], YM[:, n, :], dst, ALU.add, S("merged") if j == 2 else None)
            for n in range(DT):
                parts(f"x{n}", lambda x, c: dve.tensor_tensor(XT[:, n, c], x, XT[:, n, c], ALU.add))
            barrier(dve, 4)

            norm(2, XT, HT, "norm_ffn", T)

            def top16(values, scratch, vals, idx):
                step(dve.max(vals[:, 0:8], values))
                step(dve.match_replace(scratch, vals[:, 0:8], values, LOW))
                step(dve.max(vals[:, 8:16], scratch))
                step(dve.max_index(idx[:, 0:8], vals[:, 0:8], values))
                step(dve.max_index(idx[:, 8:16], vals[:, 8:16], scratch))

            for t in range(NTT):
                c0, m = tcols(t)
                dve.wait_ge(S("sce"), 2 * t + 2)
                for i in range(2 * PH):
                    top16(SC[0:m, i, :], SC2[0:m], V16[0:m, i, :], IX[0:m, i, :])
                dve.sem_inc(S("scf"), 1)
                copy(IF[0:m], IX[0:m])
                vs = V16[0:m].rearrange("p (h s) k -> p h s k", s=2)
                tt(CAND[0:m], bc(vs[:, :, 0, :], 3, PK), bc(vs[:, :, 1, :], 2, PK), ALU.add)
                for h in range(PH):
                    top16(CAND[0:m, h].rearrange("p a b -> p (a b)"), CAND2[0:m], TOP[0:m, h, :], PX[0:m, h, :])
                tt(GAT[0:m], TOP[0:m], bc(TOP[0:m, :, 0], 2, PK), ALU.subtract, S("gx"))
                flat = PX[0:m].rearrange("p a b -> p (a b)")
                ts(PAX[0:m], flat, 4, ALU.logical_shift_right)
                ts(PBX[0:m], flat, 15, ALU.bitwise_and)
                copy(AFX[0:m], PAX[0:m])
                copy(BFX[0:m], PBX[0:m])
                ifv = IF[0:m].rearrange("p (h s) k -> p h s k", s=2)
                for i, x in enumerate((AFX, BFX)):
                    tt(EQ[0:m], bc(x[0:m], 2, PK), bc(iota[0:m, 0:PK], 1, P), ALU.is_equal)
                    e4 = EQ[0:m].rearrange("p (h k) a -> p h k a", h=PH)
                    tt(e4, e4, bc(ifv[:, :, i, :], 2, PK))
                    tally(x[0:m], EQ[0:m])
                dve.wait_ge(S("gxe"), t + 1)
                tally(e1[0:m], GAT[0:m])
                step(dve.reciprocal(e1[0:m], e1[0:m]))
                tt(GAT[0:m], GAT[0:m], bc(e1[0:m], 2, PK), sem=S("picks"))
                ps = take(dve, f"pt{t}")
                give(dve, dve.tensor_copy(IT[:, :, c0:c0 + m], ps[:, 0, 0:3 * P].rearrange("p (a b) -> p a b", a=3)[:, :, 0:m]),
                     f"pt{t}")
            barrier(dve, 5)

            def one_hots(i, first):
                for u in range(8):
                    if not (first and u < 2):
                        dve.wait_ge(S("ohf"), 8 * i + u - 1)
                    for x in range(4):
                        j = (u % 2) * 4 + x
                        col = [IT[:, q, bass.ds(EB * i + 4 * u + x, 1)] for q in range(3)]
                        dve.tensor_scalar(OH[:, j, 0], iota[:], col[0], None, ALU.is_equal)
                        ins = dve.tensor_scalar(OH[:, j, 1], iota[:], col[1], col[2], ALU.is_equal, ALU.mult)
                    ins.then_inc(S("oh"), 1)

            one_hots(0, True)
            with dve.Fori(1, NEB) as i:
                one_hots(i, False)
            dve.wait_ge(S("oh"), 8 * NEB)
            barrier(dve, 6)

            def weight(g, b, n):
                dve.wait_ge(S(f"gl{b}"), n)
                for e in range(EG):
                    dve.wait_ge(S("af"), 4 * g + e + 1)
                    x = AC[:, b, e, :].rearrange("p (a t) -> p a t", t=EB)
                    dve.tensor_tensor(x, x, GQ[:, b, :, e, :], ALU.mult).then_inc(S("wr"), 1)

            def add(g, first=False):
                for d in range(DT):
                    dve.wait_ge(S("po"), 8 * g + d + 1)
                    if not first:
                        dve.wait_ge(S("of"), 8 * g - 7 + d)
                    x = XT[:, d, :].rearrange("p (a n) -> p a n", a=2)
                    dve.tensor_tensor(x, PS[:, d % EG, :, 0:T // 2], x, ALU.add).then_inc(S("of"), 1)

            weight(0, 0, 16)
            weight(1, 1, 16)
            add(0, True)
            with dve.Fori(1, NG // 2) as j:
                weight(2 * j, 0, 16 * j + 16)
                add(2 * j - 1)
                weight(2 * j + 1, 1, 16 * j + 16)
                add(2 * j)
            add(NG - 1)
            dve.wait_ge(S("of"), 8 * NG)
            norm(3, XT, HT, "norm_final", T)


OUTS = {"yT": (D, T), "cn": (P, MH, P + 1), "cns": (P, MH, NB, P + 1), "m": (MH, 1 + NB), "conv": (P, 8, 27),
        "S": (P, RP, RD), "Ss": (P, RP, NB, RD), "shift": (P, NRW, 9), "mk": (P, MH, NMEM), "mv": (P, 2, 512)}


def kernel(**inputs):
    import numpy as np
    import concourse.bacc as bacc
    from concourse.bass_utils import run_bass_kernel_spmd

    x = {k: np.asarray(w) for k, w in inputs.items()}
    w1 = {k: w[0] for k, w in x.items() if k != "norm_final"}

    def tiles(w):
        return w.reshape(-1, P).T

    vecs = [tiles(w1["norm_mix"])] + [tiles(w1["ml_conv_w"][j]) for j in range(4)]
    vecs += [tiles(w1[k]) for k in ("ml_conv_b", "ml_norm_w", "rw_mu", "rw_w0", "rw_a0", "rw_kk", "rw_ka", "rw_rk",
                                    "rw_ln_w", "rw_ln_b", "mem_norm", "norm_ffn")]
    vecs += [tiles(x["norm_final"])]
    cn = np.concatenate([w1["state_mlstm_C"].transpose(3, 1, 0, 2), w1["state_mlstm_n"].transpose(2, 1, 0)[..., None]], 3)
    data = {
        "xT": np.concatenate([x["x_prompt"][0].T, x["x_sample"].reshape(TS, D).T], 1),
        "memT": x["mem_prompt"][0].T,
        "vecs": np.concatenate(vecs, 1),
        "gateb": w1["ml_gate_b"].reshape(2, MH).T,
        "m0T": w1["state_mlstm_m"].T,
        "cnT": cn,
        "convT": w1["state_mlstm_conv"].transpose(2, 0, 1).reshape(8, P, 24).transpose(1, 0, 2),
        "s0T": w1["state_rwkv_S"].reshape(NB, RP, 2, RD, RD).transpose(2, 4, 1, 0, 3).reshape(P, RP, NB, RD),
        "shT": w1["state_rwkv_shift"].T.reshape(NRW, P, NB).transpose(1, 0, 2),
        "memkT": w1["cache_mem_k"].transpose(3, 2, 0, 1).reshape(P, MH, NB * NMEM),
        "memv": w1["cache_mem_v"].reshape(NB, 2, P, MH, P).transpose(2, 3, 0, 1, 4).reshape(P, MH, NB * NMEM),
        "w_in": w1["w_in"],
        "wa": np.concatenate([w1["rw_w2"], w1["rw_a2"]], 0),
        "g2": w1["rw_g2"],
        "w_mk": w1["w_mk"], "w_mv": w1["w_mv"],
        "w_branch": w1["w_branch"].reshape(3 * 512, D), "w_out": w1["w_out"], "wq": w1["pk_wq"],
        "keysT": np.stack([w1["pk_k1"].T, w1["pk_k2"].T], 1),
        "uT": w1["pk_u"].reshape(P, NK, DT, P).transpose(3, 1, 2, 0),
        "vT": w1["pk_v"].reshape(P, NK, D),
    }
    nc = bacc.Bacc("TRN2", target_bir_lowering=False, num_devices=1)
    arrays, a, o = {}, {}, {}
    for name, w in data.items():
        arrays[f"in_{name}"] = np.ascontiguousarray(w)
        a[name] = nc.dram_tensor(f"in_{name}", arrays[f"in_{name}"].shape, F32, kind="ExternalInput").ap()
    for name, shape in OUTS.items():
        o[name] = nc.dram_tensor(f"out_{name}", shape, F32, kind="ExternalOutput").ap()
    hybrid_layer(nc, a, o)
    r = run_bass_kernel_spmd(nc, [arrays], core_ids=[0]).results[0]
    r = {name: np.asarray(r[f"out_{name}"]) for name in OUTS}

    y = r["yT"].T
    conv = r["conv"].transpose(1, 0, 2).reshape(8 * P, 27)
    shift = r["shift"].transpose(1, 0, 2).reshape(NRW * P, 9)
    s = r["S"].reshape(2, RD, RP, RD).transpose(2, 0, 3, 1).reshape(1, 1, RH, RD, RD)
    ss = r["Ss"].reshape(2, RD, RP, NB, RD).transpose(3, 2, 0, 4, 1).reshape(1, NB, RH, RD, RD)
    cn, cns = r["cn"].transpose(1, 2, 0)[None, None], r["cns"].transpose(2, 1, 3, 0)[None]
    outs = (
        y[:TP].reshape(1, TP, D), y[TP:].reshape(NB, NS, D),
        cn[:, :, :, :P], cn[:, :, :, P], r["m"][:, 0].reshape(1, 1, MH), conv[:, 0:3].T[None, None], s,
        shift[:, 0].reshape(1, 1, -1), r["mk"].transpose(2, 1, 0)[None, None],
        r["mv"].transpose(1, 0, 2).reshape(1, 1, NMEM, MH, P),
        cns[:, :, :, :P], cns[:, :, :, P], r["m"][:, 1:].T[None],
        conv[:, 3:].reshape(8 * P, NB, 3).transpose(1, 2, 0)[None], ss, shift[:, 1:].T[None],
    )
    return tuple(np.ascontiguousarray(w) for w in outs)
```

```python
from contextlib import ExitStack

import concourse.bass as bass
from concourse import mybir

F32 = mybir.dt.float32
F32R = mybir.dt.float32r
U32 = mybir.dt.uint32
I32 = mybir.dt.int32
ALU = mybir.AluOpType
ACT = mybir.ActivationFunctionType
AX_X = mybir.AxisListType.X

P = 128
D = 1024
DT = D // P
TP = 512
NB, NS = 8, 4
TS = NB * NS
T = TP + TS
NTT = TP // P + 1
MH = 4
RH, RD = 8, 64
RP = RH // 2
CH = 64
NC = TP // CH
NMEM = 256
NRW = 14
PH, PK, NK = 8, 16, 128
RSEQ = [12, 13, 0, 4, 8, 1, 5, 9, 2, 6, 10, 3, 7, 11]
EPS = 1e-6
GN_EPS = 64e-5
SCALE = float(P) ** -0.5
DECAY = -float.fromhex("0x1.368b2fc6f9609p-1")
LOW = -3.0e38
COLS = [(0, TP), (TP, TS)]

OFF_QK, OFF_V, OFF_O, OFF_IF, OFF_RW = 0, 1024, 1536, 2048, 2056
OFF_XQ = OFF_RW + NRW * P
OFF_GATE = OFF_XQ + 512
NW = 6
NSLOT = 4

VEC = {}
_at = 0
for _name, _n in [("norm_mix", 8), ("conv_w", 32), ("conv_b", 8), ("ml_norm", 4), ("mu", 14), ("w0", 4), ("a0", 4),
                  ("kk", 4), ("ka", 4), ("rk", 4), ("ln_w", 4), ("ln_b", 4), ("mem_norm", 8), ("norm_ffn", 8),
                  ("norm_final", 8)]:
    VEC[_name] = _at
    _at += _n
NVEC = _at

RUNS = [(0, 1, 16), (1, 1, 8), (2, 2, 5), (4, 4, 3), (8, 8, 1)]
NCAND = sum(n * w for _, n, w in RUNS)
EB = 32
NEB = T // EB
EQT = 4
NQT = NK // EQT
NOH = 4
EG = 2
NG = NK // EG
HALF = T // 2
AREN = 28400


def product_order():
    o = ["ms0", "gi", "gf"] + [f"qk{n}" for n in range(8)] + [f"v{t}" for t in range(NTT)] + ["gt"]
    o += ["mb0", "kt0"] + [f"s0_{i}" for i in range(4)]
    for h in range(MH):
        o += [f"o{h}", f"c{h}", f"cs{h}", f"n{h}", f"m{h}"]
        if h + 1 < MH:
            o += [f"mb{h + 1}", f"kt{h + 1}", f"s{h + 1}_0", f"s{h + 1}_1", f"t{h}", f"s{h + 1}_2", f"s{h + 1}_3"]
        else:
            o += [f"t{h}"]
    o += [f"r{n}" for n in RSEQ[0:5]]
    for p in range(RP):
        nxt = [f"r{n}" for n in RSEQ[5 + 3 * p:8 + 3 * p]] + 3 * [""]
        o += [x for x in (f"w{p}", f"a{p}", nxt[0], f"kn{p}", nxt[1], f"bn{p}", nxt[2]) if x]
    inv = lambda c, i: [f"i{c}_{i}a", f"i{c}_{i}b"]
    o += ["ab0", "nt0"] + inv(0, 1) + inv(0, 2) + inv(0, 3)
    for c in range(NC):
        for i in range(4, 11):
            o += inv(c, i)
        o += [f"vt{c}", f"bt{c}"]
        if c + 1 < NC:
            o += [f"ab{c + 1}", f"nt{c + 1}", f"u{c}"] + inv(c + 1, 1) + [f"uu{c}"] + inv(c + 1, 2) + inv(c + 1, 3)
            o += [f"y{c}"]
        else:
            o += [f"u{c}", f"uu{c}", f"y{c}"]
    o += ["abs", "nts", "is1", "is2", "vts", "bts", "us", "uus", "ys"] + [f"ss{p}" for p in range(RP)]
    for p in range(RP):
        o += [f"ym{p}", f"xq{p}", f"yv{p}", f"g{p}"]
    o += ["ms1"] + [f"mk{h}" for h in range(MH)] + ["mv0", "mv1", "as0"]
    for h in range(MH):
        o += ([f"as{h + 1}"] if h + 1 < MH else []) + [f"at{h}", f"ao{h}"]
    o += [f"ds{h}" for h in range(MH)] + ["dt"] + [f"do{h}" for h in range(MH)]
    for n in range(DT):
        for j in range(3):
            o += [f"gb{n}_{j}", f"gg{n}_{j}"]
    o += [f"x{n}" for n in range(DT)]
    o += ["ms2", "pq0"]
    for i in range(1, 16):
        o += [f"pq{i}", f"ps{i - 1}"]
    o += ["ps15"] + [f"pt{t}" for t in range(NTT)]
    return o + ["ms3"]


ORDER = product_order()
NO = {k: i for i, k in enumerate(ORDER)}
NPROD = len(ORDER)


def weight_stream():
    s = [("if", "w_in", 0, DT, OFF_IF, 8, "gf")]
    s += [(f"qk{n}", "w_in", 0, DT, OFF_QK + n * P, P, f"qk{n}") for n in range(8)]
    s += [(f"v{c}", "w_in", 0, DT, OFF_V + c * P, P, f"v{NTT - 1}") for c in range(4)]
    s += [(f"o{h}", "w_in", 0, DT, OFF_O + h * P, P, f"o{h}") for h in range(MH)]
    s += [(f"r{n}", "w_in", 0, DT, OFF_RW + n * P, P, f"r{n}") for n in RSEQ]
    s += [(f"xq{h}", "w_in", 0, DT, OFF_XQ + h * P, P, f"xq{h}") for h in range(MH)]
    s += [(f"mk{h}", "w_mk", 0, DT, h * P, P, f"mk{h}") for h in range(MH)]
    s += [(f"mv{c}", "w_mv", 0, DT, c * P, P, "mv1") for c in range(4)]
    for n in range(DT):
        for j in range(3):
            s += [(f"gb{n}_{j}", "w_branch", 4 * j, 4, n * P, P, f"gb{n}_{j}")]
            s += [(f"gg{n}_{j}", "w_in", 0, DT, OFF_GATE + j * D + n * P, P, f"gg{n}_{j}")]
    s += [(f"x{n}", "w_out", 0, DT, n * P, P, f"x{n}") for n in range(DT)]
    s += [(f"pq{i}", "wq", 0, DT, i * P, P, f"pq{i}") for i in range(16)]
    return s


WS = weight_stream()
WNO = {w[0]: i for i, w in enumerate(WS)}
SPLIT = [f"gg{n}_{j}" for n in range(DT) for j in range(3)] + [f"x{n}" for n in range(DT)]


def bc(ap, axis, n):
    a = ap.unsqueeze(axis)
    shape = list(a.shape)
    shape[axis] = n
    return a.to_broadcast(shape)


class Steps:

    def __init__(self, eng, own):
        self.eng, self.own, self.n = eng, own, {}

    def __call__(self, ins, sem=None):
        sem = self.own if sem is None else sem
        k = id(sem)
        self.n[k] = self.n.get(k, 0) + 1
        ins.then_inc(sem, 1)
        self.eng.wait_ge(sem, self.n[k])


def hybrid_layer(nc, a, o):
    ctx = ExitStack()
    with ctx:
        def sb(name, shape, dt=F32, stack=ctx):
            return stack.enter_context(nc.sbuf_tensor(name, shape, dt))

        sems = {}

        def S(name):
            if name not in sems:
                sems[name] = ctx.enter_context(nc.semaphore(name))
            return sems[name]

        XT = sb("XT", [P, DT, T])
        vec = sb("vec", [P, NVEC])
        ident = sb("ident", [P, P])
        ones = sb("ones", [P, P])
        blk = sb("blk", [P, P])
        tri = sb("tri", [P, P])
        rmask = sb("rmask", [P, 2, CH])
        low = sb("low", [CH, CH])
        b16 = sb("b16", [CH, CH])
        smask = sb("smask", [TS, TS])
        slow = sb("slow", [TS, TS])
        srm = sb("srm", [2 * TS, 2, TS])
        bmask = sb("bmask", [P, NB, TS])
        bexp = sb("bexp", [2 * TS, NB])
        reset = sb("reset", [P, T])
        sel = sb("sel", [MH, MH, P])
        iota = sb("iota", [P, P])
        rstd = sb("rstd", [P, T])
        early = ExitStack()
        HT = sb("HT", [P, DT, T], stack=early)
        W = sb("W", [P, NW, DT, P], stack=early)
        BR = sb("BR", [P, 12, T], stack=early)
        part = ExitStack()
        arena = sb("arena", [P, AREN], stack=part)
        part.close()
        SGB = sb("SGB", [P, 3, T], stack=part)
        TMP = sb("TMP", [P, 2, T], stack=part)
        YM = sb("YM", [P, 2, T], stack=part)
        DH, DL, YH, YL = [sb(n, [P, DT, T], F32R, part) for n in ("DH", "DL", "YH", "YL")]
        GWH, GWL = [sb(n, [P, 2, DT, P], F32R, part) for n in ("GWH", "GWL")]
        part.close()
        arena2 = sb("arena2", [P, AREN], stack=part)
        part.close()
        early.close()
        GQ = sb("GQ", [P, NEB, EQT, EB])
        AX = sb("AX", [P, EG, T])
        WL, WH = [sb(n, [P, 2, EG, T], F32R) for n in ("WL", "WH")]
        XH, XL = [sb(n, [P, DT, T], F32R) for n in ("XH", "XL")]
        UH, UL = [sb(n, [P, 2, EG, DT, P], F32R) for n in ("UH", "UL")]
        VH, VL = [sb(n, [P, 2, EG, D], F32R) for n in ("VH", "VL")]
        raw = sb("raw", [P, 2, 2, EG * D])
        RAW = {"u": raw[:, 0], "v": raw[:, 1]}
        YO = raw[:].rearrange("p a b c -> p (a b c)")[:, 0:DT * T]
        PS = ctx.enter_context(nc.psum_tensor("PS", [P, NSLOT, 2, 512], F32))

        def carve(at, *shapes, arena=arena):
            out = []
            for shape in shapes:
                n = 1
                for d in shape:
                    n *= d
                v = arena[:, at:at + n]
                if len(shape) > 1:
                    names = "abcd"[:len(shape)]
                    v = v.rearrange("p (" + " ".join(names) + ") -> p " + " ".join(names),
                                    **{names[i]: shape[i] for i in range(len(shape) - 1)})
                out.append(v)
                at += n
            assert at <= AREN, at
            return out + [at]

        (QKP, QK, VX, SO, CN, CO, MB, DD, DS, NU, HH, SQ, KW, VB, QM, QS, GTM, CT, CHI, s1, s2, s3, s4, EI, GB, M0, MO, EIL,
         _) = carve(0, (8, 3 + TP + NB * 7), (8, T), (NTT, MH, 129), (MH, T), (MH, NB, 129), (MH, 129), (2, T + TS),
                    (4, 512), (TS,), (NTT, 129), (NTT, P), (NTT, P), (NTT, P), (NB, 129), (NB, TS), (TS,),
                    (NTT, 3, MH), (8, 27), (8, 24), (NTT,), (NTT,), (NTT,), (NTT,), (TS,), (2,), (NB,), (1 + NB,), (NB,))
        CV = DD.rearrange("p a b -> p (a b)")[:, 0:2 * T].rearrange("p (a b) -> p a b", a=2)
        rows = BR[0:MH, 4:12]
        IR, FR, LR, FC, GR, MR, MT, EM = [rows[:, i, :] for i in range(8)]
        ONR, WG = EM, LR

        RW, AR, BK, ARS, BKS, G2, S0, ST, WE, WES, LO, SH, bt = carve(
            0, (NRW, T), (RP, NC, 2, CH), (RP, NC, 2, CH), (RP, 2, TS), (RP, 2, TS), (512,), (RP, NB, RD),
            (RP, RD), (RP, NC), (RP, NB), (NRW, 9), (NRW, NB))
        RPD, TW, LW, AG, KN, SQB, CC, EW, EN, EP, KPB, OMK, WA, _ = carve(
            bt, (2, 1 + TP + NB * 5), (T,), (T,), (T,), (T,), (T,), (T,), (T,), (T,), (T,), (T,), (RP,),
            (512,))
        AB, PQ, PQD, PQ2, XX, MM, U0S, UV, BKT, _ = carve(
            bt, (2, RH, 2 * CH), (2, RH, CH), (2, RH, CH), (2, RH, CH), (2, RH, CH), (2, RH, CH), (RH, CH), (RH, RD),
            (RP, P))
        ABS, QSS, MS, XS, AM, UVS, BKTS, UVE, _ = carve(
            bt, (RH, 2 * TS), (RH, TS), (RH, TS), (RH, TS), (2, RP, NB, TS), (RH, RD), (RP, P), (2, NB, RD))
        YC, YQ, _ = carve(bt, (T,), (T,))

        (MEM, MN, MKT, MV, PA, PAT, KB, VBM, XM, PM, PT3, c1, c2, c3, _) = carve(
            0, (DT, NMEM), (DT, NMEM), (MH, NMEM), (2, 512), (2, 4, NMEM), (2, 512), (2, NB * NMEM),
            (2, NB * NMEM), (MH, NB, TS), (2, MH, NB, TS), (2, P), (4,), (4,), (4,))

        XQ = BR[:, 8:12]

        IT, = carve(AREN - 3 * T, (3, T), arena=arena2)[:1]
        (QT, SC, SC2, V16, IX, IF, CAND, CAND2, EQ, TOP, PX, P8, P5, P3, P1, ROW0, ROWB, AFX, BFX, KSEL, GAT, e1, _) = carve(
            0, (3, T), (4, NTT, P), (4, NTT, P), (NTT, 16, PK), (NTT, 16, PK), (NTT, 16, PK), (PH, NCAND),
            (PH, NCAND), (2, P, PK), (PH, PK), (PH, PK), (P,), (P,), (P,), (P,), (P,), (P,), (2, P), (2, P), (2, P), (2, PH, PK), (PH,), arena=arena2)
        IX, PX, P8, P5, P3, P1 = [x.bitcast(U32) for x in (IX, PX, P8, P5, P3, P1)]

        OH, GST, _ = carve(0, (NOH, 2, 4, P), (2, P, EB), arena=arena2)

        gate_table = nc.dram_tensor("gate_table", [NQT, P, NEB * EQT * EB], F32, kind="Internal").ap()

        mm = S("mm")
        ev = [S(f"ev{i}") for i in range(NSLOT)]
        wl = [S(f"wl{i}") for i in range(NW)]
        ld = S("ld")
        bar = S("bar")

        def slot(key):
            return PS[:, NO[key] % NSLOT]

        def take(eng, key):
            eng.wait_ge(mm, NO[key] + 1)
            return slot(key)

        def give(eng, ins, key):
            s = ev[NO[key] % NSLOT]
            ins.then_inc(s, 1)
            eng.wait_ge(s, NO[key] // NSLOT + 1)

        def barrier(eng, k):
            eng.sem_inc(bar, 1)
            eng.wait_ge(bar, 4 * k + max(0, k - 4))

        def halves(x):
            return x.rearrange("p (a n) -> p a n", a=2)

        def tcols(t):
            return (t * P, P) if t < NTT - 1 else (TP, TS)

        def after(eng, name, value):
            if not isinstance(value, int) or value > 0:
                eng.wait_ge(S(name), value)

        def turns(eng, body, n=NG):
            body(0, 0)
            with eng.Fori(1, n // 2 - 1) as j:
                body(2 * j - 1, 1)
                body(2 * j, 0)
            for g in range(n - 3, n):
                body(g, g % 2)

        def v(name, i):
            return vec[:, VEC[name] + i:VEC[name] + i + 1]

        block = ctx.enter_context(nc.Block())

        @block.sync
        def _(sp):
            sp.dma_start(XT[:], a["xT"].rearrange("(k p) t -> p k t", p=P)).then_inc(S("ldx"), 16)
            sp.dma_start(vec[:], a["vecs"]).then_inc(S("ldv"), 16)
            for i, (_, name, k0, nk, c0, wd, _) in enumerate(WS):
                if i >= NW:
                    sp.wait_ge(mm, NO[WS[i - NW][6]] + 1)
                src = a[name][k0 * P:(k0 + nk) * P, c0:c0 + wd].rearrange("(k p) n -> p k n", p=P)
                sp.dma_start(W[:, i % NW, 0:nk, 0:wd], src).then_inc(wl[i % NW], 16)
            barrier(sp, 5)

            for k in range(NEB):
                sp.wait_ge(S("ge"), 4 * (k + 1))
                sp.dma_start(gate_table[:, :, k * EQT * EB:(k + 1) * EQT * EB].rearrange("g p n -> p g n"),
                             GST[:, k % 2].rearrange("p (g e) t -> p g (e t)", e=EQT)).then_inc(S(f"gw{k % 2}"), 16)
            sp.wait_ge(S("gw0"), 16 * ((NEB + 1) // 2))
            sp.wait_ge(S("gw1"), 16 * (NEB // 2))
            barrier(sp, 6)

            def load(x, g, b):
                src = a[x + "T"][:, bass.ds(g * EG, EG)]
                dst = RAW[x][:, b]
                if x == "u":
                    src = src.rearrange("p e k n -> p e (k n)")
                sp.dma_start(dst.rearrange("p (e n) -> p e n", e=EG), src).then_inc(S(f"l{x}{b}"), 16)

            def load_gates(j):
                sp.dma_start(GQ[:].rearrange("p a b c -> p (a b c)"),
                             gate_table[bass.ds(j, 1)].rearrange("a p n -> p (a n)")).then_inc(S("lg"), 16)

            for b in range(2):
                load("u", b, b)
                load("v", b, b)
            sp.wait_ge(S("xsplit"), 1)
            load_gates(0)
            with sp.Fori(1, NG // 2) as j:
                sp.wait_ge(S("ulo"), 2 * j - 1)
                load("u", 2 * j, 0)
                sp.wait_ge(S("ulo"), 2 * j)
                load("u", 2 * j + 1, 1)
                sp.wait_ge(S("vlo"), 2 * j - 1)
                load("v", 2 * j, 0)
                sp.wait_ge(S("vlo"), 2 * j)
                load("v", 2 * j + 1, 1)
                sp.wait_ge(S("wr"), 4 * j)
                load_gates(j)
            sp.wait_ge(S("hn"), 4)
            sp.dma_start(o["yT"].rearrange("(k p) t -> p k t", p=P), YO).then_inc(S("oy"), 16)
            sp.wait_ge(S("oy"), 16)

        @block.gpsimd
        def _(pool):
            step = Steps(pool, S("pl"))

            def fill(tile, value):
                step(pool.memset(tile, value))

            def keep(tile, pattern, base, row):
                step(pool.affine_select(out=tile, in_=tile, compare_op=ALU.is_ge, fill=0.0, base=base,
                                        pattern=pattern, channel_multiplier=row))

            fill(ident[:], 0.0)
            step(pool.affine_select(out=ident[:], in_=ident[:], compare_op=ALU.not_equal, fill=1.0, base=0,
                                    pattern=[[-1, P]], channel_multiplier=1))
            fill(ones[:], 1.0)
            fill(blk[:], 0.0)
            for h in range(2):
                fill(blk[h * RD:(h + 1) * RD, h * RD:(h + 1) * RD], 1.0)
            fill(tri[:], 1.0)
            keep(tri[:], [[1, P]], 0, -1)
            fill(rmask[:], 1.0)
            for r in range(2):
                for x in range(2):
                    keep(rmask[r * CH:(r + 1) * CH, x, :], [[1, CH]], x - 1, -1)
            fill(low[:], 1.0)
            keep(low[:], [[-1, CH]], -1, 1)
            fill(b16[:], 1.0)
            b16v = b16[:].rearrange("p (a b) -> p a b", b=16)
            keep(b16v, [[-16, CH // 16], [0, 16]], 0, 1)
            keep(b16v, [[16, CH // 16], [0, 16]], 15, -1)
            fill(smask[:], 1.0)
            keep(smask[:].rearrange("p (a b) -> p a b", b=NS), [[-NS, NB], [0, NS]], 0, 1)
            keep(smask[:], [[1, TS]], 0, -1)
            fill(slow[:], 1.0)
            keep(slow[:].rearrange("p (a b) -> p a b", b=NS), [[NS, NB], [0, NS]], NS - 1, -1)
            keep(slow[:], [[-1, TS]], -1, 1)
            fill(srm[:], 1.0)
            for r in range(2):
                for x in range(2):
                    m = srm[r * TS:(r + 1) * TS, x, :]
                    keep(m.rearrange("p (a b) -> p a b", b=NS), [[-NS, NB], [0, NS]], 0, 1)
                    keep(m, [[1, TS]], x - 1, -1)
            fill(bmask[:], 0.0)
            for b in range(NB):
                fill(bmask[:, b, b * NS:(b + 1) * NS], 1.0)
            fill(bexp[:], 1.0)
            for r in range(2):
                m = bexp[r * TS:(r + 1) * TS, :]
                keep(m, [[-NS, NB]], 0, 1)
                keep(m, [[NS, NB]], NS - 1, -1)
            fill(reset[:], 1.0)
            fill(reset[:, 0:TP].rearrange("p (a b) -> p a b", b=CH)[:, :, 0:1], 0.0)
            fill(reset[:, TP:T].rearrange("p (a b) -> p a b", b=NS)[:, :, 0:1], 0.0)
            fill(sel[:], 1.0)
            keep(sel[:], [[-1, MH], [0, P]], 0, 1)
            keep(sel[:], [[1, MH], [0, P]], 0, -1)
            step(pool.iota(iota[:], [[1, P]], base=0, channel_multiplier=0, allow_small_or_imprecise_dtypes=True))
            for n in range(8):
                fill(QKP[:, n, 0:3], 0.0)
            fill(VX[:, :, :, P:P + 1], 1.0)
            fill(NU, 0.0)
            fill(GTM, 1.0)
            pool.sem_inc(S("const"), 1)
            for dst, src, n in ((CHI, "convT", "ldc"), (CN, "cnT", "ldn"), (M0[0:MH], "m0T", "ldm"),
                                (GB[0:MH], "gateb", "ldg")):
                pool.dma_start(dst, a[src]).then_inc(S(n), 16)
            pool.wait_ge(S("ctail"), 8)
            pool.dma_start(o["conv"], CT).then_inc(S("oa"), 16)
            pool.wait_ge(S("gates"), 1)
            pool.dma_start(o["m"], MO[0:MH]).then_inc(S("oa"), 16)
            pool.wait_ge(S("cnew"), MH)
            pool.dma_start(o["cn"], CO).then_inc(S("oa"), 16)
            pool.dma_start(o["cns"], CN).then_inc(S("oa"), 16)
            pool.wait_ge(S("oa"), 64)
            barrier(pool, 1)
            for i in range(2):
                fill(RPD[:, i, 0:1], 0.0)
            fill(ST, 0.0)
            pool.sem_inc(S("rzero"), 1)
            for dst, src, n in ((SH, "shT", "ldsh"), (WA, "wa", "ldwa"), (G2, "g2", "ldg2"), (S0, "s0T", "lds0")):
                pool.dma_start(dst, a[src]).then_inc(S(n), 16)
            pool.wait_ge(S("rwin"), 2 * NRW)
            pool.dma_start(o["shift"], LO).then_inc(S("ob"), 16)
            pool.wait_ge(S("stnew"), NC)
            pool.dma_start(o["S"], ST).then_inc(S("ob"), 16)
            pool.wait_ge(S("s0new"), RP)
            pool.dma_start(o["Ss"], S0).then_inc(S("ob"), 16)
            pool.wait_ge(S("ob"), 48)
            barrier(pool, 2)
            pool.dma_start(MEM, a["memT"].rearrange("(k p) t -> p k t", p=P)).then_inc(S("ldmem"), 16)
            for r in range(2):
                for h in (2 * r, 2 * r + 1):
                    if r:
                        pool.wait_ge(mm, NO[f"ds{h - 2}"] + 1)
                    pool.dma_start(KB[:, h % 2], a["memkT"][:, h]).then_inc(S(f"ldk{h % 2}"), 16)
                for h in (2 * r, 2 * r + 1):
                    if r:
                        pool.wait_ge(mm, NO[f"do{h - 2}"] + 1)
                    pool.dma_start(VBM[:, h % 2], a["memv"][:, h]).then_inc(S(f"ldvv{h % 2}"), 16)
            pool.wait_ge(S("mkv"), MH + 2)
            pool.dma_start(o["mk"], MKT).then_inc(S("oc"), 16)
            pool.dma_start(o["mv"], MV).then_inc(S("oc"), 16)
            pool.wait_ge(S("oc"), 32)
            barrier(pool, 3)
            barrier(pool, 4)
            pool.dma_start(KSEL, a["keysT"]).then_inc(S("ldkeys"), 16)
            for t in range(NTT):
                _, m = tcols(t)
                pool.wait_ge(S("pk1"), t + 1)
                ifv = IF[0:m, t].rearrange("p (h s) k -> p h s k", s=2)
                for i in range(2):
                    e4 = EQ[0:m, i].rearrange("p (h k) a -> p h k a", h=PH)
                    step(pool.tensor_tensor(e4, e4, bc(ifv[:, :, i, :], 2, PK), ALU.mult), S("eq"))
            barrier(pool, 5)

            def gate_hots(i):
                for u in range(8):
                    pool.wait_ge(S("oh1"), 8 * i + u + 1)
                    x = OH[:, u % NOH, 1]
                    pool.tensor_tensor(x, x, bc(IT[:, 2, bass.ds(EB * i + 4 * u, 4)], 2, P), ALU.mult).then_inc(S("oh2"), 1)

            with pool.Fori(0, NEB) as i:
                gate_hots(i)
            pool.wait_ge(S("oh2"), 8 * NEB)
            barrier(pool, 6)

        @block.scalar
        def _(act):
            step = Steps(act, S("ac"))

            def f(out, in_, func, sem=None, bias=None, scale=None):
                kw = {}
                if bias is not None:
                    kw["bias"] = bias
                if scale is not None:
                    kw["scale"] = scale
                step(nc.scalar.activation(out, in_, func, **kw), sem)

            def out_of(key, out, in_, func, **kw):
                give(act, nc.scalar.activation(out, in_, func, **kw), key)

            def both(key, dst, func, sem=None, **kw):
                ps = take(act, key)
                out_of(key, halves(dst), ps[0:dst.shape[0], :, 0:HALF], func, **kw)
                if sem is not None:
                    act.sem_inc(sem, 1)

            def padded(ps, key, prompt, sample):
                f(prompt[:, 0:HALF], ps[:, 0, 0:HALF], ACT.Copy)
                f(prompt[:, HALF:TP], ps[:, 1, 0:TP - HALF], ACT.Copy)
                out_of(key, sample, ps[:, 1, TP - HALF:HALF].rearrange("p (b t) -> p b t", b=NB), ACT.Copy)

            def root(i, n):
                act.wait_ge(S("rc"), i + 1)
                f(rstd[:, 0:n], rstd[:, 0:n], ACT.Sqrt, S("rs"))

            act.wait_ge(S("ldx"), 16)
            f(HT[:], XT[:], ACT.Square, S("sq"))
            root(0, T)
            act.wait_ge(S("const"), 1)
            act.wait_ge(S("ldc"), 16)
            act.wait_ge(S("gi"), 1)
            f(LR, FR, ACT.Abs)
            f(LR, LR, ACT.Exp, scale=-1.0)
            f(LR, LR, ACT.Ln, S("ls"), bias=1.0)
            act.wait_ge(S("gi"), 2)
            f(EM, MT, ACT.Exp, S("grows"), scale=-1.0)
            f(WG, WG, ACT.Exp)
            f(EI[0:MH], EI[0:MH], ACT.Exp, S("wg"))
            for n in range(9):
                if n < 8:
                    ps = take(act, f"qk{n}")
                    q = QKP[:, n, 3 + TP:].rearrange("p (b t) -> p b t", b=NB)
                    f(q[:, :, 0:3], CHI[:, n, :].rearrange("p (b t) -> p b t", b=NB), ACT.Copy)
                    padded(ps, f"qk{n}", QKP[:, n, 3:3 + TP], q[:, :, 3:7])
                    f(CT[:, n, 0:3], QKP[:, n, TP:TP + 3], ACT.Copy)
                    f(CT[:, n, 3:27].rearrange("p (b t) -> p b t", b=NB), q[:, :, 4:7], ACT.Copy, S("ctail"))
                if n:
                    act.wait_ge(S("cv"), n)
                    f(QK[:, n - 1, :], CV[:, (n - 1) % 2, :], ACT.Silu, S("silu"))
            for t in range(NTT):
                _, m = tcols(t)
                ps = take(act, f"v{t}")
                out_of(f"v{t}", VX[0:m, t, :, 0:P], ps[0:m, 0, :].rearrange("p (h d) -> p h d", h=MH), ACT.Copy)
                act.sem_inc(S("vx"), 1)
            def decays(h):
                ps = take(act, f"mb{h}")
                if h >= 2:
                    act.wait_ge(S("hnorm"), h - 1)
                f(MB[:, h % 2, 0:TP], ps[:, 0, :], ACT.Copy)
                out_of(f"mb{h}", MB[:, h % 2, TP:T + TS], ps[:, 1, 0:2 * TS], ACT.Copy)
                act.sem_inc(S("mbr"), 1)
                for i in range(4):
                    act.wait_ge(S("dd"), 5 * h + i + 1)
                    f(DD[:, i, i * P:TP], DD[:, i, i * P:TP], ACT.Exp, S("ddx"), scale=-1.0)
                act.wait_ge(S("dd"), 5 * h + 5)
                f(DS[0:TS], DS[0:TS], ACT.Exp, S("ddx"), scale=-1.0)

            decays(0)
            for h in range(MH):
                both(f"o{h}", SO[:, h, :], ACT.Sigmoid, S("so"))
                if h + 1 < MH:
                    decays(h + 1)
                act.wait_ge(S("hv"), h + 1)
                f(s3, s3, ACT.Sqrt, S("hs"))
            barrier(act, 1)

            act.wait_ge(S("rzero"), 1)
            act.wait_ge(S("ldsh"), 16)
            def window(i):
                n = RSEQ[i]
                ps = take(act, f"r{n}")
                if i >= 2:
                    act.wait_ge(S("rsh"), i - 1)
                r = RPD[:, i % 2, :]
                q = r[:, 1 + TP:].rearrange("p (b t) -> p b t", b=NB)
                f(q[:, :, 0], SH[:, n, :], ACT.Copy)
                padded(ps, f"r{n}", r[:, 1:1 + TP], q[:, :, 1:5])
                f(LO[:, n, 0:1], r[:, TP:TP + 1], ACT.Copy, S("rwin"))
                f(LO[:, n, 1:9], q[:, :, 4], ACT.Copy, S("rwin"))

            for i in range(5):
                window(i)
            act.wait_ge(S("rsh"), 2)
            f(TW[0:64], RW[0:64, 12, :], ACT.Tanh, S("tanh"))
            f(RW[:, 13, :], RW[:, 13, :], ACT.Sigmoid)
            for p in range(RP):
                if p:
                    act.wait_ge(S("rwops"), p)
                both(f"w{p}", LW, ACT.Sigmoid, bias=v("w0", p))
                both(f"a{p}", AG, ACT.Sigmoid, bias=v("a0", p))
                act.sem_inc(S("wa"), 1)
                if p + 1 < RP:
                    window(5 + 3 * p)
                act.wait_ge(S("kv"), p + 1)
                f(KN, KN, ACT.Sqrt, S("ks"))
                if p + 1 < RP:
                    window(6 + 3 * p)
                act.wait_ge(S("cum"), p + 1)
                f(EW, CC, ACT.Exp)
                f(EN, CC, ACT.Exp, scale=-1.0)
                f(EP, EP, ACT.Exp, S("dec"))
                if p + 1 < RP:
                    window(7 + 3 * p)
            hb = slice(0, CH)

            def inverse_copy(c, i):
                for z in range(2):
                    key = f"i{c}_{i}{'ab'[z]}"
                    hs = slice(4 * z, 4 * z + 4)
                    ps = take(act, key)
                    two = ps[hb, :, 0:4 * CH].rearrange("p a (h n) -> p a h n", h=4)
                    dst = MM if i == 7 else PQ2
                    if i == 8:
                        out_of(key, PQ2[hb, 0, hs], two[:, 0], ACT.Copy)
                    else:
                        out_of(key, dst[hb, :, hs], two, ACT.Copy)
                    act.sem_inc(S("icp"), 1)

            def outputs(c, key, n):
                ps = take(act, key)
                f(RW[:, 4:8, c * CH:c * CH + n], ps[:, 0, 0:RP * n].rearrange("p (a b) -> p a b", a=RP), ACT.Copy, S("yev"))

            inverse_copy(0, 1)
            inverse_copy(0, 3)
            for c in range(NC):
                for i in (5, 7, 8):
                    inverse_copy(c, i)
                if c + 1 < NC:
                    inverse_copy(c + 1, 1)
                    inverse_copy(c + 1, 3)
                outputs(c, f"y{c}", CH)
            outputs(NC, "ys", TS)
            for p in range(RP):
                both(f"xq{p}", XQ[:, p, :], ACT.Copy, S("xq"))
                act.wait_ge(S("yv"), p + 1)
                f(rstd[:], rstd[:], ACT.Sqrt, S("ysq"))
            barrier(act, 2)

            act.wait_ge(S("ldmem"), 16)
            f(MN, MEM, ACT.Square, S("sq"))
            root(1, NMEM)
            for h in range(MH):
                ps = take(act, f"mk{h}")
                out_of(f"mk{h}", MKT[:, h, :], ps[:, 0, 0:NMEM], ACT.Copy)
                act.sem_inc(S("mkv"), 1)
            for s in range(2):
                ps = take(act, f"mv{s}")
                out_of(f"mv{s}", MV[:, s, :], ps[:, 0, :], ACT.Copy)
                act.sem_inc(S("mkv"), 1)
            def exponentials(h):
                act.wait_ge(S("sx"), h + 1)
                f(PA[:, h % 2], PA[:, h % 2], ACT.Exp, S("sxe"), scale=SCALE)

            exponentials(0)
            for h in range(MH):
                if h + 1 < MH:
                    exponentials(h + 1)
                ps = take(act, f"at{h}")
                if h:
                    act.wait_ge(mm, NO[f"ao{h - 1}"] + 1)
                out_of(f"at{h}", PAT, ps, ACT.Copy)
                act.sem_inc(S("pat"), 1)
                ps = take(act, f"ao{h}")
                out_of(f"ao{h}", BR[:, 8 + h, 0:TP], ps[:, 0, :], ACT.Copy)
            act.wait_ge(S("sx"), MH + 1)
            f(PA[:, 0, 0, :], PA[:, 0, 0, :], ACT.Exp, S("sxe"), scale=SCALE)
            for h in range(MH):
                ps = take(act, f"do{h}")
                out_of(f"do{h}", BR[:, 8 + h, TP:T], ps[:, 0, 0:TS], ACT.Copy)
            barrier(act, 3)

            def weight_high(i):
                w = WNO[SPLIT[i]]
                act.wait_ge(wl[w % NW], 16 * (w // NW + 1))
                if i >= 2:
                    act.wait_ge(mm, NO[SPLIT[i - 2]] + 1)
                nc.scalar.activation(GWH[:, i % 2], W[:, w % NW], ACT.Copy).then_inc(S("gwhi"), 1)

            def merged_high(n):
                act.wait_ge(S("merged"), n + 1)
                nc.scalar.activation(YH[:, n, :], YM[:, n % 2, :], ACT.Copy).then_inc(S("yhi"), 1)

            weight_high(0)
            for k in range(DT):
                nc.scalar.activation(DH[:, k, :], HT[:, k, :], ACT.Copy).then_inc(S("dhi"), 1)
            for i in range(3 * DT):
                weight_high(i + 1)
                if i >= 3:
                    act.wait_ge(S("gated"), i - 2)
                both(SPLIT[i], SGB[:, i % 3, :], ACT.Sigmoid, S("sgb"))
                if i and i % 3 == 0:
                    merged_high(i // 3 - 1)
            merged_high(DT - 1)
            for i in range(3 * DT + 1, len(SPLIT)):
                weight_high(i)
            barrier(act, 4)

            f(HT[:], XT[:], ACT.Square, S("sq"))
            root(2, T)
            for i in range(2 * PH + 1):
                if i < 2 * PH:
                    both(f"pq{i}", QT[:, i % 3, :], ACT.Copy, S("pqe"))
                if i:
                    q = i - 1
                    if q >= 4:
                        act.wait_ge(S("scf"), q - 3)
                    ps = take(act, f"ps{q}")
                    f(SC[:, q % 4, 0:4, :], ps[:, 0, :].rearrange("p (a b) -> p a b", a=4), ACT.Copy)
                    out_of(f"ps{q}", SC[0:TS, q % 4, 4, :], ps[0:TS, 1, 0:P], ACT.Copy)
                    act.sem_inc(S("sce"), 1)
            for t in range(NTT):
                _, m = tcols(t)
                act.wait_ge(S("gx"), t + 1)
                f(GAT[0:m, t % 2], GAT[0:m, t % 2], ACT.Exp, S("gxe"))
            barrier(act, 5)

            def gate_block(i, b, write):
                if write is not None:
                    act.wait_ge(S(f"gw{b}"), write)
                for q in range(4):
                    act.wait_ge(S("ohf"), 8 * i + 2 * q + 2)
                    nc.scalar.activation(GST[:, b, :, q * 8:(q + 1) * 8].rearrange("p n t -> p t n"),
                                         PS[:, q].rearrange("p a (t n) -> p (a t) n", t=4), ACT.Copy).then_inc(S("ge"), 1)

            gate_block(0, 0, None)
            gate_block(1, 1, None)
            gate_block(2, 0, 16)
            with act.Fori(1, NEB // 2) as j:
                gate_block(2 * j + 1, 1, 16 * j)
                gate_block(2 * j + 2, 0, 16 * j + 16)
            act.wait_ge(S("ge"), 4 * NEB)
            barrier(act, 6)

            for k in range(DT):
                nc.scalar.activation(XH[:, k, :], HT[:, k, :], ACT.Copy).then_inc(S("xhi"), 1)

            def split_high(x, g, b, loaded):
                act.wait_ge(S(f"l{x}{b}"), loaded)
                if x == "u":
                    after(act, "pa", 2 * g - 2)
                    dst = UH[:, b].rearrange("p e k n -> p (e k n)")
                else:
                    after(act, "po", 8 * g - 8)
                    dst = VH[:, b].rearrange("p e n -> p (e n)")
                nc.scalar.activation(dst, RAW[x][:, b], ACT.Copy).then_inc(S(f"{x}hi"), 1)

            def gelus(g, b):
                for e in range(EG):
                    after(act, "pa", 2 * g + e + 1)
                    after(act, "wlo", 2 * g - 1 + e)
                    nc.scalar.activation(AX[:, e, :].rearrange("p (a n) -> p a n", a=2), PS[:, 2 * b + e, :, 0:HALF],
                                         ACT.Gelu).then_inc(S("af"), 1)
                after(act, "po", 8 * g - 8)
                for e in range(EG):
                    after(act, "wr", 2 * g + e + 1)
                    nc.scalar.activation(WH[:, b, e, :], AX[:, e, :], ACT.Copy).then_inc(S("whi"), 1)

            def turn_(g, b):
                fixed = isinstance(g, int)
                n = 1 - b
                if not fixed or g + 1 < NG:
                    split_high("v", g + 1, n, 16 * ((g + 1) // 2 + 1) if fixed else 8 * (g + 1 - n) + 16)
                if not fixed or g + 2 < NG:
                    split_high("u", g + 2, b, 16 * ((g + 2) // 2 + 1) if fixed else 8 * (g + 2 - b) + 16)
                if not fixed or g + 1 < NG:
                    gelus(g + 1, n)

            act.wait_ge(S("xsplit"), 1)
            split_high("u", 0, 0, 16)
            split_high("u", 1, 1, 16)
            split_high("v", 0, 0, 16)
            gelus(0, 0)
            turns(act, turn_)
            act.wait_ge(S("of"), 8 * NG)
            f(YO, XT[:].rearrange("p a b -> p (a b)"), ACT.Square, S("sq"))
            root(3, T)

        @block.tensor
        def _(pe):
            made = [0]

            def room(key):
                assert ORDER[made[0]] == key, (ORDER[made[0]], key)
                made[0] += 1
                if NO[key] >= NSLOT:
                    pe.wait_ge(ev[NO[key] % NSLOT], NO[key] // NSLOT)
                return slot(key)

            def mul(out, lhsT, rhs, first=True, last=True):
                return nc.tensor.matmul(out, lhsT, rhs, start=first, stop=last)

            def turn(out, in_):
                n = in_.shape[0]
                return nc.tensor.transpose(out, in_, ident[0:n, 0:n])

            def weights(key):
                i = WNO[key]
                pe.wait_ge(wl[i % NW], 16 * (i // NW + 1))
                return W[:, i % NW]

            def both(ps, lhs, src, nk, m=P, cols=((0, HALF), (HALF, HALF))):
                for part, (c0, n) in enumerate(cols):
                    for k in range(nk):
                        ins = mul(ps[0:m, part, 0:n], lhs(k), src(k)[:, c0:c0 + n], k == 0, k == nk - 1)
                return ins

            def project(key, src, nk=DT, wkey=None):
                w = weights(wkey or key)
                ps = room(key)
                both(ps, lambda k: w[:, k, :], src, nk).then_inc(mm, 1)

            def exact(out, w, x, first, last):
                (wh, wlo), (xh, xlo) = w, x
                for c in range(2):
                    mul(out[:, c, 0:HALF], wh, xh[:, c * HALF:(c + 1) * HALF], first, False)
                for c in range(2):
                    mul(out[:, c, 0:HALF], wh, xlo[:, c * HALF:(c + 1) * HALF], False, False)
                for c in range(2):
                    ins = mul(out[:, c, 0:HALF], wlo, xh[:, c * HALF:(c + 1) * HALF], False, last)
                return ins

            def norm(i, src, n):
                pe.wait_ge(S("sq"), i + 1)
                ps = room(f"ms{i}")
                if n == T:
                    ins = both(ps, lambda k: ones[:], src, DT)
                else:
                    for k in range(DT):
                        ins = mul(ps[:, 0, 0:n], ones[:], src(k), k == 0, k == DT - 1)
                ins.then_inc(mm, 1)

            ht = lambda k: HT[:, k, :]

            pe.wait_ge(S("const"), 1)
            norm(0, ht, T)
            pe.wait_ge(S("hn"), 1)
            w = weights("if")
            for i, key in enumerate(("gi", "gf")):
                ps = room(key)
                both(ps, lambda k: w[:, k, i * MH:(i + 1) * MH], ht, DT, MH).then_inc(mm, 1)
            for n in range(8):
                project(f"qk{n}", ht)
            for t in range(NTT):
                c0, m = tcols(t)
                ps = room(f"v{t}")
                for c in range(4):
                    w = weights(f"v{c}")
                    for k in range(DT):
                        ins = mul(ps[0:m, 0, c * P:(c + 1) * P], HT[:, k, c0:c0 + m], w[:, k, :], k == 0, k == DT - 1)
                ins.then_inc(mm, 1)
            pe.wait_ge(S("grows"), 1)
            pe.wait_ge(S("wg"), 1)
            ps = room("gt")
            for t in range(NTT):
                c0, m = tcols(t)
                for i, r in enumerate((GR, EM, WG)):
                    ins = turn(ps[0:m, 0, (t * 3 + i) * MH:(t * 3 + i + 1) * MH], r[:, c0:c0 + m])
            ins.then_inc(mm, 1)
            def keys_turned(h):
                ps = room(f"mb{h}")
                both(ps, lambda k: sel[:, h, :], lambda k: MR, 1, P, COLS)
                mul(ps[:, 1, TS:2 * TS], sel[:, h, :], EI[0:MH]).then_inc(mm, 1)
                pe.wait_ge(S("silu"), 8)
                ps = room(f"kt{h}")
                for t in range(NTT):
                    c0, m = tcols(t)
                    ins = turn(ps[0:m, t // 4, (t % 4) * P:(t % 4 + 1) * P], QK[:, MH + h, c0:c0 + m])
                ins.then_inc(mm, 1)

            def scores(h, i):
                qh, kh = QK[:, h, :], QK[:, MH + h, :]
                ps = room(f"s{h}_{i}")
                ins = mul(ps[:, 0, 0:TP - i * P], kh[:, i * P:(i + 1) * P], qh[:, i * P:TP])
                if i == 3:
                    ins = mul(ps[0:TS, 1, 0:TS], kh[:, TP:T], qh[:, TP:T])
                ins.then_inc(mm, 1)

            keys_turned(0)
            for i in range(4):
                scores(0, i)
            pe.wait_ge(S("vx"), NTT)
            for h in range(MH):
                project(f"o{h}", ht)
                pe.wait_ge(S("kw"), h + 1)
                ps = room(f"c{h}")
                for t in range(4):
                    mul(ps[:, 0, 0:129], KW[:, t, :], VX[:, t, h, :], t == 0, t == 3)
                mul(ps[:, 1, 0:258], KW[0:TS, 4, :], VB[0:TS, 6:8, :].rearrange("p a b -> p (a b)")).then_inc(mm, 1)
                ps = room(f"cs{h}")
                for i in range(2):
                    ins = mul(ps[:, i, 0:387], KW[0:TS, 4, :], VB[0:TS, 3 * i:3 * i + 3, :].rearrange("p a b -> p (a b)"))
                ins.then_inc(mm, 1)
                pe.wait_ge(S("probs"), h + 1)
                ps = room(f"n{h}")
                for t in range(4):
                    for i in range(t + 1):
                        ins = mul(ps[:, t // 2, (t % 2) * 256:(t % 2) * 256 + 129], DD[:, i, t * P:(t + 1) * P],
                                  VX[:, i, h, :], i == 0, i == t)
                ins.then_inc(mm, 1)
                ps = room(f"m{h}")
                mul(ps[0:TS, 0, 0:129], DS[0:TS], VX[0:TS, NTT - 1, h, :], True, False)
                pe.wait_ge(S("ldn"), 16)
                for b in range(NB):
                    ins = mul(ps[0:TS, 0, 0:129], QM[:, b, :], CN[:, h, b, :], False, b == NB - 1)
                ins.then_inc(mm, 1)
                if h + 1 < MH:
                    keys_turned(h + 1)
                    scores(h + 1, 0)
                    scores(h + 1, 1)
                pe.wait_ge(S("hnorm"), h + 1)
                ps = room(f"t{h}")
                for t in range(NTT):
                    c0, m = tcols(t)
                    ins = turn(ps[:, t // 4, (t % 4) * P:(t % 4) * P + m], HH[0:m, t, :])
                ins.then_inc(mm, 1)
                if h + 1 < MH:
                    scores(h + 1, 2)
                    scores(h + 1, 3)
            barrier(pe, 1)

            for n in RSEQ[0:5]:
                project(f"r{n}", ht)
            pe.wait_ge(S("ldwa"), 16)
            for p in range(RP):
                if p == 0:
                    pe.wait_ge(S("tanh"), 1)
                ps = room(f"w{p}")
                both(ps, lambda k: WA[0:64, p * P:(p + 1) * P], lambda k: TW[0:64], 1).then_inc(mm, 1)
                ps = room(f"a{p}")
                both(ps, lambda k: WA[64:P, p * P:(p + 1) * P], lambda k: RW[64:P, 12, :], 1).then_inc(mm, 1)
                nxt = RSEQ[5 + 3 * p:8 + 3 * p]
                for i in range(3):
                    if nxt:
                        project(f"r{nxt[i]}", ht)
                    if i < 2:
                        pe.wait_ge(S("kk2"), 2 * p + i + 1)
                        ps = room(f"{('kn', 'bn')[i]}{p}")
                        both(ps, lambda k: blk[:], lambda k: SQB, 1).then_inc(mm, 1)
            pe.wait_ge(S("rwops"), RP)
            def chunk_scores(c):
                ps = room(f"ab{c}")
                for h in range(RH):
                    r = slice(CH * (h % 2), CH * (h % 2) + CH)
                    ins = mul(ps[:, h % 2, (h // 2) * P:(h // 2 + 1) * P], BK[r, h // 2, c].rearrange("p a b -> p (a b)"),
                              AR[r, h // 2, c].rearrange("p a b -> p (a b)"))
                ins.then_inc(mm, 1)
                ps = room(f"nt{c}")
                for h in range(RH):
                    r = slice(CH * (h % 2), CH * (h % 2) + CH)
                    ins = mul(ps[0:CH, h % 2, (h // 2) * CH:(h // 2 + 1) * CH], AR[r, h // 2, c, 0], BK[r, h // 2, c, 0])
                ins.then_inc(mm, 1)

            No, Qo, Nd, Qd = PQ[:, 0], PQ[:, 1], PQD[:, 0], PQD[:, 1]
            N2, Q2, X, XT_, M, MTt = PQ2[:, 0], PQ2[:, 1], XX[:, 0], XX[:, 1], MM[:, 0], MM[:, 1]
            inverse_steps = {1: (Qd, Nd, Nd, Qd),
                             2: (Q2, X, N2, XT_), 3: (Q2, N2, N2, Q2),
                             4: (Q2, X, N2, XT_), 5: (Q2, N2, N2, Q2), 6: (Q2, X, N2, XT_),
                             7: (XT_, No, No, XT_),
                             8: (M, MTt),
                             9: (N2, X),
                             10: (MTt, Q2)}

            def inverse(c, i):
                x = inverse_steps[i]
                for z in range(2):
                    copied = {2: 1, 4: 3, 6: 5, 8: 7, 9: 9}.get(i)
                    summed = {4: 1, 6: 3, 7: 5, 10: 7}.get(i)
                    if i == 1 and z == 0:
                        pe.wait_ge(S("inv0"), c + 1)
                    if copied:
                        pe.wait_ge(S("icp"), 10 * c + copied + z)
                    if summed:
                        pe.wait_ge(S("iad"), 8 * c + summed + z)
                    ps = room(f"i{c}_{i}{'ab'[z]}")
                    for b in range(len(x) // 2):
                        for h in range(4):
                            ins = mul(ps[0:CH, b, h * CH:(h + 1) * CH], x[2 * b][0:CH, 4 * z + h, :],
                                      x[2 * b + 1][0:CH, 4 * z + h, :])
                    ins.then_inc(mm, 1)

            chunk_scores(0)
            for i in (1, 2, 3):
                inverse(0, i)
            for c in range(NC):
                for i in range(4, 11):
                    inverse(c, i)
                ps = room(f"vt{c}")
                for p in range(RP):
                    ins = mul(ps[CH:P, 0, p * P:(p + 1) * P], RW[:, 8 + p, c * CH:(c + 1) * CH], ident[:])
                ins.then_inc(mm, 1)
                ps = room(f"bt{c}")
                for p in range(RP):
                    ins = turn(ps[:, 0, p * P:(p + 1) * P], BK[:, p, c].rearrange("p a b -> p (a b)"))
                ins.then_inc(mm, 1)
                if c + 1 < NC:
                    chunk_scores(c + 1)
                pe.wait_ge(S("vbk"), c + 1)
                if c:
                    pe.wait_ge(S("stnew"), c)
                else:
                    pe.wait_ge(S("rzero"), 1)
                AC_ = AB[:, c % 2]
                ps = room(f"u{c}")
                for h in range(RH):
                    r = slice(CH * (h % 2), CH * (h % 2) + CH)
                    q = slice(h * CH, (h + 1) * CH)
                    mul(ps[0:CH, h % 2, q], AR[r, h // 2, c, 0], ST[r, h // 2, :], True, h % 2 == 0)
                    ins = mul(ps[0:CH, 1, q], AC_[CH:P, h, 0:CH], UV[CH:P, h, :], h % 2 == 0, True)
                ins.then_inc(mm, 1)
                if c + 1 < NC:
                    inverse(c + 1, 1)
                pe.wait_ge(S("u0"), c + 1)
                ps = room(f"uu{c}")
                for h in range(RH):
                    ins = mul(ps[0:CH, 0, h * CH:(h + 1) * CH], MM[0:CH, 0, h, :], U0S[0:CH, h, :])
                ins.then_inc(mm, 1)
                if c + 1 < NC:
                    inverse(c + 1, 2)
                    inverse(c + 1, 3)
                pe.wait_ge(S("uev"), c + 1)
                ps = room(f"y{c}")
                for h in range(RH):
                    r = slice(CH * (h % 2), CH * (h % 2) + CH)
                    q = slice((h // 2) * CH, (h // 2 + 1) * CH)
                    mul(ps[r, 0, q], ST[r, h // 2, :], AR[r, h // 2, c, 1], True, False)
                    mul(ps[r, 0, q], UV[:, h, :], AC_[:, h, CH:2 * CH], False, True)
                    ins = mul(ps[r, 1, q], BKT[:, h // 2, (h % 2) * CH:(h % 2 + 1) * CH], UV[:, h, :])
                ins.then_inc(mm, 1)
            pe.wait_ge(S("stnew"), NC)
            ps = room("abs")
            for h in range(RH):
                r = slice(CH * (h % 2), CH * (h % 2) + CH)
                ins = mul(ps[0:2 * TS, h % 2, (h // 2) * 2 * TS:(h // 2 + 1) * 2 * TS], BKS[r, h // 2].rearrange("p a b -> p (a b)"),
                          ARS[r, h // 2].rearrange("p a b -> p (a b)"))
            ins.then_inc(mm, 1)
            ps = room("nts")
            for h in range(RH):
                r = slice(CH * (h % 2), CH * (h % 2) + CH)
                ins = mul(ps[0:TS, h % 2, (h // 2) * TS:(h // 2 + 1) * TS], ARS[r, h // 2, 0], BKS[r, h // 2, 0])
            ins.then_inc(mm, 1)
            pe.wait_ge(S("sinv"), 1)
            ps = room("is1")
            for h in range(RH):
                ins = mul(ps[0:TS, 0, h * TS:(h + 1) * TS], ABS[0:TS, h, 0:TS], QSS[0:TS, h, :])
            ins.then_inc(mm, 1)
            pe.wait_ge(S("sinv"), 2)
            ps = room("is2")
            for h in range(RH):
                ins = mul(ps[0:TS, 0, h * TS:(h + 1) * TS], MS[0:TS, h, :], XS[0:TS, h, :])
            ins.then_inc(mm, 1)
            ps = room("vts")
            for p in range(RP):
                ins = mul(ps[TS:2 * TS, 0, p * P:(p + 1) * P], RW[:, 8 + p, TP:T], ident[:])
            ins.then_inc(mm, 1)
            ps = room("bts")
            for p in range(RP):
                ins = turn(ps[0:2 * TS, 0, p * P:(p + 1) * P], BKS[:, p].rearrange("p a b -> p (a b)"))
            ins.then_inc(mm, 1)
            pe.wait_ge(S("svbk"), 1)
            pe.wait_ge(S("lds0"), 16)
            ps = room("us")
            for h in range(RH):
                r = slice(CH * (h % 2), CH * (h % 2) + CH)
                q = slice((h // 2) * RD, (h // 2 + 1) * RD)
                for b in range(NB):
                    mul(ps[0:TS, h % 2, q], AM[r, 0, h // 2, b], S0[r, h // 2, b], b == 0, False)
                ins = mul(ps[0:TS, h % 2, q], ABS[TS:2 * TS, h, 0:TS], UVS[TS:2 * TS, h, :], False, True)
            ins.then_inc(mm, 1)
            pe.wait_ge(S("su"), 1)
            ps = room("uus")
            for h in range(RH):
                ins = mul(ps[0:TS, 0, h * RD:(h + 1) * RD], XS[0:TS, h, :], UVE[0:TS, 0, h, :])
            ins.then_inc(mm, 1)
            pe.wait_ge(S("su"), 2)
            ps = room("ys")
            for h in range(RH):
                r = slice(CH * (h % 2), CH * (h % 2) + CH)
                q = slice((h // 2) * TS, (h // 2 + 1) * TS)
                for b in range(NB):
                    mul(ps[r, 0, q], S0[r, h // 2, b], AM[r, 1, h // 2, b], b == 0, b == NB - 1)
                ins = mul(ps[r, 1, q], UVS[0:2 * TS, h, :], ABS[0:2 * TS, h, TS:2 * TS])
            ins.then_inc(mm, 1)
            for p in range(RP):
                pe.wait_ge(S("uve"), p + 1)
                ps = room(f"ss{p}")
                for x in range(2):
                    ins = mul(ps[CH * x:CH * x + CH, 0, :], BKTS[0:2 * TS, p, CH * x:CH * x + CH],
                              UVE[0:2 * TS, x].rearrange("p a b -> p (a b)"))
                ins.then_inc(mm, 1)
            pe.wait_ge(S("ldg2"), 16)
            for p in range(RP):
                if p == 0:
                    pe.wait_ge(S("ysum"), 1)
                ps = room(f"ym{p}")
                both(ps, lambda k: blk[:], lambda k: RW[:, 4 + p, :], 1).then_inc(mm, 1)
                project(f"xq{p}", ht)
                pe.wait_ge(S("yq"), p + 1)
                ps = room(f"yv{p}")
                both(ps, lambda k: blk[:], lambda k: YQ, 1).then_inc(mm, 1)
                ps = room(f"g{p}")
                both(ps, lambda k: G2[:, p * P:(p + 1) * P], lambda k: RW[:, 13, :], 1).then_inc(mm, 1)
            barrier(pe, 2)

            norm(1, lambda k: MN[:, k, :], NMEM)
            pe.wait_ge(S("hn"), 2)
            for h in range(MH):
                w = weights(f"mk{h}")
                ps = room(f"mk{h}")
                for k in range(DT):
                    ins = mul(ps[:, 0, 0:NMEM], w[:, k, :], MN[:, k, :], k == 0, k == DT - 1)
                ins.then_inc(mm, 1)
            for s in range(2):
                ps = room(f"mv{s}")
                for c in range(4):
                    w = weights(f"mv{c}")
                    for k in range(DT):
                        ins = mul(ps[:, 0, c * P:(c + 1) * P], MN[:, k, s * P:(s + 1) * P], w[:, k, :],
                                  k == 0, k == DT - 1)
                ins.then_inc(mm, 1)
            pe.wait_ge(S("mkv"), MH + 2)
            pe.wait_ge(S("xq"), MH)

            def memory_scores(h):
                ps = room(f"as{h}")
                for t in range(4):
                    ins = mul(ps[:, t // 2, (t % 2) * NMEM:(t % 2 + 1) * NMEM], XQ[:, h, t * P:(t + 1) * P], MKT[:, h, :])
                ins.then_inc(mm, 1)

            memory_scores(0)
            for h in range(MH):
                if h + 1 < MH:
                    memory_scores(h + 1)
                pe.wait_ge(S("soft"), h + 1)
                ps = room(f"at{h}")
                for s in range(2):
                    for t in range(4):
                        ins = turn(ps[:, s, t * P:(t + 1) * P], PA[:, h % 2, t, s * P:(s + 1) * P])
                ins.then_inc(mm, 1)
                pe.wait_ge(S("pat"), h + 1)
                ps = room(f"ao{h}")
                for s in range(2):
                    ins = mul(ps[:, 0, :], MV[:, s, h * P:(h + 1) * P], PAT[:, s, :], s == 0, s == 1)
                ins.then_inc(mm, 1)
            pe.wait_ge(S("xm"), 1)
            for h in range(MH):
                pe.wait_ge(S(f"ldk{h % 2}"), 16 * (h // 2 + 1))
                ps = room(f"ds{h}")
                for b in range(NB):
                    ins = mul(ps[h * TS:(h + 1) * TS, 0, 0:NMEM], XM[:, h, b, :], KB[:, h % 2, b * NMEM:(b + 1) * NMEM],
                              b == 0, b == NB - 1)
                ins.then_inc(mm, 1)
            pe.wait_ge(S("soft"), MH + 1)
            ps = room("dt")
            for s in range(2):
                ins = turn(ps[:, 0, s * P:(s + 1) * P], PA[:, 0, 0, s * P:(s + 1) * P])
            ins.then_inc(mm, 1)
            pe.wait_ge(S("pm"), 1)
            for h in range(MH):
                pe.wait_ge(S(f"ldvv{h % 2}"), 16 * (h // 2 + 1))
                ps = room(f"do{h}")
                for b in range(NB):
                    for s in range(2):
                        ins = mul(ps[:, 0, 0:TS], VBM[:, h % 2, (b * 2 + s) * P:(b * 2 + s + 1) * P], PM[:, s, h, b, :],
                                  b + s == 0, b + s == NB)
                ins.then_inc(mm, 1)
            barrier(pe, 3)

            def project_split(key, hi, lo):
                i = SPLIT.index(key)
                pe.wait_ge(S("gwlo"), i + 1)
                ps = room(key)
                for k in range(DT):
                    ins = exact(ps, (GWH[:, i % 2, k, :], GWL[:, i % 2, k, :]), (hi[:, k, :], lo[:, k, :]), k == 0, k == DT - 1)
                ins.then_inc(mm, 1)

            for n in range(DT):
                for j in range(3):
                    project(f"gb{n}_{j}", lambda k: BR[:, 4 * j + k, :], 4)
                    if n + j == 0:
                        pe.wait_ge(S("dlo"), 1)
                    project_split(f"gg{n}_{j}", DH, DL)
            pe.wait_ge(S("ylo"), DT)
            for n in range(DT):
                project_split(f"x{n}", YH, YL)
            barrier(pe, 4)

            norm(2, ht, T)
            pe.wait_ge(S("hn"), 3)
            pe.wait_ge(S("ldkeys"), 16)
            for i in range(2 * PH + 1):
                if i < 2 * PH:
                    project(f"pq{i}", ht)
                if i:
                    pe.wait_ge(S("pqe"), i)
                    ps = room(f"ps{i - 1}")
                    for t in range(NTT):
                        c0, m = tcols(t)
                        ins = mul(ps[0:m, t // 4, (t % 4) * P:(t % 4 + 1) * P], QT[:, (i - 1) % 3, c0:c0 + m],
                                  KSEL[:, (i - 1) % 2, :])
                    ins.then_inc(mm, 1)
            for t in range(NTT):
                _, m = tcols(t)
                pe.wait_ge(S("picks"), t + 1)
                ps = room(f"pt{t}")
                for i, x in enumerate((AFX[:, t % 2], BFX[:, t % 2], GAT[:, t % 2].rearrange("p a b -> p (a b)"))):
                    ins = turn(ps[:, 0, i * P:i * P + m], x[0:m, :])
                ins.then_inc(mm, 1)
            barrier(pe, 5)


            def gate_units(i, first):
                for u in range(8):
                    pe.wait_ge(S("oh2"), 8 * i + u + 1)
                    if not first and u % 2 == 0:
                        pe.wait_ge(S("ge"), 4 * i + u // 2 - 3)
                    for x in range(4):
                        ins = mul(PS[:, u // 2, u % 2, x * P:(x + 1) * P], OH[:, u % NOH, 0, x], OH[:, u % NOH, 1, x])
                    ins.then_inc(S("ohf"), 1)

            gate_units(0, True)
            with pe.Fori(1, NEB) as i:
                gate_units(i, False)
            barrier(pe, 6)

            def first_products(g, b):
                after(pe, "ulo", g + 1)
                for e in range(EG):
                    after(pe, "of", 8 * g - 11 + e)
                    ps = PS[:, 2 * b + e]
                    for k in range(DT):
                        ins = exact(ps, (UH[:, b, e, k, :], UL[:, b, e, k, :]), (XH[:, k, :], XL[:, k, :]),
                                    k == 0, k == DT - 1)
                    ins.then_inc(S("pa"), 1)

            def second_products(g, b):
                after(pe, "vlo", g + 1)
                after(pe, "wlo", 2 * g + 2)
                for d in range(DT):
                    if d in (2, 3):
                        if isinstance(g, int) and g == NG - 1:
                            after(pe, "of", 8 * g - 5 + d)
                        else:
                            after(pe, "af", 2 * g + 1 + d)
                    elif d >= EG + 2:
                        after(pe, "of", 8 * g - 3 + d)
                    elif isinstance(g, int) and g == 0:
                        after(pe, "af", d + 1)
                    else:
                        after(pe, "of", 8 * g - 1 + d)
                    ps = PS[:, (2 * b + d) % NSLOT]
                    for e in range(EG):
                        ins = exact(ps, [x[:, b, e, d * P:(d + 1) * P] for x in (VH, VL)],
                                    [x[:, b, e, :] for x in (WH, WL)], e == 0, e == EG - 1)
                    ins.then_inc(S("po"), 1)

            def turn_(g, b):
                if not isinstance(g, int) or g + 1 < NG:
                    first_products(g + 1, 1 - b)
                second_products(g, b)

            after(pe, "xsplit", 1)
            first_products(0, 0)
            turns(pe, turn_)
            norm(3, lambda k: YO[:, k * T:(k + 1) * T], T)

        @block.vector
        def _(dve):
            step = Steps(dve, S("dv"))

            def tt(out, x, y, op=ALU.mult, sem=None):
                step(dve.tensor_tensor(out, x, y, op), sem)

            def ts(out, x, s1_, op0, s2_=None, op1=None, sem=None):
                if op1 is None:
                    step(dve.tensor_scalar(out, x, s1_, None, op0), sem)
                else:
                    step(dve.tensor_scalar(out, x, s1_, s2_, op0, op1), sem)

            def stt(out, x, s, y, op0=ALU.mult, op1=ALU.mult, sem=None):
                step(dve.scalar_tensor_tensor(out=out, in0=x, scalar=s, in1=y, op0=op0, op1=op1), sem)

            def tally(out, x, op=ALU.add):
                step(dve.tensor_reduce(out, x, AX_X, op))

            def copy(out, x, sem=None):
                step(dve.tensor_copy(out, x), sem)

            def full(key, fn):
                ps = take(dve, key)
                give(dve, fn(ps[:, :, 0:HALF]), key)

            def norm(i, src, dst, g, n):
                if n == T:
                    full(f"ms{i}", lambda x: dve.tensor_scalar(halves(rstd), x, 1.0 / D, EPS, ALU.mult, ALU.add))
                else:
                    ps = take(dve, f"ms{i}")
                    give(dve, dve.tensor_scalar(rstd[:, 0:n], ps[:, 0, 0:n], 1.0 / D, EPS, ALU.mult, ALU.add), f"ms{i}")
                step(dve.reciprocal(rstd[:, 0:n], rstd[:, 0:n]), S("rc"))
                dve.wait_ge(S("rs"), i + 1)
                for k in range(DT):
                    stt(dst[:, k, :], src[:, k, :], v(g, k), rstd[:, 0:n], sem=S("hn") if k == DT - 1 else None)

            dve.wait_ge(S("ldv"), 16)
            dve.wait_ge(S("ldx"), 16)
            norm(0, XT, HT, "norm_mix", T)
            dve.wait_ge(S("ldg"), 16)
            dve.wait_ge(S("ldm"), 16)
            for key, r, i in (("gi", IR, 0), ("gf", FR, 1)):
                ps = take(dve, key)
                give(dve, dve.tensor_scalar(halves(r), ps[0:MH, :, 0:HALF], GB[0:MH, i:i + 1], None, ALU.add), key)
            step(dve.memset(ONR, 1.0), S("gi"))
            dve.wait_ge(S("ls"), 1)
            stt(FR, FR, 0.0, LR, ALU.min, ALU.subtract)
            step(dve.tensor_tensor_scan(FC[:, 0:TP], ONR[:, 0:TP], FR[:, 0:TP], 0.0, ALU.mult, ALU.add))
            fs, gs, ms_, lf = [x[:, TP:T].rearrange("p (b t) -> p b t", b=NB) for x in (FC, GR, MR, FR)]
            copy(fs[:, :, 0], lf[:, :, 0])
            for j in range(1, NS):
                tt(fs[:, :, j], fs[:, :, j - 1], lf[:, :, j], ALU.add)
            tt(GR, IR, FC, ALU.subtract)
            step(dve.tensor_tensor_scan(MR[:, 0:TP], GR[:, 0:TP], GR[:, 0:TP], 0.0, ALU.max, ALU.max))
            tt(ms_[:, :, 0], M0[0:MH], gs[:, :, 0], ALU.max)
            for j in range(1, NS):
                tt(ms_[:, :, j], ms_[:, :, j - 1], gs[:, :, j], ALU.max)
            tt(MT, FC, MR, ALU.add)
            ts(WG[:, 0:TP], GR[:, 0:TP], MR[:, TP - 1:TP], ALU.subtract)
            ws = WG[:, TP:T].rearrange("p (b t) -> p b t", b=NB)
            tt(ws, gs, bc(ms_[:, :, NS - 1], 2, NS), ALU.subtract)
            copy(MO[0:MH, 0:1], MT[:, TP - 1:TP])
            copy(MO[0:MH, 1:1 + NB], MT[:, TP:T].rearrange("p (b t) -> p b t", b=NB)[:, :, NS - 1], S("gates"))
            tt(EI[0:MH].rearrange("p (b t) -> p b t", b=NB), bc(M0[0:MH], 2, NS), ms_, ALU.subtract, S("gi"))
            for n in range(8):
                dve.wait_ge(S("ctail"), n + 1)
                if n >= 2:
                    dve.wait_ge(S("silu"), n - 1)
                q = QKP[:, n, 3 + TP:].rearrange("p (b t) -> p b t", b=NB)
                cp = CV[:, n % 2, 0:TP]
                cs = CV[:, n % 2, TP:T].rearrange("p (b t) -> p b t", b=NB)
                ts(cp, QKP[:, n, 0:TP], v("conv_w", n), ALU.mult, v("conv_b", n), ALU.add)
                ts(cs, q[:, :, 0:4], v("conv_w", n), ALU.mult, v("conv_b", n), ALU.add)
                for j in range(1, 4):
                    stt(cp, QKP[:, n, j:j + TP], v("conv_w", 8 * j + n), cp, ALU.mult, ALU.add)
                    stt(cs, q[:, :, j:j + 4], v("conv_w", 8 * j + n), cs, ALU.mult, ALU.add,
                        sem=S("cv") if j == 3 else None)
            ps = take(dve, "gt")
            copy(GTM[:, 0:4], ps[:, 0, 0:4 * 3 * MH].rearrange("p (a b c) -> p a b c", a=4, b=3))
            give(dve, dve.tensor_copy(GTM[0:TS, 4], ps[0:TS, 0, 4 * 3 * MH:5 * 3 * MH].rearrange("p (b c) -> p b c", b=3)),
                 "gt")
            def exponents(h):
                dve.wait_ge(S("mbr"), h + 1)
                mb = MB[:, h % 2]
                for i in range(4):
                    ts(DD[:, i, i * P:TP], mb[:, i * P:TP], GTM[:, i, 0, h:h + 1], ALU.subtract, 0.0, ALU.max, S("dd"))
                ts(DS[0:TS], mb[0:TS, TP:T], GTM[0:TS, 4, 0, h:h + 1], ALU.subtract, 0.0, ALU.max, S("dd"))
                ps = take(dve, f"kt{h}")
                dve.wait_ge(S("vx"), NTT)
                dve.tensor_tensor(KW[:, 0:4, :], ps[:, 0, :].rearrange("p (a b) -> p a b", a=4), bc(GTM[:, 0:4, 2, h], 2, P),
                                  ALU.mult)
                give(dve, dve.tensor_scalar(KW[0:TS, 4, :], ps[0:TS, 1, 0:P], GTM[0:TS, 4, 2, h:h + 1], None, ALU.mult),
                     f"kt{h}")
                tt(VB[0:TS], bc(VX[0:TS, NTT - 1, h, :], 1, NB), bc(bexp[0:TS, :], 2, 129), sem=S("kw"))

            def weigh(h, i):
                dve.wait_ge(S("ddx"), 5 * h + i + 1)
                ps = take(dve, f"s{h}_{i}")
                if i == 3:
                    dve.wait_ge(S("ddx"), 5 * h + 5)
                    stt(DS[0:TS], ps[0:TS, 1, 0:TS], SCALE, DS[0:TS])
                    dve.tensor_tensor(DS[0:TS], DS[0:TS], smask[:], ALU.mult)
                give(dve, dve.scalar_tensor_tensor(out=DD[:, i, i * P:TP], in0=ps[:, 0, 0:TP - i * P], scalar=SCALE,
                                                   in1=DD[:, i, i * P:TP], op0=ALU.mult, op1=ALU.mult), f"s{h}_{i}")
                dve.tensor_tensor(DD[:, i, i * P:(i + 1) * P], DD[:, i, i * P:(i + 1) * P], tri[:], ALU.mult)

            def turned(h):
                dve.wait_ge(S("so"), h + 1)
                ps = take(dve, f"t{h}")
                for part, (c0, n) in enumerate(COLS):
                    c = slice(c0, c0 + n)
                    ins = dve.scalar_tensor_tensor(out=BR[:, h, c], in0=ps[:, part, 0:n], scalar=v("ml_norm", h),
                                                   in1=SO[:, h, c], op0=ALU.mult, op1=ALU.mult)
                give(dve, ins, f"t{h}")

            exponents(0)
            for h in range(MH):
                for i in range(4):
                    if h and i == 2:
                        turned(h - 1)
                    weigh(h, i)
                mb = MB[:, h % 2]
                stt(QS, QK[:, h, TP:T], SCALE, mb[:, T:T + TS])
                tt(QM, bc(QS, 1, NB), bmask[:], sem=S("probs"))
                ps = take(dve, f"n{h}")
                give(dve, dve.tensor_copy(NU[:, 0:4, :], ps.rearrange("p a (b n) -> p (a b) n", b=2)[:, :, 0:129]), f"n{h}")
                ps = take(dve, f"m{h}")
                give(dve, dve.tensor_copy(NU[0:TS, 4, :], ps[0:TS, 0, 0:129]), f"m{h}")
                ps = take(dve, f"c{h}")
                tt(CN[:, h], CN[:, h], bc(mb[:, T:T + TS].rearrange("p (b t) -> p b t", b=NB)[:, :, NS - 1], 2, 129))
                dve.tensor_copy(CO[:, h, :], ps[:, 0, 0:129])
                cn = CN[:, h].rearrange("p a b -> p (a b)")
                give(dve, dve.tensor_tensor(cn[:, 774:1032], cn[:, 774:1032], ps[:, 1, 0:258], ALU.add), f"c{h}")
                ps = take(dve, f"cs{h}")
                dve.tensor_tensor(cn[:, 0:387], cn[:, 0:387], ps[:, 0, 0:387], ALU.add)
                give(dve, dve.tensor_tensor(cn[:, 387:774], cn[:, 387:774], ps[:, 1, 0:387], ALU.add), f"cs{h}")
                dve.sem_inc(S("cnew"), 1)
                if h + 1 < MH:
                    exponents(h + 1)
                den, em = NU[:, :, P], GTM[:, :, 1, h]
                stt(s1, den, -1.0, den, ALU.mult, ALU.max)
                tt(s1, s1, em, ALU.max)
                step(dve.reciprocal(s1, s1))
                tt(HH, NU[:, :, 0:P], bc(s1, 2, P))
                tally(s2, HH)
                ts(s2, s2, 1.0 / P, ALU.mult)
                tt(HH, HH, bc(s2, 2, P), ALU.subtract)
                tt(SQ, HH, HH)
                tally(s3, SQ)
                ts(s3, s3, 1.0 / P, ALU.mult, EPS, ALU.add)
                step(dve.reciprocal(s3, s3), S("hv"))
                dve.wait_ge(S("hs"), h + 1)
                tt(HH, HH, bc(s3, 2, P), sem=S("hnorm"))
            turned(MH - 1)
            barrier(dve, 1)

            def shift(i):
                n = RSEQ[i]
                dve.wait_ge(S("rwin"), 2 * i + 2)
                r = RPD[:, i % 2, :]
                q = r[:, 1 + TP:].rearrange("p (b t) -> p b t", b=NB)
                o1, o2 = RW[:, n, 0:TP], RW[:, n, TP:T].rearrange("p (b t) -> p b t", b=NB)
                dve.tensor_tensor(o1, r[:, 0:TP], r[:, 1:1 + TP], ALU.subtract)
                tt(o2, q[:, :, 0:4], q[:, :, 1:5], ALU.subtract)
                dve.scalar_tensor_tensor(out=o1, in0=o1, scalar=v("mu", n), in1=r[:, 1:1 + TP], op0=ALU.mult, op1=ALU.add)
                stt(o2, o2, v("mu", n), q[:, :, 1:5], ALU.mult, ALU.add, sem=S("rsh"))

            for i in range(5):
                shift(i)
            ts(OMK, vec[:, VEC["ka"]:VEC["ka"] + RP], -1.0, ALU.mult, 1.0, ALU.add)
            for p in range(RP):
                dve.wait_ge(S("wa"), p + 1)
                r_, k_, v_ = RW[:, p, :], RW[:, 4 + p, :], RW[:, 8 + p, :]
                ts(SQB, k_, v("kk", p), ALU.mult)
                tt(SQB, SQB, SQB, sem=S("kk2"))
                ts(KPB, AG, v("ka", p), ALU.mult, OMK[:, p:p + 1], ALU.add)
                tt(KPB, KPB, k_)
                ts(LW, LW, DECAY, ALU.mult)
                step(dve.tensor_tensor_scan(CC, reset[:], LW, 0.0, ALU.mult, ALU.add))
                tt(EP, CC, LW, ALU.subtract)
                if p + 1 < RP:
                    shift(5 + 3 * p)
                full(f"kn{p}", lambda x: dve.tensor_scalar(halves(KN), x, 1e-24, None, ALU.max))
                step(dve.reciprocal(KN, KN), S("kv"))
                dve.sem_inc(S("cum"), 1)
                stt(SQB, r_, v("rk", p), KPB, sem=S("kk2"))
                dve.wait_ge(S("ks"), p + 1)
                if p + 1 < RP:
                    shift(6 + 3 * p)
                stt(KN, k_, v("kk", p), KN)
                tt(AG, AG, KN)
                dve.wait_ge(S("dec"), p + 1)
                chunks = lambda x: x[:, 0:TP].rearrange("p (c t) -> p c t", c=NC)
                for x, y, dst, dsts, i in ((AG, EN, BK, BKS, 0), (KPB, EN, BK, BKS, 1), (r_, EW, AR, ARS, 1)):
                    tt(dst[:, p, :, i, :], chunks(x), chunks(y))
                    tt(dsts[:, p, i, :], x[:, TP:T], y[:, TP:T])
                stt(AR[:, p, :, 0, :], chunks(KN), -1.0, chunks(EP))
                stt(ARS[:, p, 0, :], KN[:, TP:T], -1.0, EP[:, TP:T])
                copy(WE[:, p, :], chunks(EW)[:, :, CH - 1])
                copy(WES[:, p, :], EW[:, TP:T].rearrange("p (b t) -> p b t", b=NB)[:, :, NS - 1])
                full(f"bn{p}", lambda x: dve.tensor_tensor(halves(RW[:, p, :]), x, halves(RW[:, 8 + p, :]), ALU.mult))
                dve.sem_inc(S("rwops"), 1)
                if p + 1 < RP:
                    shift(7 + 3 * p)
            hb = slice(0, CH)
            split = lambda x: x.rearrange("p (b a) n -> p a b n", a=2)
            banks = lambda ps, m, n: ps[0:m, :, 0:RP * n].rearrange("p a (b n) -> p a b n", b=RP)
            bank = lambda ps, i, n=CH: ps[0:n, i, 0:RH * n].rearrange("p (h n) -> p h n", h=RH)
            def chunk_masks(c):
                ps = take(dve, f"ab{c}")
                give(dve, dve.tensor_tensor(split(AB[:, c % 2]), ps.rearrange("p a (b n) -> p a b n", b=RP),
                                            bc(bc(rmask[:].rearrange("p a b -> p (a b)"), 1, RP), 1, 2), ALU.mult), f"ab{c}")
                ps = take(dve, f"nt{c}")
                give(dve, dve.tensor_tensor(split(PQ[hb, 1]), banks(ps, CH, CH), bc(bc(low[:], 1, RP), 1, 2), ALU.mult),
                     f"nt{c}")

            def start_inverse(c):
                N = AB[hb, c % 2, :, 0:CH]
                dve.tensor_tensor(PQD[hb, 0], N, bc(b16[:], 1, RH), ALU.mult)
                tt(PQD[hb, 1], PQ[hb, 1], bc(b16[:], 1, RH))
                dve.tensor_tensor(XX[hb, 0], PQD[hb, 0], bc(ident[hb, hb], 1, RH), ALU.add)
                tt(XX[hb, 1], PQD[hb, 1], bc(ident[hb, hb], 1, RH), ALU.add, S("inv0"))
                dve.tensor_tensor(PQ[hb, 0], N, PQD[hb, 0], ALU.subtract)
                tt(PQ[hb, 1], PQ[hb, 1], PQD[hb, 1], ALU.subtract)

            def inverse_sum(c, i):
                for z in range(2):
                    key = f"i{c}_{i}{'ab'[z]}"
                    hs = slice(4 * z, 4 * z + 4)
                    ps = take(dve, key)
                    one = ps[hb, 0, 0:4 * CH].rearrange("p (h n) -> p h n", h=4)
                    if i in (2, 4, 6):
                        two = ps[hb, :, 0:4 * CH].rearrange("p a (h n) -> p a h n", h=4)
                        ins = dve.tensor_tensor(XX[hb, :, hs], XX[hb, :, hs], two, ALU.add)
                    elif i == 9:
                        ins = dve.tensor_tensor(PQ2[hb, 1, hs], XX[hb, 0, hs], one, ALU.add)
                    else:
                        ins = dve.tensor_tensor(MM[hb, 0, hs], PQ2[hb, 1, hs], one, ALU.add)
                    give(dve, ins, key)
                    if i < 10:
                        dve.sem_inc(S("iad"), 1)

            chunk_masks(0)
            start_inverse(0)
            inverse_sum(0, 2)
            for c in range(NC):
                for i in (4, 6, 9, 10):
                    inverse_sum(c, i)
                ps = take(dve, f"vt{c}")
                give(dve, dve.tensor_copy(UV[CH:P], ps[CH:P, 0, :].rearrange("p (h n) -> p h n", h=RH)), f"vt{c}")
                ps = take(dve, f"bt{c}")
                give(dve, dve.tensor_copy(BKT, ps[:, 0, :].rearrange("p (h n) -> p h n", h=RP)), f"bt{c}")
                dve.sem_inc(S("vbk"), 1)
                if c + 1 < NC:
                    chunk_masks(c + 1)
                ps = take(dve, f"u{c}")
                copy(U0S[hb], bank(ps, 1))
                even = split(U0S[hb])[:, 0]
                give(dve, dve.tensor_tensor(even, even, split(bank(ps, 0))[:, 0], ALU.add), f"u{c}")
                dve.sem_inc(S("u0"), 1)
                if c + 1 < NC:
                    start_inverse(c + 1)
                ps = take(dve, f"uu{c}")
                give(dve, dve.tensor_copy(UV[hb], bank(ps, 0)), f"uu{c}")
                dve.sem_inc(S("uev"), 1)
                if c + 1 < NC:
                    inverse_sum(c + 1, 2)
                ps = take(dve, f"y{c}")
                dve.wait_ge(S("yev"), c + 1)
                give(dve, dve.tensor_tensor(ST, ps[:, 1, 0:RP * RD].rearrange("p (a b) -> p a b", a=RP), ST, ALU.add),
                     f"y{c}")
                tt(ST, ST, bc(WE[:, :, c], 2, RD), sem=S("stnew"))
            sl = slice(0, TS)
            ps = take(dve, "abs")
            give(dve, dve.tensor_tensor(split(ABS[0:2 * TS]), banks(ps, 2 * TS, 2 * TS),
                                        bc(bc(srm[:].rearrange("p a b -> p (a b)"), 1, RP), 1, 2), ALU.mult), "abs")
            ps = take(dve, "nts")
            give(dve, dve.tensor_tensor(split(QSS[sl]), banks(ps, TS, TS), bc(bc(slow[:], 1, RP), 1, 2), ALU.mult), "nts")
            tt(XS[sl], ABS[sl, :, 0:TS], bc(ident[sl, sl], 1, RH), ALU.add, S("sinv"))
            ps = take(dve, "is1")
            give(dve, dve.tensor_copy(MS[sl], bank(ps, 0, TS)), "is1")
            dve.sem_inc(S("sinv"), 1)
            ps = take(dve, "is2")
            give(dve, dve.tensor_tensor(XS[sl], XS[sl], bank(ps, 0, TS), ALU.add), "is2")
            ps = take(dve, "vts")
            give(dve, dve.tensor_copy(UVS[TS:2 * TS], ps[TS:2 * TS, 0, :].rearrange("p (h n) -> p h n", h=RH)), "vts")
            ps = take(dve, "bts")
            give(dve, dve.tensor_copy(BKTS[0:2 * TS], ps[0:2 * TS, 0, :].rearrange("p (h n) -> p h n", h=RP)), "bts")
            for x in range(2):
                for p in range(RP):
                    tt(AM[:, x, p], bc(ARS[:, p, x, :], 1, NB), bmask[:])
            dve.sem_inc(S("svbk"), 1)
            ps = take(dve, "us")
            give(dve, dve.tensor_copy(split(UVE[sl, 0]), banks(ps, TS, RD)), "us")
            dve.sem_inc(S("su"), 1)
            ps = take(dve, "uus")
            give(dve, dve.tensor_copy(UVS[sl], ps[sl, 0, :].rearrange("p (h n) -> p h n", h=RH)), "uus")
            dve.sem_inc(S("su"), 1)
            ps = take(dve, "ys")
            dve.wait_ge(S("yev"), NC + 1)
            ysm = RW[:, 4:8, TP:T]
            give(dve, dve.tensor_tensor(ysm, ysm, ps[:, 1, 0:RP * TS].rearrange("p (a b) -> p a b", a=RP), ALU.add), "ys")
            dve.sem_inc(S("ysum"), 1)
            for p in range(RP):
                for x in range(2):
                    tt(UVE[0:2 * TS, x], bc(UVS[0:2 * TS, 2 * p + x, :], 1, NB), bc(bexp[:], 2, RD),
                       sem=S("uve") if x else None)
                ps = take(dve, f"ss{p}")
                give(dve, dve.tensor_tensor(S0[:, p], ps[:, 0, :].rearrange("p (a b) -> p a b", a=NB), S0[:, p], ALU.add),
                     f"ss{p}")
                tt(S0[:, p], S0[:, p], bc(WES[:, p, :], 2, RD), sem=S("s0new"))
            for p in range(RP):
                full(f"ym{p}", lambda x: dve.scalar_tensor_tensor(out=halves(YC), in0=x, scalar=-1.0 / RD,
                                                                      in1=halves(RW[:, 4 + p, :]), op0=ALU.mult, op1=ALU.add))
                tt(YQ, YC, YC, sem=S("yq"))
                full(f"yv{p}", lambda x: dve.tensor_scalar(halves(rstd), x, 1.0 / RD, GN_EPS, ALU.mult, ALU.add))
                step(dve.reciprocal(rstd[:], rstd[:]), S("yv"))
                dve.wait_ge(S("ysq"), p + 1)
                tt(YC, YC, rstd[:])
                ts(YC, YC, v("ln_w", p), ALU.mult, v("ln_b", p), ALU.add)
                tt(YC, YC, RW[:, p, :], ALU.add)
                full(f"g{p}", lambda x: dve.tensor_tensor(halves(BR[:, 4 + p, :]), x, halves(YC), ALU.mult))
            barrier(dve, 2)

            dve.wait_ge(S("ldmem"), 16)
            norm(1, MEM, MN, "mem_norm", NMEM)

            def below_max(i, q, src):
                tally(c1[:, 0:q], src, ALU.max)
                ins = dve.tensor_tensor(PA[:, i % 2, 0:q], src, bc(c1[:, 0:q], 2, NMEM), ALU.subtract)
                if i < MH:
                    give(dve, ins, f"as{i}")
                else:
                    step(ins)
                dve.sem_inc(S("sx"), 1)

            def normalise(i, q):
                pa = PA[:, i % 2, 0:q]
                dve.wait_ge(S("sxe"), i + 1)
                tally(c2[:, 0:q], pa)
                step(dve.reciprocal(c2[:, 0:q], c2[:, 0:q]))
                tt(pa, pa, bc(c2[:, 0:q], 2, NMEM), sem=S("soft"))

            dve.wait_ge(S("xq"), MH)
            for h in range(MH):
                tt(XM[:, h], bc(XQ[:, h, TP:T], 1, NB), bmask[:], sem=S("xm") if h == MH - 1 else None)
            for h in range(MH + 1):
                if h < MH:
                    ps = take(dve, f"as{h}")
                    below_max(h, 4, ps.rearrange("p a (b n) -> p (a b) n", b=2))
                if h:
                    normalise(h - 1, 4)
            for h in range(MH):
                ps = take(dve, f"ds{h}")
                q = slice(h * TS, (h + 1) * TS)
                give(dve, dve.tensor_copy(PA[q, 0, 0, :], ps[q, 0, 0:NMEM]), f"ds{h}")
            below_max(MH, 1, PA[:, 0, 0:1, :])
            normalise(MH, 1)
            ps = take(dve, "dt")
            give(dve, dve.tensor_copy(PT3, ps[:, 0, 0:2 * P].rearrange("p (a b) -> p a b", a=2)), "dt")
            for s in range(2):
                for h in range(MH):
                    tt(PM[:, s, h], bc(PT3[:, s, h * TS:(h + 1) * TS], 1, NB), bmask[:],
                       sem=S("pm") if s * h == MH - 1 else None)
            barrier(dve, 3)

            def weight_rest(i):
                dve.wait_ge(S("gwhi"), i + 1)
                dve.tensor_tensor(GWL[:, i % 2], W[:, WNO[SPLIT[i]] % NW], GWH[:, i % 2].bitcast(F32),
                                  ALU.subtract).then_inc(S("gwlo"), 1)

            def merged_rest(n):
                dve.wait_ge(S("yhi"), n + 1)
                dve.tensor_tensor(YL[:, n, :], YM[:, n % 2, :], YH[:, n, :].bitcast(F32), ALU.subtract).then_inc(S("ylo"), 1)

            weight_rest(0)
            for k in range(DT):
                dve.wait_ge(S("dhi"), k + 1)
                ins = dve.tensor_tensor(DL[:, k, :], HT[:, k, :], DH[:, k, :].bitcast(F32), ALU.subtract)
            ins.then_inc(S("dlo"), 1)
            for i in range(3 * DT):
                n, j = i // 3, i % 3
                weight_rest(i + 1)
                dve.wait_ge(S("sgb"), i + 1)
                dst = TMP[:, i % 2, :] if j else YM[:, n % 2, :]
                full(f"gb{n}_{j}", lambda x: dve.tensor_tensor(halves(dst), x, halves(SGB[:, i % 3, :]), ALU.mult))
                dve.sem_inc(S("gated"), 1)
                if j:
                    tt(YM[:, n % 2, :], YM[:, n % 2, :], dst, ALU.add, S("merged") if j == 2 else None)
                if i and j == 0:
                    merged_rest(n - 1)
            merged_rest(DT - 1)
            for i in range(3 * DT + 1, len(SPLIT)):
                weight_rest(i)
                n = i - 3 * DT - 1
                full(f"x{n}", lambda x: dve.tensor_tensor(halves(XT[:, n, :]), x, halves(XT[:, n, :]), ALU.add))
            n = DT - 1
            full(f"x{n}", lambda x: dve.tensor_tensor(halves(XT[:, n, :]), x, halves(XT[:, n, :]), ALU.add))
            barrier(dve, 4)

            norm(2, XT, HT, "norm_ffn", T)

            def top16(sets):
                for x, _, vals, _ in sets:
                    ins = dve.max(vals[:, 0:8], x)
                step(ins)
                for x, y, vals, _ in sets:
                    ins = dve.match_replace(y, vals[:, 0:8], x, LOW)
                step(ins)
                for _, y, vals, _ in sets:
                    ins = dve.max(vals[:, 8:16], y)
                step(ins)
                for x, y, vals, idx in sets:
                    dve.max_index(idx[:, 0:8], vals[:, 0:8], x)
                    ins = dve.max_index(idx[:, 8:16], vals[:, 8:16], y)
                return ins

            for i in range(2 * PH):
                dve.wait_ge(S("sce"), i + 1)
                step(top16([(SC[0:tcols(t)[1], i % 4, t, :], SC2[0:tcols(t)[1], i % 4, t, :],
                             V16[0:tcols(t)[1], t, i, :], IX[0:tcols(t)[1], t, i, :]) for t in range(NTT)]), S("scf"))
            for t in range(NTT - 1):
                dve.tensor_copy(IF[:, t], IX[:, t])
            copy(IF[0:TS, NTT - 1], IX[0:TS, NTT - 1])

            def candidates(t):
                _, m = tcols(t)
                b = t % 2
                vs = V16[0:m, t].rearrange("p (h s) k -> p h s k", s=2)
                at = 0
                for i, n, w in RUNS:
                    ins = dve.tensor_tensor(CAND[0:m, :, at:at + n * w].rearrange("p h (i j) -> p h i j", i=n),
                                            bc(vs[:, :, 0, i:i + n], 3, w), bc(vs[:, :, 1, 0:w], 2, n), ALU.add)
                    at += n * w
                step(ins)
                step(top16([(CAND[0:m, h], CAND2[0:m, h], TOP[0:m, h, :], PX[0:m, h, :]) for h in range(PH)]))
                flat = PX[0:m].rearrange("p a b -> p (a b)")
                p8, p5, p3, p1 = [x[0:m] for x in (P8, P5, P3, P1)]
                for x, base in ((p8, 8), (p5, 14), (p3, 22), (p1, 38)):
                    ins = dve.tensor_scalar(x, flat, base, 0, ALU.subtract, ALU.max)
                step(ins)
                dve.tensor_scalar(p5, p5, 13, None, ALU.mult)
                dve.tensor_scalar(p3, p3, 11, None, ALU.mult)
                ts(p8, p8, 3, ALU.logical_shift_right)
                dve.tensor_scalar(p5, p5, 6, None, ALU.logical_shift_right)
                dve.tensor_tensor(p1, p1, p8, ALU.max)
                ts(p3, p3, 5, ALU.logical_shift_right)
                tt(p1, p1, p5, ALU.max)
                tt(p1, p1, p3, ALU.max)
                row, r0, rb = AFX[0:m, b], ROW0[0:m], ROWB[0:m]
                copy(row, p1)
                dve.tensor_scalar(r0, row, 8, 8, ALU.mult, ALU.add)
                ts(rb, row, 5, ALU.mult, 14, ALU.add)
                stt(r0, row, 16, r0, ALU.mult, ALU.min)
                tt(r0, r0, rb, ALU.min)
                ts(rb, row, 3, ALU.mult, 22, ALU.add)
                stt(r0, row, 38, r0, ALU.add, ALU.min)
                tt(r0, r0, rb, ALU.min)
                copy(rb, flat)
                tt(BFX[0:m, b], rb, r0, ALU.subtract)
                tt(GAT[0:m, b], TOP[0:m], bc(TOP[0:m, :, 0], 2, PK), ALU.subtract, S("gx"))

            def picks(t):
                c0, m = tcols(t)
                b = t % 2
                dve.wait_ge(S("gxe"), t + 1)
                tally(e1[0:m], GAT[0:m, b])
                step(dve.reciprocal(e1[0:m], e1[0:m]))
                dve.tensor_tensor(GAT[0:m, b], GAT[0:m, b], bc(e1[0:m], 2, PK), ALU.mult)
                for i, x in enumerate((AFX, BFX)):
                    dve.wait_ge(S("eq"), 2 * t + i + 1)
                    step(dve.tensor_reduce(x[0:m, b], EQ[0:m, i], AX_X, ALU.add), S("picks") if i else S("dvx"))

            def place_hots(t):
                _, m = tcols(t)
                for i, x in enumerate((AFX, BFX)):
                    ins = dve.tensor_tensor(EQ[0:m, i], bc(x[0:m, t % 2], 2, PK), bc(iota[0:m, 0:PK], 1, P), ALU.is_equal)
                step(ins, S("pk1"))

            def pick_rows(t):
                c0, m = tcols(t)
                ps = take(dve, f"pt{t}")
                give(dve, dve.tensor_copy(IT[:, :, c0:c0 + m], ps[:, 0, 0:3 * P].rearrange("p (a b) -> p a b", a=3)[:, :, 0:m]),
                     f"pt{t}")

            for t in range(NTT + 1):
                if t >= 2:
                    pick_rows(t - 2)
                if t < NTT:
                    candidates(t)
                if t:
                    picks(t - 1)
                if t < NTT:
                    place_hots(t)
            pick_rows(NTT - 1)
            barrier(dve, 5)

            def one_hots(i, first):
                for u in range(8):
                    if not (first and u < NOH):
                        dve.wait_ge(S("ohf"), 8 * i + u + 1 - NOH)
                    ins = dve.tensor_tensor(OH[:, u % NOH], bc(bc(iota[:], 1, 4), 1, 2),
                                            bc(IT[:, 0:2, bass.ds(EB * i + 4 * u, 4)], 3, P), ALU.is_equal)
                    ins.then_inc(S("oh1"), 1)

            one_hots(0, True)
            with dve.Fori(1, NEB) as i:
                one_hots(i, False)
            dve.wait_ge(S("oh1"), 8 * NEB)
            barrier(dve, 6)

            for k in range(DT):
                dve.wait_ge(S("xhi"), k + 1)
                ins = dve.tensor_tensor(XL[:, k, :], HT[:, k, :], XH[:, k, :].bitcast(F32), ALU.subtract)
            step(ins, S("xsplit"))

            def split_low(x, g, b):
                after(dve, f"{x}hi", g + 1)
                hi, lo = (UH, UL) if x == "u" else (VH, VL)
                flat = "p e k n -> p (e k n)" if x == "u" else "p e n -> p (e n)"
                dve.tensor_tensor(lo[:, b].rearrange(flat), RAW[x][:, b], hi[:, b].rearrange(flat).bitcast(F32),
                                  ALU.subtract).then_inc(S(f"{x}lo"), 1)

            def weight(g, b, loaded):
                dve.wait_ge(S("lg"), loaded)
                for e in range(EG):
                    after(dve, "af", 2 * g + e + 1)
                    x = AX[:, e, :].rearrange("p (a t) -> p a t", t=EB)
                    dve.tensor_tensor(x, x, GQ[:, :, 2 * b + e, :], ALU.mult).then_inc(S("wr"), 1)

            def weight_low(g, b, e):
                after(dve, "whi", 2 * g + e + 1)
                dve.tensor_tensor(WL[:, b, e, :], AX[:, e, :], WH[:, b, e, :].bitcast(F32), ALU.subtract).then_inc(S("wlo"), 1)

            def add(g, b, ds_):
                for d in ds_:
                    after(dve, "po", 8 * g + d + 1)
                    after(dve, "of", 8 * g - 7 + d)
                    x = XT[:, d, :].rearrange("p (a n) -> p a n", a=2)
                    dve.tensor_tensor(x, PS[:, (2 * b + d) % NSLOT, :, 0:HALF], x, ALU.add).then_inc(S("of"), 1)

            def turn_(g, b):
                fixed = isinstance(g, int)
                n = 1 - b
                more = not fixed or g + 1 < NG
                if more:
                    split_low("v", g + 1, n)
                if not fixed or g + 2 < NG:
                    split_low("u", g + 2, b)
                if more:
                    weight(g + 1, n, 16 * ((g + 1) // 2 + 1) if fixed else 8 * (g + 1 - n) + 16)
                    weight_low(g + 1, n, 0)
                add(g, b, range(2))
                if more:
                    weight_low(g + 1, n, 1)
                add(g, b, range(2, DT))

            split_low("u", 0, 0)
            split_low("u", 1, 1)
            split_low("v", 0, 0)
            weight(0, 0, 16)
            weight_low(0, 0, 0)
            weight_low(0, 0, 1)
            turns(dve, turn_)
            dve.wait_ge(S("of"), 8 * NG)
            yo = YO.rearrange("p (k t) -> p k t", k=DT)
            norm(3, XT, yo, "norm_final", T)


OUTS = {"yT": (D, T), "cn": (P, MH, P + 1), "cns": (P, MH, NB, P + 1), "m": (MH, 1 + NB), "conv": (P, 8, 27),
        "S": (P, RP, RD), "Ss": (P, RP, NB, RD), "shift": (P, NRW, 9), "mk": (P, MH, NMEM), "mv": (P, 2, 512)}


def kernel(**inputs):
    import numpy as np
    import concourse.bacc as bacc
    from concourse.bass_utils import run_bass_kernel_spmd

    x = {k: np.asarray(w) for k, w in inputs.items()}
    w1 = {k: w[0] for k, w in x.items() if k != "norm_final"}

    def tiles(w):
        return w.reshape(-1, P).T

    vecs = [tiles(w1["norm_mix"])] + [tiles(w1["ml_conv_w"][j]) for j in range(4)]
    vecs += [tiles(w1[k]) for k in ("ml_conv_b", "ml_norm_w", "rw_mu", "rw_w0", "rw_a0", "rw_kk", "rw_ka", "rw_rk",
                                    "rw_ln_w", "rw_ln_b", "mem_norm", "norm_ffn")]
    vecs += [tiles(x["norm_final"])]
    cn = np.concatenate([w1["state_mlstm_C"].transpose(3, 1, 0, 2), w1["state_mlstm_n"].transpose(2, 1, 0)[..., None]], 3)
    data = {
        "xT": np.concatenate([x["x_prompt"][0].T, x["x_sample"].reshape(TS, D).T], 1),
        "memT": x["mem_prompt"][0].T,
        "vecs": np.concatenate(vecs, 1),
        "gateb": w1["ml_gate_b"].reshape(2, MH).T,
        "m0T": w1["state_mlstm_m"].T,
        "cnT": cn,
        "convT": w1["state_mlstm_conv"].transpose(2, 0, 1).reshape(8, P, 24).transpose(1, 0, 2),
        "s0T": w1["state_rwkv_S"].reshape(NB, RP, 2, RD, RD).transpose(2, 4, 1, 0, 3).reshape(P, RP, NB, RD),
        "shT": w1["state_rwkv_shift"].T.reshape(NRW, P, NB).transpose(1, 0, 2),
        "memkT": w1["cache_mem_k"].transpose(3, 2, 0, 1).reshape(P, MH, NB * NMEM),
        "memv": w1["cache_mem_v"].reshape(NB, 2, P, MH, P).transpose(2, 3, 0, 1, 4).reshape(P, MH, NB * NMEM),
        "w_in": w1["w_in"],
        "wa": np.concatenate([w1["rw_w2"], w1["rw_a2"]], 0),
        "g2": w1["rw_g2"],
        "w_mk": w1["w_mk"], "w_mv": w1["w_mv"],
        "w_branch": w1["w_branch"].reshape(3 * 512, D), "w_out": w1["w_out"], "wq": w1["pk_wq"],
        "keysT": np.stack([w1["pk_k1"].T, w1["pk_k2"].T], 1),
        "uT": w1["pk_u"].reshape(P, NK, DT, P).transpose(3, 1, 2, 0),
        "vT": w1["pk_v"].reshape(P, NK, D),
    }
    nc = bacc.Bacc("TRN2", target_bir_lowering=False, num_devices=1)
    arrays, a, o = {}, {}, {}
    for name, w in data.items():
        arrays[f"in_{name}"] = np.ascontiguousarray(w)
        a[name] = nc.dram_tensor(f"in_{name}", arrays[f"in_{name}"].shape, F32, kind="ExternalInput").ap()
    for name, shape in OUTS.items():
        o[name] = nc.dram_tensor(f"out_{name}", shape, F32, kind="ExternalOutput").ap()
    hybrid_layer(nc, a, o)
    r = run_bass_kernel_spmd(nc, [arrays], core_ids=[0]).results[0]
    r = {name: np.asarray(r[f"out_{name}"]) for name in OUTS}

    y = r["yT"].T
    conv = r["conv"].transpose(1, 0, 2).reshape(8 * P, 27)
    shift = r["shift"].transpose(1, 0, 2).reshape(NRW * P, 9)
    s = r["S"].reshape(2, RD, RP, RD).transpose(2, 0, 3, 1).reshape(1, 1, RH, RD, RD)
    ss = r["Ss"].reshape(2, RD, RP, NB, RD).transpose(3, 2, 0, 4, 1).reshape(1, NB, RH, RD, RD)
    cn, cns = r["cn"].transpose(1, 2, 0)[None, None], r["cns"].transpose(2, 1, 3, 0)[None]
    outs = (
        y[:TP].reshape(1, TP, D), y[TP:].reshape(NB, NS, D),
        cn[:, :, :, :P], cn[:, :, :, P], r["m"][:, 0].reshape(1, 1, MH), conv[:, 0:3].T[None, None], s,
        shift[:, 0].reshape(1, 1, -1), r["mk"].transpose(2, 1, 0)[None, None],
        r["mv"].transpose(1, 0, 2).reshape(1, 1, NMEM, MH, P),
        cns[:, :, :, :P], cns[:, :, :, P], r["m"][:, 1:].T[None],
        conv[:, 3:].reshape(8 * P, NB, 3).transpose(1, 2, 0)[None], ss, shift[:, 1:].T[None],
    )
    return tuple(np.ascontiguousarray(w) for w in outs)
```
